# Optimizing a Trainium2 kernel written in Bass

```python
import jax, jax.numpy as jnp
from jax import lax
import numpy as np

D_MODEL = 1024
BATCH = 1
SEQ = 512
DEPTH = 1

CHUNK = 64
RWKV_HEADS = 16
RWKV_HEAD_DIM = 64
RWKV_DIM = RWKV_HEADS * RWKV_HEAD_DIM
DECAY_LORA = 64
ICL_LORA = 64
GATE_LORA = 128
RWKV_COLS = 3 * RWKV_DIM + DECAY_LORA + ICL_LORA + GATE_LORA
RWKV_SPLITS = (RWKV_DIM, 2 * RWKV_DIM, 3 * RWKV_DIM, 3 * RWKV_DIM + DECAY_LORA, 3 * RWKV_DIM + DECAY_LORA + ICL_LORA)
GN_EPS = 64e-5
ATT_HQ = 16
ATT_HKV = 4
ATT_GROUP = ATT_HQ // ATT_HKV
ATT_DH = 64
WINDOW = 128
WINDOW_CHUNKS = WINDOW // CHUNK
Q_COLS = ATT_HQ * ATT_DH
KV_COLS = ATT_HKV * ATT_DH
QKV_COLS = Q_COLS + 2 * KV_COLS
N_BRANCH = 2
GATE_COLS = N_BRANCH * D_MODEL
IN_COLS = RWKV_COLS + QKV_COLS + GATE_COLS
D_FF = 2816
CONV_WIDTH = 3
RMS_EPS = 1e-6
NEG_INF = -1e30

kernel_name = 'hybrid_rwkv7_swa_sink_convffn'

def rmsnorm(x, g):
    xf = x.astype(jnp.float32)
    y = xf * lax.rsqrt(jnp.mean(xf * xf, axis=-1, keepdims=True) + RMS_EPS)
    return (y * g.astype(jnp.float32)).astype(x.dtype)

def token_shift(z):
    return jnp.pad(z[:, :-1], ((0, 0), (1, 0), (0, 0)))

def rwkv7_time_mix(z, mu, w0, w2, a0, a2, g2, k_k, k_a, r_k, lnx_w, lnx_b):
    B, T, _ = z.shape
    f32 = jnp.float32
    z = z + (token_shift(z) - z) * mu
    r, k, v, zw, za, zg = jnp.split(z, RWKV_SPLITS, axis=-1)
    w_log = -jax.nn.softplus(-(w0 + jnp.tanh(zw) @ w2).astype(f32)) - 0.5
    decay = jnp.exp(-jnp.exp(w_log))
    a = jax.nn.sigmoid((a0 + za @ a2).astype(f32))
    g = jax.nn.sigmoid(zg) @ g2

    def heads(t):
        return t.reshape(B, T, RWKV_HEADS, RWKV_HEAD_DIM)

    kf = k.astype(f32)
    kk = heads(kf * k_k.astype(f32))
    kk = kk / jnp.maximum(jnp.sqrt(jnp.sum(kk * kk, axis=-1, keepdims=True)), 1e-12)
    k_mod = kf * (1.0 + (a - 1.0) * k_a.astype(f32))
    rh, wh, kh, vh, ah = heads(r.astype(f32)), heads(decay), heads(k_mod), heads(v.astype(f32)), heads(a)

    def tm(t):
        return jnp.swapaxes(t, 0, 1)

    def step(S, inp):
        r_t, w_t, k_t, v_t, aa_t, bb_t = inp
        sa = jnp.einsum('bhvk,bhk->bhv', S, aa_t)
        S = S * w_t[:, :, None, :] + sa[..., None] * bb_t[:, :, None, :] + v_t[..., None] * k_t[:, :, None, :]
        y_t = jnp.einsum('bhvk,bhk->bhv', S, r_t)
        return S, y_t

    S0 = jnp.zeros((B, RWKV_HEADS, RWKV_HEAD_DIM, RWKV_HEAD_DIM), f32)
    _, y = lax.scan(step, S0, (tm(rh), tm(wh), tm(kh), tm(vh), tm(-kk), tm(kk * ah)))
    y = tm(y)
    mean = jnp.mean(y, axis=-1, keepdims=True)
    var = jnp.mean(jnp.square(y - mean), axis=-1, keepdims=True)
    y = (y - mean) * lax.rsqrt(var + GN_EPS)
    y = y.reshape(B, T, RWKV_DIM) * lnx_w.astype(f32) + lnx_b.astype(f32)
    bonus = jnp.sum(rh * kh * r_k.astype(f32), axis=-1, keepdims=True) * vh
    y = (y + bonus.reshape(B, T, RWKV_DIM)) * g.astype(f32)
    return y.astype(z.dtype)

def window_sink_attention(q, k, v, sink):
    B, T, _ = q.shape
    f32 = jnp.float32
    n_chunks = T // CHUNK
    qb = q.reshape(B, n_chunks, CHUNK, ATT_HKV, ATT_GROUP, ATT_DH).astype(f32)
    kb = k.reshape(B, n_chunks, CHUNK, ATT_HKV, ATT_DH).astype(f32)
    vb = v.reshape(B, n_chunks, CHUNK, ATT_HKV, ATT_DH).astype(f32)
    pad = ((0, 0), (WINDOW_CHUNKS - 1, 0), (0, 0), (0, 0), (0, 0))
    kp = jnp.pad(kb, pad)
    vp = jnp.pad(vb, pad)
    keys = jnp.concatenate([kp[:, i:i + n_chunks] for i in range(WINDOW_CHUNKS)], axis=2)
    vals = jnp.concatenate([vp[:, i:i + n_chunks] for i in range(WINDOW_CHUNKS)], axis=2)
    key_chunk = (jnp.arange(n_chunks)[:, None] - (WINDOW_CHUNKS - 1)
                 + jnp.repeat(jnp.arange(WINDOW_CHUNKS), CHUNK)[None, :])
    valid = key_chunk >= 0
    s = jnp.einsum('bcqhgd,bckhd->bchgqk', qb, keys) * (ATT_DH ** -0.5)
    s = jnp.where(valid[None, :, None, None, None, :], s, NEG_INF)
    sink_logit = jnp.broadcast_to(sink.astype(f32).reshape(ATT_HKV, ATT_GROUP)[None, None, :, :, None, None],
                                  s.shape[:-1] + (1,))
    p = jax.nn.softmax(jnp.concatenate([s, sink_logit], axis=-1), axis=-1)[..., :-1]
    o = jnp.einsum('bchgqk,bckhd->bcqhgd', p, vals)
    return o.reshape(B, T, Q_COLS).astype(q.dtype)

def conv_ffn(h, w_up, conv_w, conv_b, w_down):
    T = h.shape[1]
    u = h @ w_up
    up = jnp.pad(u, ((0, 0), (CONV_WIDTH - 1, 0), (0, 0)))
    c = conv_b + sum(conv_w[i] * up[:, i:i + T] for i in range(CONV_WIDTH))
    gate, val = jnp.split(c, 2, axis=-1)
    return (jax.nn.silu(gate) * val) @ w_down

def setup_inputs(seed: int = 0) -> dict:
    key = jax.random.key(seed)
    ks = jax.random.split(key, 32)
    f32 = jnp.float32
    L = DEPTH

    def nrm(k, shape, scale):
        return jax.random.normal(k, shape, f32) * scale

    return {
        'x': nrm(ks[0], (BATCH, SEQ, D_MODEL), 1.0),
        'norm1_g': 1.0 + nrm(ks[1], (L, D_MODEL), 0.05),
        'w_in': nrm(ks[2], (L, D_MODEL, IN_COLS), D_MODEL ** -0.5),
        'rwkv_mu': jax.random.uniform(ks[3], (L, RWKV_COLS), f32),
        'w0': jax.random.uniform(ks[4], (L, RWKV_DIM), f32, -6.0, 0.0),
        'w2': nrm(ks[5], (L, DECAY_LORA, RWKV_DIM), 0.1),
        'a0': nrm(ks[6], (L, RWKV_DIM), 0.5),
        'a2': nrm(ks[7], (L, ICL_LORA, RWKV_DIM), ICL_LORA ** -0.5),
        'g2': nrm(ks[8], (L, GATE_LORA, RWKV_DIM), GATE_LORA ** -0.5),
        'k_k': 0.85 + nrm(ks[9], (L, RWKV_DIM), 0.05),
        'k_a': 1.0 + nrm(ks[10], (L, RWKV_DIM), 0.05),
        'r_k': nrm(ks[11], (L, RWKV_HEADS, RWKV_HEAD_DIM), 0.1),
        'lnx_w': 1.0 + nrm(ks[12], (L, RWKV_DIM), 0.05),
        'lnx_b': nrm(ks[13], (L, RWKV_DIM), 0.02),
        'b_qkv': nrm(ks[14], (L, QKV_COLS), 0.02),
        'attn_sink': nrm(ks[15], (L, ATT_HQ), 1.0),
        'gate_b': nrm(ks[16], (L, GATE_COLS), 0.1),
        'w_proj_a': nrm(ks[17], (L, RWKV_DIM, D_MODEL), RWKV_DIM ** -0.5),
        'w_proj_b': nrm(ks[18], (L, Q_COLS, D_MODEL), Q_COLS ** -0.5),
        'w_out': nrm(ks[19], (L, D_MODEL, D_MODEL), D_MODEL ** -0.5),
        'norm2_g': 1.0 + nrm(ks[20], (L, D_MODEL), 0.05),
        'w_up': nrm(ks[21], (L, D_MODEL, 2 * D_FF), D_MODEL ** -0.5),
        'conv_w': nrm(ks[22], (L, CONV_WIDTH, 2 * D_FF), CONV_WIDTH ** -0.5),
        'conv_b': nrm(ks[23], (L, 2 * D_FF), 0.02),
        'w_down': nrm(ks[24], (L, D_FF, D_MODEL), D_FF ** -0.5),
        'normf_g': 1.0 + nrm(ks[25], (D_MODEL,), 0.05),
    }

def reference(x, norm1_g, w_in, rwkv_mu, w0, w2, a0, a2, g2, k_k, k_a, r_k, lnx_w, lnx_b,
              b_qkv, attn_sink, gate_b, w_proj_a, w_proj_b, w_out, norm2_g, w_up, conv_w,
              conv_b, w_down, normf_g):
    for l in range(DEPTH):
        h = rmsnorm(x, norm1_g[l])
        z = h @ w_in[l]
        z_rwkv, z_qkv, z_gate = jnp.split(z, (RWKV_COLS, RWKV_COLS + QKV_COLS), axis=-1)
        z_qkv = z_qkv + b_qkv[l]
        q, k, v = jnp.split(z_qkv, (Q_COLS, Q_COLS + KV_COLS), axis=-1)
        gates = jax.nn.sigmoid(z_gate + gate_b[l])
        g_a, g_b = jnp.split(gates, N_BRANCH, axis=-1)
        y_a = rwkv7_time_mix(z_rwkv, rwkv_mu[l], w0[l], w2[l], a0[l], a2[l], g2[l],
                             k_k[l], k_a[l], r_k[l], lnx_w[l], lnx_b[l]) @ w_proj_a[l]
        y_b = window_sink_attention(q, k, v, attn_sink[l]) @ w_proj_b[l]
        x = x + (g_a * y_a + g_b * y_b) @ w_out[l]
        x = x + conv_ffn(rmsnorm(x, norm2_g[l]), w_up[l], conv_w[l], conv_b[l], w_down[l])
    return rmsnorm(x, normf_g)


_drawn_inputs = setup_inputs


def setup_inputs(seed=0):
    import zlib

    import numpy as np

    out = dict(_drawn_inputs(seed))
    spreads = {}
    factors = {'w2': 4.484,
     'k_k': 4.216,
     'k_a': 3.26,
     'lnx_w': 3.757,
     'lnx_b': 8.0,
     'b_qkv': 4.393,
     'attn_sink': 8.0,
     'gate_b': 4.425,
     'conv_b': 4.033}
    for name, (base, spread) in spreads.items():
        noise = np.random.default_rng([zlib.crc32(name.encode()), seed]).standard_normal(out[name].shape)
        drawn = base * np.exp(spread * noise) if base else spread * noise
        out[name] = __import__('jax').numpy.asarray(drawn.astype(out[name].dtype))
    for name, factor in factors.items():
        out[name] = (out[name] * factor).astype(out[name].dtype)
    return out
```

```python
from contextlib import ExitStack, contextmanager

import numpy as np

import concourse.bass as bass
from concourse import mybir

F32 = mybir.dt.float32
F32R = mybir.dt.float32r
F16 = mybir.dt.float16
U32 = mybir.dt.uint32
ALU = mybir.AluOpType
ACT = mybir.ActivationFunctionType
AX = mybir.AxisListType.X

P = 128
T = 512
D = 1024
KT = D // P
NT = T // P
C = 128
HD = 64
PAIRS = 8
DFF = 2816
FT = DFF // P
RW = 3328
QKV = 1536
AC = 64
LEVELS = 7
CHAINED = 16
HALF_EXP = float(-0.5 * np.exp(-0.5))
NEG = -1e30

RAW, HL = 4, 2
N_AUX, N_RKV, N_QKV, N_GATE, N_PROJ, N_OUT, N_UP = 0, 2, 26, 38, 54, 70, 78
N_DOWN = N_UP + 2 * FT
N_END = N_DOWN + 3 * KT
DOWN_K = (8, 8, FT - 16)


PARAMS, N_PAR = {}, 0
for _name, _n in (("g1", 8), ("gn2", 8), ("mu", 26), ("w0", 8), ("a0", 8), ("kk", 8), ("ka", 8),
                  ("rk", 8), ("lw", 8), ("lb", 8), ("bq", 12), ("bg", 16),
                  ("cw0", 2 * FT), ("cw1", 2 * FT), ("cw2", 2 * FT), ("cb", 2 * FT)):
    PARAMS[_name] = (N_PAR, _n)
    N_PAR += _n
PAR_ROWS = (126, 88, 88)


class Chain:

    def __init__(self, eng, sem):
        self.eng, self.sem, self.base, self.k = eng, sem, 0, 0

    def __call__(self, ins):
        self.k += 1
        ins.then_inc(self.sem, 1)
        self.eng.wait_ge(self.sem, self.base + self.k)

    @contextmanager
    def loop(self, count, per):
        start = self.base + self.k
        with self.eng.Fori(0, count) as i:
            self.base, self.k = i * per + start, 0
            yield i
            assert self.k == per, f"the body uses the chain {self.k} times"
        self.base, self.k = start + count * per, 0


def build(nc, x, norm1_g, w_in, rwkv_mu, w0, w2, a0, a2, g2, k_k, k_a, r_k, lnx_w, lnx_b,
          b_qkv, attn_sink, gate_b, w_proj_a, w_proj_b, w_out, norm2_g, w_up, conv_w,
          conv_b, w_down, normf_g, out):
    with ExitStack() as ctx:
        def sb(name, shape, dt=F32):
            return ctx.enter_context(nc.sbuf_tensor(name, shape, dt))

        def sem(name):
            return ctx.enter_context(nc.semaphore(name))

        ident = sb("ident", [P, P])
        ident16 = sb("ident16", [P, P], F16)
        nident16 = sb("nident16", [P, P], F16)
        headones = sb("headones", [P, P])
        headmean = sb("headmean", [P, P])
        ones = sb("ones", [P, P])
        level_mask = sb("level_mask", [P, LEVELS, P], F16)
        causal = sb("causal", [P, 2 * C])
        notstart = sb("notstart", [P, T])
        notfirst = sb("notfirst", [P, AC * 9])
        par = sb("par", [P, N_PAR])
        col = {name: par[:, o:o + n] for name, (o, n) in PARAMS.items()}
        omu = sb("omu", [P, 26])
        whalf = sb("whalf", [P, KT])
        ahalf = sb("ahalf", [P, KT])
        eps_col = sb("eps_col", [P, 2])
        sink = sb("sink", [P, 8])
        lora = sb("lora", [P, D])
        g2s = sb("g2s", [P, D])
        lora_w_in = sb("lora_w_in", [P, T])
        lora_a_in = sb("lora_a_in", [P, T])
        lora_g_in = sb("lora_g_in", [P, T])
        raw = sb("raw", [P, RAW, KT, P])
        whi = sb("whi", [P, HL, KT, P], F32R)
        wlo = sb("wlo", [P, HL, KT, P], F32R)
        stat = sb("stat", [P, 16])
        carrier = sb("carrier", [P, 8])

        arena_bytes = (nc.sbuf_top - nc.sbuf_base - 64) // 32 * 32
        arena = sb("arena", [P, arena_bytes // 4])
        base = nc.lookup_mloc(arena).addr
        K = 1024

        def size(shape, dt):
            return (int(np.prod(shape[1:])) * (2 if dt == F16 else 4) + 31) // 32 * 32

        def at(off, name, shape, dt=F32):
            assert off + size(shape, dt) <= arena_bytes, name
            return nc.alloc_sbuf_tensor_at(name, shape, dt, offset=base + off)

        def taker(off, end):
            place = [off]

            def take(name, shape, dt=F32):
                t = at(place[0], name, shape, dt)
                place[0] += size(shape, dt)
                assert place[0] <= end, name
                return t
            return take

        XHL, ZR, QR, KVR = 0, 32 * K, 80 * K, 96 * K
        WR = KVR + 2 * 2 * (T + AC) * 4
        xh = at(XHL, "xh", [P, KT, T], F32R)
        xl = at(XHL + 16 * K, "xl", [P, KT, T], F32R)
        z = at(ZR, "z", [P, 24, T])
        q = at(QR, "q", [P, KT, T])
        kb = at(KVR, "kb", [P, 2, AC + T])
        vb = at(KVR + 2 * (T + AC) * 4, "vb", [P, 2, AC + T])
        xt = at(ZR, "xt", [P, NT, D])
        junk = at(QR, "junk", [P, D])
        rows = at(QR + 4 * K, "rows", [P, 3, P])
        mixed = at(WR, "mixed", [P, 2, T])
        gst = at(WR + 4 * K, "gst", [P, 2, T])

        take = taker(WR + 8 * K, arena_bytes)
        qc = take("qc", [P, KT, AC])
        kc = take("kc", [P, 2, 2, P])
        vc = take("vc", [P, 2, P])
        vtok = take("vtok", [P, 2, P])
        sc = take("sc", [P, 8, P])
        pt = take("pt", [P, 8, P])
        mx = take("mx", [P, 8])
        nmx = take("nmx", [P, 8])
        es = take("es", [P, 8])
        den = take("den", [P, 8])

        take = taker(KVR, arena_bytes)
        gb = take("gb", [P, NT, 2, 2 * C])
        gk = take("gk", [P, NT, 2, 2 * C])
        ar = take("ar", [P, NT, 2 * C])
        xf = take("xf", [P, NT, 2, C])
        bp = take("bp", [P, 2, T])
        kp = take("kp", [P, 2, T])
        vp = take("vp", [P, NT, 4, HD])
        e = take("e", [P, NT, C + 1])
        vfix = take("vfix", [P, T])
        kqn = take("kqn", [P, T])
        wcum = take("wcum", [P, T])
        take = taker(XHL, ZR)
        ei = take("ei", [P, T])
        kkn = take("kkn", [P, T])
        kmod = take("kmod", [P, T])
        t0 = take("t0", [P, T])
        t1 = take("t1", [P, T])
        t2 = take("t2", [P, T])
        btok = take("btok", [P, NT, P])
        ktok = take("ktok", [P, NT, P])
        n1 = take("n1", [P, NT, 2, C], F16)
        n2 = take("n2", [P, NT, 2, C], F16)
        xx = take("xx", [P, NT, 2, C], F16)
        yy = take("yy", [P, NT, 2, C], F16)
        v1 = take("v1", [P, NT, 2, C], F16)
        up = take("up", [P, 4, HD])
        zp = take("zp", [P, 4, HD])
        state = take("state", [P, P])
        stm = take("stm", [P, P])
        lorap = take("lorap", [P, P])
        g2p = take("g2p", [P, P])
        em = take("em", [P, NT])
        dtot = take("dtot", [P, NT])

        yah = at(XHL, "yah", [P, KT, T], F32R)
        yal = at(XHL + 16 * K, "yal", [P, KT, T], F32R)
        ybh = at(ZR + 16 * K, "ybh", [P, KT, T], F32R)
        ybl = at(ZR + 32 * K, "ybl", [P, KT, T], F32R)
        mh = at(ZR, "mh", [P, KT, T], F32R)
        ml = at(QR, "ml", [P, KT, T], F32R)
        gl = at(KVR, "gl", [P, 2, 2, T])
        ta = at(KVR + 8 * K, "ta", [P, 2, T])
        xblk = at(KVR + 12 * K, "xblk", [P, 2, NT, P])
        hh = at(ZR, "hh", [P, FT, T], F32R)
        hl = at(ZR + 2 * K * FT, "hl", [P, FT, T], F32R)
        X1 = ZR + 4 * K * FT
        x1 = at(X1, "x1", [P, KT, T])
        sq1 = at(X1 + 16 * K, "sq1", [P, 2, T])
        rs1 = at(X1 + 20 * K, "rs1", [P, T])
        xnh = at(XHL, "xnh", [P, KT, T], F32R)
        xnl = at(XHL + 16 * K, "xnl", [P, KT, T], F32R)
        cg = at(X1 + 22 * K, "cg", [P, T])
        cv = at(X1 + 24 * K, "cv", [P, T])
        gf = at(X1 + 26 * K, "gf", [P, D])
        yt = at(ZR, "yt", [P, NT, D])

        gates = nc.dram_tensor("gates_scratch", (16, P, T), F32, kind="Internal").ap()
        ps = [ctx.enter_context(nc.psum_tensor(f"ps{b}", [P, T], F32)) for b in range(8)]

        loaded = [sem(f"loaded{b}") for b in range(RAW)]
        w_hi = sem("w_hi")
        w_lo = sem("w_lo")
        slot_done = sem("slot_done")
        ps_free = sem("ps_free")
        half_read = sem("half_read")
        consts = sem("consts")
        pool_chain = sem("pool_chain")
        act_chain = sem("act_chain")
        dve_chain = sem("dve_chain")
        rows_in = sem("rows_in")
        misc_in = sem("misc_in")
        x_in = [sem(f"x_in{j}") for j in range(NT)]
        par_t = sem("par_t")
        par_ready = sem("par_ready")
        x_sq = sem("x_sq")
        x_scaled = sem("x_scaled")
        x_t = sem("x_t")
        xh_ready = sem("xh_ready")
        xl_ready = sem("xl_ready")
        gate_stored = [sem(f"gate_stored{b}") for b in range(2)]
        gate_in = [sem(f"gate_in{b}") for b in range(2)]
        win_in = sem("win_in")
        scores_ps = sem("scores_ps")
        vtok_ps = sem("vtok_ps")
        sc_ready = sem("sc_ready")
        exp_done = sem("exp_done")
        probs_ready = sem("probs_ready")
        pt_ps = sem("pt_ps")
        pt_ready = sem("pt_ready")
        o_ps = sem("o_ps")
        o_done = sem("o_done")
        lora_copied = sem("lora_copied")
        pair_done = sem("pair_done")
        lora_ps = sem("lora_ps")
        sq_ready = sem("sq_ready")
        ss_ps = sem("ss_ps")
        norm_ready = sem("norm_ready")
        tanh_ready = sem("tanh_ready")
        rel_ready = sem("rel_ready")
        exps_ready = sem("exps_ready")
        ops_ready = sem("ops_ready")
        hats_ready = sem("hats_ready")
        rk_ready = sem("rk_ready")
        g_ps = sem("g_ps")
        g_ready = sem("g_ready")
        tok_ps = sem("tok_ps")
        tok_ready = sem("tok_ready")
        n1_ready = sem("n1_ready")
        n2_ready = sem("n2_ready")
        v_ps = sem("v_ps")
        v_ready = sem("v_ready")
        y_ps = sem("y_ps")
        y_ready = sem("y_ready")
        x_ps = sem("x_ps")
        x_ready = sem("x_ready")
        r_ps = sem("r_ps")
        r_ready = sem("r_ready")
        n_ps = sem("n_ps")
        xf_ready = sem("xf_ready")
        z_ps = sem("z_ps")
        z_ready = sem("z_ready")
        u_ps = sem("u_ps")
        u_ready = sem("u_ready")
        s_ps = sem("s_ps")
        s_ready = sem("s_ready")
        out_ps = sem("out_ps")
        y_copied = sem("y_copied")
        mean_ps = sem("mean_ps")
        yc_ready = sem("yc_ready")
        ysq_ready = sem("ysq_ready")
        var_ps = sem("var_ps")
        std_ready = sem("std_ready")
        bonus_ps = sem("bonus_ps")
        gmul_ps = sem("gmul_ps")
        yh_ready = sem("yh_ready")
        yl_ready = sem("yl_ready")
        mix_ready = sem("mix_ready")
        mh_ready = sem("mh_ready")
        ml_ready = sem("ml_ready")
        xblk_in = [sem(f"xblk_in{b}") for b in range(2)]
        sq1_ready = sem("sq1_ready")
        acc_ready = sem("acc_ready")
        tot_ps = sem("tot_ps")
        rms_ready = sem("rms_ready")
        xs_ready = sem("xs_ready")
        xnh_ready = sem("xnh_ready")
        xnl_ready = sem("xnl_ready")
        conv_ready = sem("conv_ready")
        silu_ready = sem("silu_ready")
        h_ready = sem("h_ready")
        hh_ready = sem("hh_ready")
        hl_ready = sem("hl_ready")
        gf_in = sem("gf_in")
        y_t = sem("y_t")
        y_sq = sem("y_sq")
        y_rms = sem("y_rms")
        out_ready = sem("out_ready")
        stored = sem("stored")

        w_in_v = w_in[0].rearrange("(k p) c -> p k c", p=P)
        w_up_v = w_up[0].rearrange("(k p) c -> p k c", p=P)
        w_down_v = w_down[0].rearrange("(k p) c -> p k c", p=P)
        w_out_v = w_out[0].rearrange("(k p) c -> p k c", p=P)
        w_pa_v = w_proj_a[0].rearrange("(k p) c -> p k c", p=P)
        w_pb_v = w_proj_b[0].rearrange("(h k p) c -> h p k c", h=2, p=HD)
        w_q_v = w_in[0, :, RW:RW + D].rearrange("(k p) (h t c) -> h p k t c", p=P, h=2, c=HD)
        w_k_v = w_in[0, :, RW + D:RW + QKV].rearrange("(k p) (b h t c) -> b h p k t c", p=P, b=2,
                                                      h=2, c=HD)
        x_v = x[0].rearrange("(j p) c -> p j c", p=P)
        out_v = out[0].rearrange("(j p) c -> p j c", p=P)

        def flat(ap):
            return ap.rearrange("p a b -> p (a b)")

        def load_values(n, b):
            return (n - b) * 8 + 32

        block = ctx.enter_context(nc.Block())

        @block.sync
        def _(sp):
            def load(n, b, pieces, reuse=True):
                if reuse:
                    sp.wait_ge(w_lo, n - 3)
                for dst, src in pieces:
                    sp.dma_start(dst, src).then_inc(loaded[b], 16)

            def by_k(b, src, kn=KT):
                h = kn // 2
                return [(raw[:, b, 0:h, :], src[:, 0:h]), (raw[:, b, h:kn, :], src[:, h:kn])]

            def by_col(b, lo, hi):
                return [(raw[:, b, :, 0:HD], lo), (raw[:, b, :, HD:P], hi)]

            for j in range(NT):
                sp.dma_start(xt[:, j, :], x_v[:, j, :]).then_inc(x_in[j], 16)
            for n in range(2):
                load(n, n, by_k(n, w_in_v[:, :, 3 * D + n * P:3 * D + (n + 1) * P]), reuse=False)
            for n in range(2, 6):
                load(n, n % RAW, by_k(n % RAW, w_in_v[:, :, (n - 2) * P:(n - 1) * P]), reuse=n >= 4)
            with sp.Fori(0, 5) as i:
                for u in range(4):
                    b = (2 + u) % RAW
                    load(i * 4 + 6 + u, b, by_k(b, w_in_v[:, :, bass.ts(i * 4 + 4 + u, P)]))
            with sp.Fori(0, 2) as i:
                for u in range(4):
                    b = (2 + u) % RAW
                    t = i * 4 + u
                    load(i * 4 + N_QKV + u, b, by_col(b, w_q_v[0][:, :, t, :], w_q_v[1][:, :, t, :]))
            for u in range(4):
                b = (2 + u) % RAW
                kv, g = divmod(u, 2)
                load(N_QKV + 8 + u, b, by_col(b, w_k_v[kv][0][:, :, g, :], w_k_v[kv][1][:, :, g, :]))
            with sp.Fori(0, 4) as i:
                for u in range(4):
                    b = (2 + u) % RAW
                    load(i * 4 + N_GATE + u, b,
                         by_k(b, w_in_v[:, :, RW + QKV:][:, :, bass.ts(i * 4 + u, P)]))
            with sp.Fori(0, 4) as i:
                for u in range(4):
                    b = (2 + u) % RAW
                    cols = bass.ts(i * 2 + u // 2, P)
                    if u % 2 == 0:
                        pieces = by_k(b, w_pa_v[:, :, cols])
                    else:
                        pieces = [(raw[0:HD, b], w_pb_v[0][:, :, cols]),
                                  (raw[HD:P, b], w_pb_v[1][:, :, cols])]
                    load(i * 4 + N_PROJ + u, b, pieces)
            with sp.Fori(0, 2) as i:
                for u in range(4):
                    b = (2 + u) % RAW
                    load(i * 4 + N_OUT + u, b, by_k(b, w_out_v[:, :, bass.ts(i * 4 + u, P)]))
            with sp.Fori(0, FT // 2) as i:
                for u in range(4):
                    b = (2 + u) % RAW
                    src = w_up_v[:, :, (u % 2) * DFF:][:, :, bass.ts(i * 2 + u // 2, P)]
                    load(i * 4 + N_UP + u, b, by_k(b, src))
            with sp.Fori(0, 2) as i:
                for u in range(12):
                    b = (2 + u) % RAW
                    m, s = divmod(u, 3)
                    src = w_down_v[:, 8 * s:8 * s + DOWN_K[s], bass.ts(i * 4 + m, P)]
                    load(i * 12 + N_DOWN + u, b, by_k(b, src, DOWN_K[s]))
            load(N_END, N_END % RAW, by_k(N_END % RAW, w_down_v[:, 0:8, 0:P]))
            for j in range(NT):
                sp.wait_ge(out_ready, j + 1)
                sp.dma_start(out_v[:, j, :], yt[:, j, :]).then_inc(stored, 16)
            sp.wait_ge(stored, 16 * NT)

        @block.gpsimd
        def _(pool):
            chain = Chain(pool, pool_chain)
            for name, src in (("g1", norm1_g[0]), ("gn2", norm2_g[0]), ("mu", rwkv_mu[0]),
                              ("w0", w0[0]), ("a0", a0[0]), ("kk", k_k[0]), ("ka", k_a[0]),
                              ("rk", r_k[0].rearrange("h d -> (h d)")), ("lw", lnx_w[0]),
                              ("lb", lnx_b[0]), ("bg", gate_b[0])):
                o, n = PARAMS[name]
                pool.dma_start(rows[o:o + n, 0, :], src.rearrange("(n p) -> n p", p=P))\
                    .then_inc(rows_in, 16)
            o = PARAMS["bq"][0]
            bq, bk = b_qkv[0][0:D], b_qkv[0][D:QKV]
            bqv = bq.rearrange("(h t d) -> h t d", h=2, d=HD)
            bkv = bk.rearrange("(b h t d) -> b h t d", b=2, h=2, d=HD)
            for h in range(2):
                dst = rows[:, 0, h * HD:(h + 1) * HD]
                pool.dma_start(dst[o:o + 8], bqv[h]).then_inc(rows_in, 16)
                pool.dma_start(dst[o + 8:o + 10], bkv[0][h]).then_inc(rows_in, 16)
                pool.dma_start(dst[o + 10:o + 12], bkv[1][h]).then_inc(rows_in, 16)
            for i in range(3):
                src = conv_w[0][i].rearrange("(n p) -> n p", p=P)
                dst = rows[(i % 2) * 44:(i % 2) * 44 + 44, 1 + i // 2, :]
                pool.dma_start(dst, src).then_inc(rows_in, 16)
            pool.dma_start(rows[44:88, 2, :], conv_b[0].rearrange("(n p) -> n p", p=P))\
                .then_inc(rows_in, 16)
            pool.dma_start(lora[0:HD, :], w2[0]).then_inc(misc_in, 16)
            pool.dma_start(lora[HD:P, :], a2[0]).then_inc(misc_in, 16)
            pool.dma_start(g2s[:, :], g2[0]).then_inc(misc_in, 16)
            sv = attn_sink[0].rearrange("(half g ii b) -> b g ii half", half=2, g=2, ii=2)
            for b in range(2):
                for u in range(4):
                    g, ii = divmod(u, 2)
                    src = sv[b][g][ii:ii + 1].to_broadcast([HD, 2])
                    pool.dma_start(sink[b * HD:(b + 1) * HD, 2 * u:2 * u + 2], src,
                                   allow_slow_non_contiguous=True).then_inc(misc_in, 16)

            def diagonal(t, value):
                chain(pool.memset(t[:, :], 0.0))
                chain(pool.affine_select(out=t[:, :], in_=t[:, :], compare_op=ALU.not_equal,
                                         fill=value, base=0, pattern=[[-1, P]],
                                         channel_multiplier=1))

            diagonal(ident, 1.0)
            diagonal(ident16, 1.0)
            diagonal(nident16, -1.0)
            chain(pool.memset(eps_col[:, 0:1], 1e-6))
            chain(pool.memset(eps_col[:, 1:2], 64e-5))
            chain(pool.memset(ones[:, :], 1.0))
            for t, value in ((headones, 1.0), (headmean, 1.0 / HD)):
                chain(pool.memset(t[:, :], 0.0))
                for h in range(2):
                    chain(pool.memset(t[h * HD:(h + 1) * HD, h * HD:(h + 1) * HD], value))
            chain(pool.memset(causal[:, :], 1.0))
            for o, op in ((0, ALU.is_gt), (C, ALU.is_ge)):
                chain(pool.affine_select(out=causal[:, o:o + C], in_=causal[:, o:o + C],
                                         compare_op=op, fill=0.0, base=0, pattern=[[1, C]],
                                         channel_multiplier=-1))
            chain(pool.memset(level_mask[:, :, :], 0.0))
            for lv in range(LEVELS):
                m = 1 << lv
                view = level_mask[:, lv, :].rearrange("p (a b c) -> p a b c", b=2, c=m)[:, :, 0, :]
                chain(pool.memset(view, 1.0))
                n = P // (2 * m)
                chain(pool.affine_select(out=view, in_=view, compare_op=ALU.is_ge, fill=0.0,
                                         base=-m, pattern=[[-2 * m, n], [0, m]],
                                         channel_multiplier=1))
                chain(pool.affine_select(out=view, in_=view, compare_op=ALU.is_ge, fill=0.0,
                                         base=2 * m - 1, pattern=[[2 * m, n], [0, m]],
                                         channel_multiplier=-1))
            chain(pool.memset(notstart[:, :], 1.0))
            chain(pool.memset(notstart[:, :].rearrange("p (j t) -> p j t", t=C)[:, :, 0:1], 0.0))
            chain(pool.memset(notfirst[:, :], 0.0))
            chain(pool.memset(notfirst[:, 0:AC], NEG))
            chain(pool.memset(lora_w_in[HD:P, :], 0.0))
            chain(pool.memset(lora_a_in[0:HD, :], 0.0))
            chain(pool.memset(kb[:, :, 0:AC], 0.0))
            chain(pool.memset(vb[:, :, 0:AC], 0.0))
            chain(pool.memset(kc[0:HD, :, 1, :], 0.0))
            pool.memset(kc[HD:P, :, 0, :], 0.0).then_inc(consts, 1)

            with pool.Fori(0, 8) as i:
                for u in range(2):
                    pool.wait_ge(ps_free, i * 2 + N_GATE + u + 1)
                    pool.dma_start(gates[i * 2 + u], gst[:, u, :]).then_inc(gate_stored[u], 16)

            pool.wait_ge(o_done, 8)
            for g in gate_stored:
                pool.wait_ge(g, 16 * 8)
            chain(pool.memset(gb[:, :, :, :], 0.0))
            chain(pool.memset(gk[:, :, :, :], 0.0))
            chain(pool.memset(bp[HD:P, 0, :], 0.0))
            chain(pool.memset(bp[0:HD, 1, :], 0.0))
            chain(pool.memset(kp[HD:P, 0, :], 0.0))
            chain(pool.memset(kp[0:HD, 1, :], 0.0))
            chain(pool.memset(vp[:, :, 1:3, :], 0.0))
            chain(pool.memset(up[:, 1:3, :], 0.0))
            pool.memset(zp[:, 1:3, :], 0.0).then_inc(consts, 1)
            pool.wait_ge(misc_in, 16 * 11)
            with pool.Fori(0, PAIRS) as p:
                pool.wait_ge(pair_done, p + 1)
                pool.tensor_copy(lorap[:, :], lora[:, bass.ts(p, P)])
                pool.tensor_copy(g2p[:, :], g2s[:, bass.ts(p, P)]).then_inc(lora_copied, 1)
                pool.wait_ge(n1_ready, p + 1)
                pool.tensor_tensor(n2[:, :, :, :], gb[:, :, :, 0:C], n1[:, :, :, :], ALU.subtract)\
                    .then_inc(n2_ready, 1)

            pool.wait_ge(pair_done, PAIRS + 1)

            def gates_back(m, b):
                pool.dma_start(gl[:, b, 0, :], gates[m]).then_inc(gate_in[b], 16)
                pool.dma_start(gl[:, b, 1, :], gates[m + 8]).then_inc(gate_in[b], 16)

            for m in range(2):
                gates_back(m, m)
            with pool.Fori(0, 3) as i:
                for u in range(2):
                    pool.wait_ge(mix_ready, i * 2 + u + 1)
                    gates_back(i * 2 + 2 + u, u)
            for m in range(2):
                pool.dma_start(xblk[:, m], x_v[:, :, bass.ts(m, P)]).then_inc(xblk_in[m], 16)
            with pool.Fori(0, 3) as i:
                for u in range(2):
                    pool.wait_ge(slot_done, i * 2 + N_OUT + u + 1)
                    pool.dma_start(xblk[:, u], x_v[:, :, bass.ts(i * 2 + 2 + u, P)])\
                        .then_inc(xblk_in[u], 16)
            pool.dma_start(gf[:, :], normf_g.rearrange("(o n) -> o n", o=1).to_broadcast([P, D]))\
                .then_inc(gf_in, 16)
            pool.wait_ge(gf_in, 16)

        @block.scalar
        def _(act):
            chain = Chain(act, act_chain)

            def split(n, b, hb, first=False):
                act.wait_ge(loaded[b], load_values(n, b))
                if not first:
                    act.wait_ge(slot_done, n - 1)
                act.activation(flat(whi[:, hb]), flat(raw[:, b]), ACT.Copy).then_inc(w_hi, 1)

            act.wait_ge(consts, 1)
            for j in range(NT):
                act.wait_ge(x_in[j], 16)
                chain(act.activation(junk[:, :], xt[:, j, :], ACT.Square,
                                     accum_out=stat[:, j:j + 1]))
            act.activation(stat[:, 4:8], stat[:, 0:4], ACT.Sqrt, scale=1.0 / D,
                           bias=eps_col[:, 0:1]).then_inc(x_sq, 1)
            act.wait_ge(par_t, 1)
            act.activation(par[:, :], ps[7][:, 0:N_PAR], ACT.Copy).then_inc(par_ready, 1)
            act.wait_ge(par_ready, 1)
            split(0, 0, 0, first=True)
            split(1, 1, 1, first=True)
            for k in range(KT):
                act.wait_ge(x_t, k + 1)
                act.activation(xh[:, k, :], ps[2 + k % 4][:, :], ACT.Copy,
                               scale=col["g1"][:, k:k + 1]).then_inc(xh_ready, 1)

            def keep(dst, n, bank, mt):
                act.wait_ge(slot_done, n + 1)
                act.activation(dst, ps[bank][:, :], ACT.Copy, scale=omu[:, mt:mt + 1] if
                               isinstance(mt, int) else omu[:, bass.ds(mt, 1)]).then_inc(half_read, 1)

            act.wait_ge(par_ready, 2)
            keep(mixed[:, 0, :], 0, 0, 24)
            split(2, 2, 0)
            keep(mixed[:, 1, :], 1, 1, 25)
            act.wait_ge(ps_free, 2)
            act.activation(lora_w_in[0:HD, :], mixed[0:HD, 0, :], ACT.Tanh)
            act.activation(lora_a_in[HD:P, :], mixed[HD:P, 0, :], ACT.Copy)
            act.activation(lora_g_in[:, :], mixed[:, 1, :], ACT.Sigmoid)
            with act.Fori(0, 6) as i:
                for u in range(4):
                    n, m = i * 4 + N_RKV + u, i * 4 + u
                    split(n + 1, (3 + u) % RAW, (1 + u) % 2)
                    keep(z[:, bass.ds(m, 1), :], n, u % 2, m)

            def biased(dst, n, bank, func, bias):
                act.wait_ge(slot_done, n + 1)
                act.activation(dst, ps[bank][:, :], func, bias=bias).then_inc(ps_free, 1)

            oq = PARAMS["bq"][0]
            with act.Fori(0, 2) as i:
                for u in range(4):
                    n, m = i * 4 + N_QKV + u, i * 4 + u
                    split(n + 1, (3 + u) % RAW, (1 + u) % 2)
                    biased(q[:, bass.ds(m, 1), :], n, u % 2, ACT.Identity,
                           par[:, bass.ds(m + oq, 1)])
            for u in range(4):
                n = N_QKV + 8 + u
                split(n + 1, (3 + u) % RAW, (1 + u) % 2)
                biased((kb, vb)[u // 2][:, u % 2, AC:], n, u % 2, ACT.Identity,
                       par[:, oq + 8 + u:oq + 9 + u])
            og = PARAMS["bg"][0]

            def gate_tile(n, m, u):
                split(n + 1, (3 + u) % RAW, (1 + u) % 2)
                biased(gst[:, u % 2, :], n, u % 2, ACT.Sigmoid, par[:, bass.ds(m + og, 1)])

            for u in range(2):
                gate_tile(N_GATE + u, u, u)
            with act.Fori(0, 3) as i:
                for u in range(4):
                    m = i * 4 + 2 + u
                    act.wait_ge(gate_stored[u % 2], (i * 2 + u // 2) * 16 + 16)
                    gate_tile(m + N_GATE, m, (2 + u) % 4)
            for m in range(14, 16):
                act.wait_ge(gate_stored[m % 2], (m // 2) * 16)
                gate_tile(N_GATE + m, m, m % 4)

            with act.Fori(0, 8) as c:
                win = bass.ds(c * AC, P)
                act.activation(qc[:, :, :], q[:, :, bass.ds(c * AC, AC)], ACT.Copy,
                               scale=HD ** -0.5)
                act.activation(kc[0:HD, :, 0, :], kb[0:HD, :, win], ACT.Copy)
                act.activation(kc[HD:P, :, 1, :], kb[HD:P, :, win], ACT.Copy)
                act.activation(vc[:, :, :], vb[:, :, win], ACT.Copy).then_inc(win_in, 1)
                act.wait_ge(vtok_ps, c + 1)
                act.activation(flat(vtok), ps[4][:, 0:2 * P], ACT.Copy)
                act.wait_ge(sc_ready, c + 1)
                for u in range(8):
                    act.activation(sc[:, u, :], sc[:, u, :], ACT.Exp, bias=nmx[:, u:u + 1],
                                   accum_out=den[:, u:u + 1])
                act.activation(es[:, :], es[:, :], ACT.Exp).then_inc(exp_done, 1)
                act.wait_ge(pt_ps, c + 1)
                for g in range(2):
                    act.activation(flat(pt[:, 4 * g:4 * g + 4, :]), ps[5 + g][:, :], ACT.Copy)\
                        .then_inc(pt_ready, 1)

            act.wait_ge(consts, 2)
            with act.Fori(0, PAIRS) as p:
                v_p = z[:, bass.ds(p + 16, 1), :]
                k_p = z[:, bass.ds(p + 8, 1), :]

                def pcol(name):
                    return par[:, bass.ds(p + PARAMS[name][0], 1)]

                act.wait_ge(pair_done, p + 1)
                act.activation(vfix[:, :], v_p, ACT.Copy)
                act.activation(t2[:, :], k_p, ACT.Square, scale=pcol("kk")).then_inc(sq_ready, 1)
                act.wait_ge(ss_ps, p + 1)
                act.activation(kqn[:, :], ps[4][:, :], ACT.Sqrt).then_inc(norm_ready, 1)
                act.wait_ge(lora_ps, p + 1)
                act.activation(t0[:, :], ps[2][:, :], ACT.Tanh, scale=0.5,
                               bias=whalf[:, bass.ds(p, 1)])
                act.activation(t1[:, :], ps[3][:, :], ACT.Tanh, scale=0.5,
                               bias=ahalf[:, bass.ds(p, 1)]).then_inc(tanh_ready, 1)
                act.wait_ge(rel_ready, p + 1)
                cum = wcum[:, :].rearrange("p (j t) -> p j t", t=C)
                act.activation(e[:, :, 1:C + 1], t0[:, :].rearrange("p (j t) -> p j t", t=C), ACT.Exp)
                act.activation(e[:, :, 0:1], cum[:, :, C // 2 - 1:C // 2], ACT.Exp, scale=-1.0)
                act.activation(em[:, :].unsqueeze(2), cum[:, :, C // 2 - 1:C // 2], ACT.Exp)
                act.activation(dtot[:, :].unsqueeze(2), cum[:, :, C - 1:C], ACT.Exp)
                act.activation(ei[:, :], t0[:, :], ACT.Exp, scale=-1.0).then_inc(exps_ready, 1)
                act.wait_ge(g_ready, p * 8 + 4)
                act.activation(n1[:, :, :, :], gb[:, :, :, 0:C], ACT.Copy).then_inc(n1_ready, 1)
                act.wait_ge(tok_ps, p + 1)
                act.activation(flat(btok), ps[2][:, :], ACT.Copy)
                act.activation(flat(ktok), ps[3][:, :], ACT.Copy)
                act.activation(vp[:, :, 0:4:3, :],
                               ps[4][:, :].rearrange("p (j h v) -> p j h v", h=2, v=HD), ACT.Copy)\
                    .then_inc(tok_ready, 1)
                for lv in range(LEVELS):
                    for g in range(2):
                        act.wait_ge(x_ps, p * (2 * LEVELS) + (2 * lv + g + 1))
                        act.activation(xx[:, 2 * g:2 * g + 2].rearrange("p j h t -> p (j h t)"),
                                       ps[4 + 3 * g][:, :], ACT.Copy).then_inc(x_ready, 1)
                for g in range(2):
                    act.wait_ge(r_ps, p * 2 + g + 1)
                    act.activation(v1[:, 2 * g:2 * g + 2].rearrange("p j h t -> p (j h t)"),
                                   ps[2 + 3 * g][:, :], ACT.Copy).then_inc(r_ready, 1)
                act.wait_ge(out_ps, p + 1)
                act.activation(ei[:, :], ps[7][:, :], ACT.Copy).then_inc(y_copied, 1)
                act.wait_ge(yc_ready, p + 1)
                act.activation(kkn[:, :], ei[:, :], ACT.Square).then_inc(ysq_ready, 1)
                act.wait_ge(var_ps, p + 1)
                act.activation(kkn[:, :], ps[3][:, :], ACT.Sqrt, bias=eps_col[:, 1:2])\
                    .then_inc(std_ready, 1)

            act.wait_ge(pair_done, PAIRS + 1)
            for dst, src in ((yah, z), (ybh, q)):
                for i in range(4):
                    act.activation(flat(dst[:, 2 * i:2 * i + 2]), flat(src[:, 2 * i:2 * i + 2]),
                                   ACT.Copy).then_inc(yh_ready, 1)
            with act.Fori(0, 4) as i:
                for u in range(4):
                    n, m = i * 4 + N_PROJ + u, i * 2 + u // 2
                    split(n + 1, (3 + u) % RAW, (1 + u) % 2)
                    if u % 2:
                        act.wait_ge(mix_ready, m + 1)
                        act.activation(mh[:, bass.ds(m, 1), :], ta[:, u // 2, :], ACT.Copy)\
                            .then_inc(mh_ready, 1)
            with act.Fori(0, 2) as i:
                for u in range(4):
                    n, m = i * 4 + N_OUT + u, i * 4 + u
                    split(n + 1, (3 + u) % RAW, (1 + u) % 2)
                    act.wait_ge(slot_done, n + 1)
                    act.activation(x1[:, bass.ds(m, 1), :], ps[u % 2][:, :], ACT.Copy)
                    act.wait_ge(acc_ready, m + 1)
                    act.activation(sq1[:, 0, :], ps[u % 2][:, :], ACT.Square).then_inc(ps_free, 1)
            act.wait_ge(tot_ps, 1)
            act.activation(rs1[:, :], ps[2][:, :], ACT.Sqrt, scale=1.0 / D, bias=eps_col[:, 0:1])\
                .then_inc(rms_ready, 1)
            for k in range(KT):
                act.wait_ge(xs_ready, k + 1)
                act.activation(xnh[:, k, :], sq1[:, k % 2, :], ACT.Copy,
                               scale=col["gn2"][:, k:k + 1]).then_inc(xnh_ready, 1)
            with act.Fori(0, FT // 2) as i:
                for u in range(4):
                    n, j = i * 4 + N_UP + u, i * 2 + u // 2
                    split(n + 1, (3 + u) % RAW, (1 + u) % 2)
                    act.wait_ge(slot_done, n + 1)
                    c, half = (cg, cv)[u % 2], (u % 2) * FT
                    act.activation(c[:, :], ps[u % 2][:, :], ACT.Identity,
                                   scale=par[:, bass.ds(j + (PARAMS["cw2"][0] + half), 1)],
                                   bias=par[:, bass.ds(j + (PARAMS["cb"][0] + half), 1)])\
                        .then_inc(half_read, 1)
                    if u % 2 == 0:
                        act.wait_ge(ps_free, n + 1)
                        act.activation(cg[:, :], cg[:, :], ACT.Silu).then_inc(silu_ready, 1)
                    else:
                        act.wait_ge(h_ready, j + 1)
                        act.activation(hh[:, bass.ds(j, 1), :], cv[:, :], ACT.Copy)\
                            .then_inc(hh_ready, 1)
            with act.Fori(0, 2) as i:
                for u in range(12):
                    split(i * 12 + N_DOWN + u + 1, (3 + u) % RAW, (1 + u) % 2)
            for j in range(NT):
                act.wait_ge(y_t, j + 1)
                for h in range(2):
                    chain(act.activation(sq1[:, 0, :], ps[2 + 2 * (j % 2) + h][:, :], ACT.Square,
                                         accum_out=stat[:, 2 * j + h:2 * j + h + 1]))
                act.activation(stat[:, 8 + j:9 + j], stat[:, 2 * j:2 * j + 1], ACT.Identity,
                               bias=stat[:, 2 * j + 1:2 * j + 2]).then_inc(y_sq, 1)
                act.wait_ge(y_sq, 2 * j + 1)
                act.activation(stat[:, 8 + j:9 + j], stat[:, 8 + j:9 + j], ACT.Sqrt, scale=1.0 / D,
                               bias=eps_col[:, 0:1]).then_inc(y_sq, 1)

        @block.vector
        def _(dve):
            chain = Chain(dve, dve_chain)

            def split(n, b, hb):
                dve.wait_ge(w_hi, n + 1)
                dve.tensor_tensor(flat(wlo[:, hb]), flat(raw[:, b]), flat(whi[:, hb]).bitcast(F32),
                                  ALU.subtract).then_inc(w_lo, 1)

            def lo_part(dst, src, hi, s, k):
                dve.tensor_tensor(dst, src, hi.bitcast(F32), ALU.subtract).then_inc(s, k)

            dve.wait_ge(x_sq, 1)
            chain(dve.reciprocal(stat[:, 8:12], stat[:, 4:8]))
            for j in range(NT):
                dve.tensor_scalar(xt[:, j, :], xt[:, j, :], stat[:, 8 + j:9 + j], None, ALU.mult)\
                    .then_inc(x_scaled, 1)
            dve.wait_ge(par_ready, 1)
            dve.tensor_scalar(whalf[:, :], col["w0"], 0.5, None, ALU.mult)
            dve.tensor_scalar(ahalf[:, :], col["a0"], 0.5, None, ALU.mult)
            dve.tensor_scalar(omu[:, :], col["mu"], -1.0, 1.0, ALU.mult, ALU.add)\
                .then_inc(par_ready, 1)
            split(0, 0, 0)
            split(1, 1, 1)
            for k in range(KT):
                dve.wait_ge(xh_ready, k + 1)
                dve.scalar_tensor_tensor(xl[:, k, :], ps[2 + k % 4][:, :], col["g1"][:, k:k + 1],
                                         xh[:, k, :].bitcast(F32), ALU.mult, ALU.subtract)\
                    .then_inc(xl_ready, 1)

            om = PARAMS["mu"][0]

            def shift(dst, n, bank, mt):
                dve.wait_ge(half_read, n + 1)
                dve.scalar_tensor_tensor(dst[:, 1:T], ps[bank][:, 0:T - 1],
                                         par[:, bass.ds(mt + om, 1)], dst[:, 1:T], ALU.mult,
                                         ALU.add).then_inc(ps_free, 1)

            shift(mixed[:, 0, :], 0, 0, 24)
            split(2, 2, 0)
            shift(mixed[:, 1, :], 1, 1, 25)
            with dve.Fori(0, 6) as i:
                for u in range(4):
                    n, m = i * 4 + N_RKV + u, i * 4 + u
                    split(n + 1, (3 + u) % RAW, (1 + u) % 2)
                    shift(z[:, bass.ds(m, 1), :].rearrange("p a t -> p (a t)"), n, u % 2, m)
            with dve.Fori(0, 7) as i:
                for u in range(4):
                    split(i * 4 + N_QKV + u + 1, (3 + u) % RAW, (1 + u) % 2)

            dve.wait_ge(misc_in, 16 * 11)
            with chain.loop(8, 5) as c:
                mask = notfirst[:, bass.ds(c * AC, P)].unsqueeze(1).to_broadcast([P, 4, P])
                dve.wait_ge(scores_ps, c + 1)
                for g in range(2):
                    s = dve.tensor_tensor(sc[:, 4 * g:4 * g + 4, :],
                                          ps[2 + g][:, :].rearrange("p (u k) -> p u k", k=P),
                                          mask, ALU.add)
                chain(s)
                chain(dve.tensor_reduce(mx[:, :], sc[:, :, :], AX, ALU.max))
                chain(dve.tensor_tensor(mx[:, :], mx[:, :], sink[:, :], ALU.max))
                dve.tensor_scalar(nmx[:, :], mx[:, :], -1.0, None, ALU.mult)
                dve.tensor_tensor(es[:, :], sink[:, :], mx[:, :], ALU.subtract)\
                    .then_inc(sc_ready, 1)
                dve.wait_ge(exp_done, c + 1)
                chain(dve.tensor_tensor(den[:, :], den[:, :], es[:, :], ALU.add))
                chain(dve.reciprocal(den[:, :], den[:, :]))
                dve.tensor_tensor(sc[:, :, :], sc[:, :, :],
                                  den[:, :].unsqueeze(2).to_broadcast([P, 8, P]), ALU.mult)\
                    .then_inc(probs_ready, 1)
                dve.wait_ge(o_ps, c + 1)
                dve.tensor_copy(q[:, :, bass.ds(c * AC, AC)],
                                ps[7][:, :].rearrange("p (t s) -> p t s", s=AC)).then_inc(o_done, 1)

            dve.wait_ge(consts, 2)
            dve.sem_inc(pair_done, 1)
            with chain.loop(PAIRS, CHAINED) as p:
                r_p = z[:, bass.ds(p, 1), :].rearrange("p a t -> p (a t)")
                k_p = z[:, bass.ds(p + 8, 1), :].rearrange("p a t -> p (a t)")

                def pcol(name):
                    return par[:, bass.ds(p + PARAMS[name][0], 1)]

                def chunks(t):
                    return t.rearrange("p (j t) -> p j t", t=C)

                dve.memset(state[:, :], 0.0)
                dve.memset(stm[:, :], 0.0).then_inc(s_ready, 1)
                dve.wait_ge(tanh_ready, p + 1)
                chain(dve.tensor_scalar(t0[:, :], t0[:, :], 1.0, HALF_EXP, ALU.add, ALU.mult))
                chain(dve.tensor_tensor_scan(wcum[:, :], notstart[:, :], t0[:, :], 0.0, ALU.mult,
                                             ALU.add))
                dve.tensor_tensor(chunks(t0[:, :]), chunks(wcum[:, :]),
                                  chunks(wcum[:, :])[:, :, C // 2 - 1:C // 2].to_broadcast(
                                      [P, NT, C]), ALU.subtract).then_inc(rel_ready, 1)
                chain(dve.tensor_scalar(t1[:, :], t1[:, :], 0.5, 0.5, ALU.mult, ALU.add))
                dve.wait_ge(norm_ready, p + 1)
                chain(dve.tensor_scalar(kqn[:, :], kqn[:, :], 1e-12, None, ALU.max))
                chain(dve.reciprocal(kqn[:, :], kqn[:, :]))
                dve.scalar_tensor_tensor(kkn[:, :], k_p, pcol("kk"), kqn[:, :], ALU.mult, ALU.mult)
                chain(dve.tensor_scalar(t2[:, :], t1[:, :], 1.0, pcol("ka"), ALU.subtract, ALU.mult))
                dve.scalar_tensor_tensor(kmod[:, :], t2[:, :], 1.0, k_p, ALU.add, ALU.mult)
                chain(dve.tensor_tensor(t1[:, :], kkn[:, :], t1[:, :], ALU.mult))
                dve.wait_ge(exps_ready, p + 1)
                dve.scalar_tensor_tensor(ar[:, :, 0:C], chunks(kkn[:, :]), -1.0, e[:, :, 0:C],
                                         ALU.mult, ALU.mult)
                dve.tensor_tensor(ar[:, :, C:2 * C], chunks(r_p), e[:, :, 1:C + 1], ALU.mult)
                for h in range(2):
                    hs = slice(h * HD, (h + 1) * HD)
                    dve.tensor_tensor(bp[hs, h, :], t1[hs, :], ei[hs, :], ALU.mult)
                    last = dve.tensor_tensor(kp[hs, h, :], kmod[hs, :], ei[hs, :], ALU.mult)
                last.then_inc(ops_ready, 1)
                chain(dve.tensor_tensor(chunks(t0[:, :]), chunks(ei[:, :]),
                                        e[:, :, C:C + 1].to_broadcast([P, NT, C]), ALU.mult))
                dve.tensor_tensor(t1[:, :], t1[:, :], t0[:, :], ALU.mult)
                dve.tensor_tensor(t0[:, :], kmod[:, :], t0[:, :], ALU.mult).then_inc(hats_ready, 1)
                dve.scalar_tensor_tensor(t2[:, :], r_p, pcol("rk"), kmod[:, :], ALU.mult, ALU.mult)\
                    .then_inc(rk_ready, 1)
                for f in range(8):
                    dst = (gb, gk)[f // 4][:, f % 4]
                    dve.wait_ge(g_ps, p * 8 + f + 1)
                    dve.memset(carrier[:, f:f + 1], 0.0)
                    dve.copy_predicated(dst, causal[:, :].bitcast(U32).unsqueeze(1)
                                        .to_broadcast([P, 2, 2 * C]),
                                        ps[2 + f % 6][:, :].rearrange("p (h t) -> p h t", h=2))\
                        .then_inc(g_ready, 1)
                for lv in range(LEVELS):
                    for g in range(2):
                        dve.wait_ge(v_ps, p * (2 * LEVELS) + (2 * lv + g + 1))
                        mask = level_mask[:, lv, :].unsqueeze(1).to_broadcast([P, 4, C])
                        dve.tensor_tensor(v1[:, 2 * g:2 * g + 2].rearrange("p j h t -> p (j h) t"),
                                          ps[2 + 3 * g][:, :].rearrange("p (u t) -> p u t", t=C),
                                          mask, ALU.mult).then_inc(v_ready, 1)
                    for g in range(2):
                        yg = yy[:, 2 * g:2 * g + 2].rearrange("p j h t -> p (j h) t")
                        dve.wait_ge(y_ps, p * (2 * LEVELS) + (2 * lv + g + 1))
                        dve.tensor_tensor(yg, ps[3 + 3 * g][:, :].rearrange("p (u t) -> p u t", t=C),
                                          yg if lv else
                                          ident16[:, :].unsqueeze(1).to_broadcast([P, 4, C]),
                                          ALU.add).then_inc(y_ready, 1)
                for g in range(2):
                    dve.wait_ge(n_ps, p * 2 + g + 1)
                    dve.tensor_tensor(xf[:, 2 * g:2 * g + 2].rearrange("p j h t -> p (j h t)"),
                                      ps[4 + 3 * g][:, :],
                                      xx[:, 2 * g:2 * g + 2].rearrange("p j h t -> p (j h t)"),
                                      ALU.add).then_inc(xf_ready, 1)
                for j in range(NT):
                    dve.wait_ge(z_ps, p * NT + j + 1)
                    dve.tensor_copy(zp[:, 0:4:3, :],
                                    ps[2][:, 0:P].rearrange("p (h v) -> p h v", h=2))\
                        .then_inc(z_ready, 1)
                    dve.wait_ge(u_ps, p * NT + j + 1)
                    dve.tensor_copy(up[:, 0:4:3, :],
                                    ps[3][:, 0:P].rearrange("p (h v) -> p h v", h=2))\
                        .then_inc(u_ready, 1)
                    if j < NT - 1:
                        dve.wait_ge(s_ps, p * (NT - 1) + j + 1)
                        chain(dve.scalar_tensor_tensor(state[:, :], state[:, :], dtot[:, j:j + 1],
                                                       ps[4][:, 0:P], ALU.mult, ALU.add))
                        dve.scalar_tensor_tensor(stm[:, :], state[:, :], em[:, j + 1:j + 2],
                                                 headones[:, :], ALU.mult, ALU.mult)\
                            .then_inc(s_ready, 1)
                dve.wait_ge(mean_ps, p + 1)
                dve.tensor_tensor(ei[:, :], ei[:, :], ps[2][:, :], ALU.subtract).then_inc(yc_ready, 1)
                dve.wait_ge(bonus_ps, p + 1)
                chain(dve.tensor_tensor(t2[:, :], vfix[:, :], ps[4][:, :], ALU.mult))
                dve.wait_ge(std_ready, p + 1)
                chain(dve.reciprocal(kkn[:, :], kkn[:, :]))
                chain(dve.tensor_tensor(ei[:, :], ei[:, :], kkn[:, :], ALU.mult))
                chain(dve.tensor_scalar(ei[:, :], ei[:, :], pcol("lw"), pcol("lb"), ALU.mult, ALU.add))
                chain(dve.tensor_tensor(ei[:, :], ei[:, :], t2[:, :], ALU.add))
                dve.wait_ge(gmul_ps, p + 1)
                dve.tensor_tensor(r_p, ei[:, :], ps[5][:, :], ALU.mult).then_inc(pair_done, 1)

            for t, (dst, src, hi) in enumerate(((yal, z, yah), (ybl, q, ybh))):
                for i in range(4):
                    dve.wait_ge(yh_ready, 4 * t + i + 1)
                    lo_part(flat(dst[:, 2 * i:2 * i + 2]), flat(src[:, 2 * i:2 * i + 2]),
                            flat(hi[:, 2 * i:2 * i + 2]), yl_ready, 1)
            with dve.Fori(0, 4) as i:
                for u in range(4):
                    n, m = i * 4 + N_PROJ + u, i * 2 + u // 2
                    split(n + 1, (3 + u) % RAW, (1 + u) % 2)
                    dve.wait_ge(slot_done, n + 1)
                    if u % 2 == 0:
                        dve.wait_ge(gate_in[u // 2], i * 32 + 32)
                        dve.tensor_tensor(ta[:, u // 2, :], ps[0][:, :], gl[:, u // 2, 0, :],
                                          ALU.mult).then_inc(ps_free, 1)
                    else:
                        dve.tensor_tensor(gl[:, u // 2, 1, :], ps[1][:, :], gl[:, u // 2, 1, :],
                                          ALU.mult).then_inc(ps_free, 1)
                        dve.wait_ge(ps_free, n + 1)
                        dve.tensor_tensor(ta[:, u // 2, :], ta[:, u // 2, :], gl[:, u // 2, 1, :],
                                          ALU.add).then_inc(mix_ready, 1)
                        dve.wait_ge(mh_ready, m + 1)
                        lo_part(ml[:, bass.ds(m, 1), :], ta[:, u // 2, :].unsqueeze(1),
                                mh[:, bass.ds(m, 1), :], ml_ready, 1)
            dve.memset(rs1[:, :], 0.0).then_inc(acc_ready, 1)
            with dve.Fori(0, 2) as i:
                for u in range(4):
                    n, m = i * 4 + N_OUT + u, i * 4 + u
                    split(n + 1, (3 + u) % RAW, (1 + u) % 2)
                    dve.wait_ge(ps_free, n + 1)
                    dve.wait_ge(acc_ready, m + 1)
                    dve.tensor_tensor(rs1[:, :], rs1[:, :], sq1[:, 0, :], ALU.add)\
                        .then_inc(acc_ready, 1)
            dve.wait_ge(rms_ready, 1)
            chain(dve.reciprocal(rs1[:, :], rs1[:, :]))
            for k in range(KT):
                dve.tensor_tensor(sq1[:, k % 2, :], x1[:, k, :], rs1[:, :], ALU.mult)\
                    .then_inc(xs_ready, 1)
                dve.wait_ge(xnh_ready, k + 1)
                dve.scalar_tensor_tensor(xnl[:, k, :], sq1[:, k % 2, :], col["gn2"][:, k:k + 1],
                                         xnh[:, k, :].bitcast(F32), ALU.mult, ALU.subtract)\
                    .then_inc(xnl_ready, 1)
            with chain.loop(FT // 2, 4) as i:
                for u in range(4):
                    n, j = i * 4 + N_UP + u, i * 2 + u // 2
                    split(n + 1, (3 + u) % RAW, (1 + u) % 2)
                    c, half = (cg, cv)[u % 2], (u % 2) * FT
                    dve.wait_ge(half_read, n - (N_UP - 26) + 1)
                    chain(dve.scalar_tensor_tensor(
                        c[:, 1:T], ps[u % 2][:, 0:T - 1],
                        par[:, bass.ds(j + (PARAMS["cw1"][0] + half), 1)], c[:, 1:T],
                        ALU.mult, ALU.add))
                    dve.scalar_tensor_tensor(
                        c[:, 2:T], ps[u % 2][:, 0:T - 2],
                        par[:, bass.ds(j + (PARAMS["cw0"][0] + half), 1)], c[:, 2:T],
                        ALU.mult, ALU.add).then_inc(ps_free, 1)
                    if u % 2:
                        dve.wait_ge(ps_free, n + 1)
                        dve.wait_ge(silu_ready, j + 1)
                        dve.tensor_tensor(cv[:, :], cv[:, :], cg[:, :], ALU.mult)\
                            .then_inc(h_ready, 1)
                        dve.wait_ge(hh_ready, j + 1)
                        dve.tensor_tensor(hl[:, bass.ds(j, 1), :], cv[:, :],
                                          hh[:, bass.ds(j, 1), :].bitcast(F32),
                                          ALU.subtract).then_inc(hl_ready, 1)
            with dve.Fori(0, 2) as i:
                for u in range(12):
                    n = i * 12 + N_DOWN + u
                    split(n + 1, (3 + u) % RAW, (1 + u) % 2)
                    if u % 3 == 2:
                        m = i * 4 + u // 3
                        xm = x1[:, bass.ds(m, 1), :]
                        dve.wait_ge(slot_done, n + 1)
                        dve.tensor_tensor(xm, xm, ps[(u // 3) % 2][:, :], ALU.add)\
                            .then_inc(ps_free, 1)
            dve.wait_ge(gf_in, 16)
            for j in range(NT):
                dve.wait_ge(y_sq, 2 * j + 2)
                chain(dve.reciprocal(stat[:, 12 + j:13 + j], stat[:, 8 + j:9 + j]))
                for h in range(2):
                    last = dve.scalar_tensor_tensor(
                        yt[:, j, h * T:(h + 1) * T], ps[2 + 2 * (j % 2) + h][:, :],
                        stat[:, 12 + j:13 + j], gf[:, h * T:(h + 1) * T], ALU.mult, ALU.mult)
                last.then_inc(out_ready, 1)

        @block.tensor
        def _(pe):
            def product(n, hb, bank, hi, lo, kn=KT, first=True, last=True, tile_n=None,
                        before_last=None):
                pe.wait_ge(w_lo, n + 1)
                if first and tile_n is not None:
                    pe.wait_ge(ps_free, tile_n - 1)
                for k in range(kn):
                    pe.matmul(ps[bank][:, :], whi[:, hb, k, :], hi(k), start=first and k == 0,
                              stop=False)
                    pe.matmul(ps[bank][:, :], whi[:, hb, k, :], lo(k), start=False, stop=False)
                    if k == kn - 1 and before_last:
                        before_last()
                    ins = pe.matmul(ps[bank][:, :], wlo[:, hb, k, :], hi(k), start=False,
                                    stop=last and k == kn - 1)
                ins.then_inc(slot_done, 1)

            pe.wait_ge(consts, 1)
            pe.wait_ge(rows_in, 16 * 21)
            o = 0
            for i, n in enumerate(PAR_ROWS):
                ins = pe.transpose(ps[7][:, o:o + n], rows[0:n, i, :], ident[0:n, 0:n])
                o += n
            ins.then_inc(par_t, 1)
            pe.wait_ge(x_scaled, NT)
            for k in range(KT):
                if k >= 4:
                    pe.wait_ge(xl_ready, k - 3)
                for j in range(NT):
                    ins = pe.transpose(ps[2 + k % 4][:, j * P:(j + 1) * P],
                                       xt[:, j, k * P:(k + 1) * P], ident[:, :])
                ins.then_inc(x_t, 1)
            pe.wait_ge(xl_ready, KT)

            def xs(t):
                return lambda k: t[:, k, :]

            for n in range(2):
                product(n, n % 2, n % 2, xs(xh), xs(xl))
            for n0, cnt in ((N_RKV, 6), (N_QKV, 7)):
                with pe.Fori(0, cnt) as i:
                    for u in range(4):
                        n = i * 4 + n0 + u
                        product(n, u % 2, u % 2, xs(xh), xs(xl), tile_n=n)

            with pe.Fori(0, 8) as c:
                pe.wait_ge(win_in, c + 1)
                for g in range(2):
                    for ii in range(2):
                        t = 4 * g + 2 * ii
                        ins = pe.matmul(ps[2 + g][:, ii * 2 * P:(ii + 1) * 2 * P],
                                        flat(qc[:, t:t + 2, :]),
                                        flat(kc[:, g, :, :]), start=True, stop=True)
                ins.then_inc(scores_ps, 1)
                for g in range(2):
                    ins = pe.transpose(ps[4][:, g * P:(g + 1) * P], vc[:, g, :], ident[:, :])
                ins.then_inc(vtok_ps, 1)
                pe.wait_ge(probs_ready, c + 1)
                for u in range(8):
                    ins = pe.transpose(ps[5 + u // 4][:, (u % 4) * P:(u % 4 + 1) * P], sc[:, u, :],
                                       ident[:, :])
                ins.then_inc(pt_ps, 1)
                for u in range(8):
                    if u % 4 == 0:
                        pe.wait_ge(pt_ready, c * 2 + u // 4 + 1)
                    g, ii, half = u // 4, (u // 2) % 2, u % 2
                    t = 4 * g + 2 * ii
                    ins = pe.matmul(ps[7][half * HD:(half + 1) * HD, t * AC:(t + 2) * AC],
                                    vtok[:, g, half * HD:(half + 1) * HD], pt[:, u, :],
                                    start=True, stop=True)
                ins.then_inc(o_ps, 1)

            pe.wait_ge(o_done, 8)
            with pe.Fori(0, PAIRS) as p:
                pe.wait_ge(pair_done, p + 1)
                pe.wait_ge(lora_copied, p + 1)
                pe.matmul(ps[2][:, :], lorap[:, :], lora_w_in[:, :], start=True, stop=True)
                pe.matmul(ps[3][:, :], lorap[:, :], lora_a_in[:, :], start=True, stop=True)\
                    .then_inc(lora_ps, 1)
                pe.wait_ge(sq_ready, p + 1)
                pe.matmul(ps[4][:, :], headones[:, :], t2[:, :], start=True, stop=True)\
                    .then_inc(ss_ps, 1)
                pe.wait_ge(ops_ready, p + 1)
                for f in range(8):
                    src, j = (bp, kp)[f // 4], f % 4
                    if f >= 6:
                        pe.wait_ge(g_ready, p * 8 + f - 5)
                    for h in range(2):
                        ins = pe.matmul(ps[2 + f % 6][:, h * 2 * C:(h + 1) * 2 * C],
                                        src[:, h, j * C:(j + 1) * C], ar[:, j, :],
                                        start=True, stop=True)
                    ins.then_inc(g_ps, 1)
                pe.wait_ge(hats_ready, p + 1)
                pe.wait_ge(g_ready, p * 8 + 8)
                for b, src in ((2, t1), (3, t0), (4, vfix)):
                    for j in range(NT):
                        ins = pe.transpose(ps[b][:, j * P:(j + 1) * P], src[:, j * P:(j + 1) * P],
                                           ident[:, :])
                ins.then_inc(tok_ps, 1)
                pe.wait_ge(tok_ready, p + 1)
                pe.wait_ge(n1_ready, p + 1)
                L2 = 2 * LEVELS
                for lv in range(LEVELS):
                    for g in range(2):
                        if lv:
                            pe.wait_ge(y_ready, p * L2 + (2 * (lv - 1) + g + 1))
                        for u in range(4):
                            j, h = 2 * g + u // 2, u % 2
                            ins = pe.matmul(ps[2 + 3 * g][:, u * C:(u + 1) * C], n1[:, j, h, :],
                                            yy[:, j, h, :] if lv else ident16[:, :],
                                            start=True, stop=True)
                        ins.then_inc(v_ps, 1)
                    for g in range(2):
                        pe.wait_ge(v_ready, p * L2 + (2 * lv + g + 1))
                        if lv:
                            pe.wait_ge(x_ready, p * L2 + (2 * (lv - 1) + g + 1))
                        for u in range(4):
                            j, h = 2 * g + u // 2, u % 2
                            ins = pe.matmul(ps[3 + 3 * g][:, u * C:(u + 1) * C],
                                            xx[:, j, h, :] if lv else ident16[:, :],
                                            v1[:, j, h, :], start=True, stop=True)
                        ins.then_inc(y_ps, 1)
                        for u in range(4):
                            j, h = 2 * g + u // 2, u % 2
                            x_u = xx[:, j, h, :] if lv else ident16[:, :]
                            o = ps[4 + 3 * g][:, u * C:(u + 1) * C]
                            pe.matmul(o, ident16[:, :], x_u, start=True, stop=False)
                            ins = pe.matmul(o, v1[:, j, h, :], x_u, start=False, stop=True)
                        ins.then_inc(x_ps, 1)
                pe.wait_ge(n2_ready, p + 1)
                for g in range(2):
                    pe.wait_ge(y_ready, p * L2 + (2 * (LEVELS - 1) + g + 1))
                    for u in range(4):
                        j, h = 2 * g + u // 2, u % 2
                        o = ps[2 + 3 * g][:, u * C:(u + 1) * C]
                        pe.matmul(o, ident16[:, :], ident16[:, :], start=True, stop=False)
                        pe.matmul(o, nident16[:, :], yy[:, j, h, :], start=False, stop=False)
                        pe.matmul(o, n1[:, j, h, :], yy[:, j, h, :], start=False, stop=False)
                        ins = pe.matmul(o, n2[:, j, h, :], yy[:, j, h, :], start=False, stop=True)
                    ins.then_inc(r_ps, 1)
                for g in range(2):
                    pe.wait_ge(r_ready, p * 2 + g + 1)
                    for u in range(4):
                        j, h = 2 * g + u // 2, u % 2
                        ins = pe.matmul(ps[4 + 3 * g][:, u * C:(u + 1) * C], v1[:, j, h, :],
                                        xx[:, j, h, :], start=True, stop=True)
                    ins.then_inc(n_ps, 1)
                pe.wait_ge(xf_ready, p * 2 + 2)
                pe.wait_ge(s_ready, p * NT + 1)
                for j in range(NT):
                    v_h = [flat(vp[:, j, 2 * h:2 * h + 2, :]) for h in range(2)]
                    z_h = [flat(zp[:, 2 * h:2 * h + 2, :]) for h in range(2)]
                    u_h = [flat(up[:, 2 * h:2 * h + 2, :]) for h in range(2)]
                    for h in range(2):
                        pe.matmul(ps[2][:, 0:P], gk[:, j, h, 0:C], v_h[h], start=h == 0, stop=False)
                    if j:
                        pe.wait_ge(s_ready, p * NT + j + 1)
                    pe.matmul(ps[2][:, 0:P], ar[:, j, 0:C], stm[:, :], start=False, stop=True)\
                        .then_inc(z_ps, 1)
                    o = ps[7][:, j * C:(j + 1) * C]
                    pe.matmul(o, stm[:, :], ar[:, j, C:2 * C], start=True, stop=False)
                    for h in range(2):
                        pe.matmul(o, v_h[h], gk[:, j, h, C:2 * C], start=False, stop=False)
                    if j < NT - 1:
                        pe.matmul(ps[4][:, 0:P], ktok[:, j, :], vp[:, j, 0:4:3, :], start=True,
                                  stop=False)
                    pe.wait_ge(z_ready, p * NT + j + 1)
                    pe.matmul(ps[3][:, 0:P], xf[:, j, 0, :], z_h[0], start=True, stop=False)
                    pe.matmul(ps[3][:, 0:P], xf[:, j, 1, :], z_h[1], start=False, stop=True)\
                        .then_inc(u_ps, 1)
                    pe.wait_ge(u_ready, p * NT + j + 1)
                    if j < NT - 1:
                        pe.matmul(ps[4][:, 0:P], btok[:, j, :], up[:, 0:4:3, :], start=False,
                                  stop=True).then_inc(s_ps, 1)
                    pe.matmul(o, u_h[0], gb[:, j, 0, C:2 * C], start=False, stop=False)
                    ins = pe.matmul(o, u_h[1], gb[:, j, 1, C:2 * C], start=False, stop=True)
                ins.then_inc(out_ps, 1)
                pe.wait_ge(y_copied, p + 1)
                pe.matmul(ps[2][:, :], headmean[:, :], ei[:, :], start=True, stop=True)\
                    .then_inc(mean_ps, 1)
                pe.wait_ge(rk_ready, p + 1)
                pe.matmul(ps[4][:, :], headones[:, :], t2[:, :], start=True, stop=True)\
                    .then_inc(bonus_ps, 1)
                pe.matmul(ps[5][:, :], g2p[:, :], lora_g_in[:, :], start=True, stop=True)\
                    .then_inc(gmul_ps, 1)
                pe.wait_ge(ysq_ready, p + 1)
                pe.matmul(ps[3][:, :], headmean[:, :], kkn[:, :], start=True, stop=True)\
                    .then_inc(var_ps, 1)

            pe.wait_ge(yl_ready, 8)
            with pe.Fori(0, 4) as i:
                for u in range(4):
                    n = i * 4 + N_PROJ + u
                    hi, lo = ((yah, yal), (ybh, ybl))[u % 2]
                    product(n, u % 2, u % 2, xs(hi), xs(lo), tile_n=n)
            pe.wait_ge(ml_ready, KT)
            with pe.Fori(0, 2) as i:
                for u in range(4):
                    n, m = i * 4 + N_OUT + u, i * 4 + u

                    def residual():
                        pe.wait_ge(xblk_in[u % 2], (i * 2 + u // 2) * 16 + 16)
                        for j in range(NT):
                            pe.matmul(ps[u % 2][:, j * P:(j + 1) * P], xblk[:, u % 2, j, :],
                                      ident[:, :], start=False, stop=False)

                    product(n, u % 2, u % 2, xs(mh), xs(ml), tile_n=n, before_last=residual)
            pe.wait_ge(acc_ready, 9)
            pe.matmul(ps[2][:, :], ones[:, :], rs1[:, :], start=True, stop=True).then_inc(tot_ps, 1)
            pe.wait_ge(xnl_ready, KT)
            with pe.Fori(0, FT // 2) as i:
                for u in range(4):
                    n = i * 4 + N_UP + u
                    product(n, u % 2, u % 2, xs(xnh), xs(xnl), tile_n=n)
            pe.wait_ge(hl_ready, FT)
            with pe.Fori(0, 2) as i:
                for u in range(12):
                    n = i * 12 + N_DOWN + u
                    m, s = divmod(u, 3)
                    product(n, u % 2, m % 2, lambda k: hh[:, 8 * s + k, :],
                            lambda k: hl[:, 8 * s + k, :], kn=DOWN_K[s], first=s == 0,
                            last=s == 2, tile_n=i * 4 + N_DOWN + m)
            pe.wait_ge(ps_free, N_DOWN + KT)
            for j in range(NT):
                if j >= 2:
                    pe.wait_ge(out_ready, j - 1)
                for k in range(KT):
                    ins = pe.transpose(ps[2 + 2 * (j % 2) + k // 4][:, (k % 4) * P:(k % 4 + 1) * P],
                                       x1[:, k, j * P:(j + 1) * P], ident[:, :])
                ins.then_inc(y_t, 1)


_INS = ["x", "norm1_g", "w_in", "rwkv_mu", "w0", "w2", "a0", "a2", "g2", "k_k", "k_a", "r_k",
        "lnx_w", "lnx_b", "b_qkv", "attn_sink", "gate_b", "w_proj_a", "w_proj_b", "w_out",
        "norm2_g", "w_up", "conv_w", "conv_b", "w_down", "normf_g"]


def kernel(**inputs):
    import concourse.bacc as bacc
    from concourse.bass_utils import run_bass_kernel_spmd

    nc = bacc.Bacc("TRN2", target_bir_lowering=False, num_devices=1)
    arrays, args = {}, []
    for name in _INS:
        a = np.ascontiguousarray(inputs[name])
        arrays[f"in_{name}"] = a
        args.append(nc.dram_tensor(f"in_{name}", a.shape, mybir.dt.from_np(a.dtype),
                                   kind="ExternalInput").ap())
    args.append(nc.dram_tensor("out", (1, T, D), F32, kind="ExternalOutput").ap())
    build(nc, *args)
    return run_bass_kernel_spmd(nc, [arrays], core_ids=[0]).results[0]["out"]
```

```python
from contextlib import ExitStack, contextmanager

import numpy as np

import concourse.bass as bass
from concourse import mybir

F32 = mybir.dt.float32
F32R = mybir.dt.float32r
F16 = mybir.dt.float16
U32 = mybir.dt.uint32
ALU = mybir.AluOpType
ACT = mybir.ActivationFunctionType
AX = mybir.AxisListType.X

P = 128
T = 512
D = 1024
KT = D // P
NT = T // P
C = 128
HD = 64
PAIRS = 8
DFF = 2816
FT = DFF // P
RW = 3328
QKV = 1536
AC = 64
LEVELS = 7
CHAINED = 16
HALF_EXP = float(-0.5 * np.exp(-0.5))
NEG = -1e30

RAW, HL = 4, 2
N_AUX, N_RKV, N_QKV, N_GATE, N_PROJ, N_OUT, N_UP = 0, 2, 26, 38, 54, 70, 78
N_DOWN = N_UP + 2 * FT
N_END = N_DOWN + 3 * KT
DOWN_K = (8, 8, FT - 16)


PARAMS, N_PAR = {}, 0
for _name, _n in (("g1", 8), ("gn2", 8), ("mu", 26), ("w0", 8), ("a0", 8), ("kk", 8), ("ka", 8),
                  ("rk", 8), ("lw", 8), ("lb", 8), ("bq", 12), ("bg", 16),
                  ("cw0", 2 * FT), ("cw1", 2 * FT), ("cw2", 2 * FT), ("cb", 2 * FT)):
    PARAMS[_name] = (N_PAR, _n)
    N_PAR += _n
PAR_ROWS = (126, 88, 88)


class Chain:

    def __init__(self, eng, sem):
        self.eng, self.sem, self.base, self.k = eng, sem, 0, 0

    def __call__(self, ins):
        self.k += 1
        ins.then_inc(self.sem, 1)
        self.eng.wait_ge(self.sem, self.base + self.k)

    @contextmanager
    def loop(self, count, per):
        start = self.base + self.k
        with self.eng.Fori(0, count) as i:
            self.base, self.k = i * per + start, 0
            yield i
            assert self.k == per, f"the body uses the chain {self.k} times"
        self.base, self.k = start + count * per, 0


def build(nc, x, norm1_g, w_in, rwkv_mu, w0, w2, a0, a2, g2, k_k, k_a, r_k, lnx_w, lnx_b,
          b_qkv, attn_sink, gate_b, w_proj_a, w_proj_b, w_out, norm2_g, w_up, conv_w,
          conv_b, w_down, normf_g, out):
    with ExitStack() as ctx:
        def sb(name, shape, dt=F32):
            return ctx.enter_context(nc.sbuf_tensor(name, shape, dt))

        def sem(name):
            return ctx.enter_context(nc.semaphore(name))

        ident = sb("ident", [P, P])
        ident16 = sb("ident16", [P, P], F16)
        nident16 = sb("nident16", [P, P], F16)
        headones = sb("headones", [P, P])
        headmean = sb("headmean", [P, P])
        ones = sb("ones", [P, P])
        level_mask = sb("level_mask", [P, LEVELS, P], F16)
        causal = sb("causal", [P, 2 * C])
        notstart = sb("notstart", [P, T])
        notfirst = sb("notfirst", [P, AC * 9])
        par = sb("par", [P, N_PAR])
        col = {name: par[:, o:o + n] for name, (o, n) in PARAMS.items()}
        omu = sb("omu", [P, 26])
        whalf = sb("whalf", [P, KT])
        ahalf = sb("ahalf", [P, KT])
        eps_col = sb("eps_col", [P, 2])
        sink = sb("sink", [P, 8])
        lora = sb("lora", [P, D])
        g2s = sb("g2s", [P, D])
        lora_w_in = sb("lora_w_in", [P, T])
        lora_a_in = sb("lora_a_in", [P, T])
        lora_g_in = sb("lora_g_in", [P, T])
        raw = sb("raw", [P, RAW, KT, P])
        whi = sb("whi", [P, HL, KT, P], F32R)
        wlo = sb("wlo", [P, HL, KT, P], F32R)
        stat = sb("stat", [P, 16])
        carrier = sb("carrier", [P, 8])

        arena_bytes = (nc.sbuf_top - nc.sbuf_base - 64) // 32 * 32
        arena = sb("arena", [P, arena_bytes // 4])
        base = nc.lookup_mloc(arena).addr
        K = 1024

        def size(shape, dt):
            return (int(np.prod(shape[1:])) * (2 if dt == F16 else 4) + 31) // 32 * 32

        def at(off, name, shape, dt=F32):
            assert off + size(shape, dt) <= arena_bytes, name
            return nc.alloc_sbuf_tensor_at(name, shape, dt, offset=base + off)

        def taker(off, end):
            place = [off]

            def take(name, shape, dt=F32):
                t = at(place[0], name, shape, dt)
                place[0] += size(shape, dt)
                assert place[0] <= end, name
                return t
            return take

        XHL, ZR, QR, KVR = 0, 32 * K, 80 * K, 96 * K
        WR = KVR + 2 * 2 * (T + AC) * 4
        xh = at(XHL, "xh", [P, KT, T], F32R)
        xl = at(XHL + 16 * K, "xl", [P, KT, T], F32R)
        z = at(ZR, "z", [P, 24, T])
        q = at(QR, "q", [P, KT, T])
        kb = at(KVR, "kb", [P, 2, AC + T])
        vb = at(KVR + 2 * (T + AC) * 4, "vb", [P, 2, AC + T])
        xt = at(ZR, "xt", [P, NT, D])
        junk = at(QR, "junk", [P, D])
        rows = at(QR + 4 * K, "rows", [P, 3, P])
        mixed = at(WR, "mixed", [P, 2, T])
        gst = at(WR + 4 * K, "gst", [P, 2, T])

        take = taker(WR + 8 * K, arena_bytes)
        qc = take("qc", [P, KT, AC])
        kc = take("kc", [P, 2, 2, P])
        vc = take("vc", [P, 2, P])
        vtok = take("vtok", [P, 2, P])
        sc = take("sc", [P, 8, P])
        pt = take("pt", [P, 8, P])
        mx = take("mx", [P, 8])
        nmx = take("nmx", [P, 8])
        es = take("es", [P, 8])
        den = take("den", [P, 8])

        take = taker(KVR, arena_bytes)
        gb = take("gb", [P, NT, 2, 2 * C])
        gk = take("gk", [P, NT, 2, 2 * C])
        ar = take("ar", [P, 2, NT, 2 * C])
        xf = take("xf", [P, NT, 2, C])
        bp = take("bp", [P, 2, T])
        kp = take("kp", [P, 2, T])
        vp = take("vp", [P, NT, 4, HD])
        e = take("e", [P, NT, C + 1])
        vfix = take("vfix", [P, T])
        kqn = take("kqn", [P, T])
        ysb = take("ysb", [P, T])
        ysq = take("ysq", [P, T])
        wcum = take("wcum", [P, T])
        take = taker(XHL, ZR)
        ei = take("ei", [P, T])
        kkn = take("kkn", [P, T])
        kmod = take("kmod", [P, T])
        t0 = take("t0", [P, T])
        t1 = take("t1", [P, T])
        t2 = take("t2", [P, T])
        btok = take("btok", [P, NT, P])
        ktok = take("ktok", [P, NT, P])
        n1 = take("n1", [P, NT, 2, C], F16)
        n2 = take("n2", [P, NT, 2, C], F16)
        xx = take("xx", [P, NT, 2, C], F16)
        yy = take("yy", [P, NT, 2, C], F16)
        v1 = take("v1", [P, NT, 2, C], F16)
        up = take("up", [P, 4, HD])
        zp = take("zp", [P, 4, HD])
        state = take("state", [P, P])
        stm = take("stm", [P, P])
        lorap = take("lorap", [P, P])
        g2p = take("g2p", [P, P])
        em = take("em", [P, 2, NT])
        dtot = take("dtot", [P, 2, NT])

        yah = at(XHL, "yah", [P, KT, T], F32R)
        yal = at(XHL + 16 * K, "yal", [P, KT, T], F32R)
        ybh = at(ZR + 16 * K, "ybh", [P, KT, T], F32R)
        ybl = at(ZR + 32 * K, "ybl", [P, KT, T], F32R)
        mh = at(ZR, "mh", [P, KT, T], F32R)
        ml = at(QR, "ml", [P, KT, T], F32R)
        gl = at(KVR, "gl", [P, 2, 2, T])
        gs = at(KVR + 28 * K + 8 * K, "gs", [P, 2, 2, T])
        ta = at(KVR + 8 * K, "ta", [P, 2, T])
        xblk = at(KVR + 12 * K, "xblk", [P, 2, NT, P])
        hh = at(ZR, "hh", [P, FT, T], F32R)
        hl = at(ZR + 2 * K * FT, "hl", [P, FT, T], F32R)
        X1 = ZR + 4 * K * FT
        x1 = at(X1, "x1", [P, KT, T])
        sq1 = at(X1 + 16 * K, "sq1", [P, 2, T])
        rs1 = at(X1 + 20 * K, "rs1", [P, T])
        xnh = at(XHL, "xnh", [P, KT, T], F32R)
        xnl = at(XHL + 16 * K, "xnl", [P, KT, T], F32R)
        cg = at(X1 + 22 * K, "cg", [P, T])
        cv = at(X1 + 24 * K, "cv", [P, T])
        gf = at(X1 + 26 * K, "gf", [P, D])
        yt = at(ZR, "yt", [P, NT, D])

        gates = nc.dram_tensor("gates_scratch", (16, P, T), F32, kind="Internal").ap()
        ps = [ctx.enter_context(nc.psum_tensor(f"ps{b}", [P, T], F32)) for b in range(8)]

        loaded = [sem(f"loaded{b}") for b in range(RAW)]
        w_hi = sem("w_hi")
        w_lo = sem("w_lo")
        slot_done = sem("slot_done")
        ps_free = sem("ps_free")
        half_read = sem("half_read")
        consts = sem("consts")
        pool_chain = sem("pool_chain")
        act_chain = sem("act_chain")
        dve_chain = sem("dve_chain")
        rows_in = sem("rows_in")
        misc_in = sem("misc_in")
        x_in = [sem(f"x_in{j}") for j in range(NT)]
        par_t = sem("par_t")
        par_ready = sem("par_ready")
        x_sq = sem("x_sq")
        x_scaled = sem("x_scaled")
        x_t = sem("x_t")
        xh_ready = sem("xh_ready")
        xl_ready = sem("xl_ready")
        gst_free = [sem(f"gst_free{b}") for b in range(2)]
        gate_stored = [sem(f"gate_stored{b}") for b in range(2)]
        gate_in = [sem(f"gate_in{b}") for b in range(2)]
        gate_ready = sem("gate_ready")
        win_in = sem("win_in")
        scores_ps = sem("scores_ps")
        vtok_ps = sem("vtok_ps")
        sc_ready = sem("sc_ready")
        exp_done = sem("exp_done")
        probs_ready = sem("probs_ready")
        pt_ps = sem("pt_ps")
        pt_ready = sem("pt_ready")
        o_ps = sem("o_ps")
        o_done = sem("o_done")
        lora_copied = sem("lora_copied")
        g2_copied = sem("g2_copied")
        pair_done = sem("pair_done")
        lora_ps = sem("lora_ps")
        sq_ready = sem("sq_ready")
        ss_ps = sem("ss_ps")
        norm_ready = sem("norm_ready")
        tanh_ready = sem("tanh_ready")
        rel_ready = sem("rel_ready")
        exps_ready = sem("exps_ready")
        ops_ready = sem("ops_ready")
        hats_ready = sem("hats_ready")
        rk_ready = sem("rk_ready")
        g_ps = sem("g_ps")
        g_ready = sem("g_ready")
        tok_ps = sem("tok_ps")
        tok_ready = sem("tok_ready")
        n1_ready = sem("n1_ready")
        n2_ready = sem("n2_ready")
        v_ps = sem("v_ps")
        v_ready = sem("v_ready")
        y_ps = sem("y_ps")
        y_ready = sem("y_ready")
        x_ps = sem("x_ps")
        x_ready = sem("x_ready")
        r_ps = sem("r_ps")
        r_ready = sem("r_ready")
        n_ps = sem("n_ps")
        xf_ready = sem("xf_ready")
        z_ps = sem("z_ps")
        z_ready = sem("z_ready")
        u_ps = sem("u_ps")
        u_ready = sem("u_ready")
        s_ps = sem("s_ps")
        s_ready = sem("s_ready")
        out_ps = sem("out_ps")
        y_copied = sem("y_copied")
        mean_ps = sem("mean_ps")
        yc_ready = sem("yc_ready")
        ysq_ready = sem("ysq_ready")
        var_ps = sem("var_ps")
        std_ready = sem("std_ready")
        bonus_ps = sem("bonus_ps")
        gmul_ps = sem("gmul_ps")
        yh_ready = sem("yh_ready")
        yl_ready = sem("yl_ready")
        mix_ready = sem("mix_ready")
        mh_ready = sem("mh_ready")
        ml_ready = sem("ml_ready")
        xblk_in = [sem(f"xblk_in{b}") for b in range(2)]
        sq1_ready = sem("sq1_ready")
        acc_ready = sem("acc_ready")
        tot_ps = sem("tot_ps")
        rms_ready = sem("rms_ready")
        xs_ready = sem("xs_ready")
        xnh_ready = sem("xnh_ready")
        xnl_ready = sem("xnl_ready")
        conv_ready = sem("conv_ready")
        silu_ready = sem("silu_ready")
        h_ready = sem("h_ready")
        hh_ready = sem("hh_ready")
        hl_ready = sem("hl_ready")
        gf_in = sem("gf_in")
        y_t = sem("y_t")
        y_sq = sem("y_sq")
        y_rms = sem("y_rms")
        out_ready = sem("out_ready")
        stored = sem("stored")

        w_in_v = w_in[0].rearrange("(k p) c -> p k c", p=P)
        w_up_v = w_up[0].rearrange("(k p) c -> p k c", p=P)
        w_down_v = w_down[0].rearrange("(k p) c -> p k c", p=P)
        w_out_v = w_out[0].rearrange("(k p) c -> p k c", p=P)
        w_pa_v = w_proj_a[0].rearrange("(k p) c -> p k c", p=P)
        w_pb_v = w_proj_b[0].rearrange("(h k p) c -> h p k c", h=2, p=HD)
        w_q_v = w_in[0, :, RW:RW + D].rearrange("(k p) (h t c) -> h p k t c", p=P, h=2, c=HD)
        w_k_v = w_in[0, :, RW + D:RW + QKV].rearrange("(k p) (b h t c) -> b h p k t c", p=P, b=2,
                                                      h=2, c=HD)
        x_v = x[0].rearrange("(j p) c -> p j c", p=P)
        out_v = out[0].rearrange("(j p) c -> p j c", p=P)

        def flat(ap):
            return ap.rearrange("p a b -> p (a b)")

        def load_values(n, b):
            return (n - b) * 8 + 32

        block = ctx.enter_context(nc.Block())

        @block.sync
        def _(sp):
            def load(n, b, pieces, reuse=True):
                if reuse:
                    sp.wait_ge(w_lo, n - 3)
                for dst, src in pieces:
                    sp.dma_start(dst, src).then_inc(loaded[b], 16)

            def by_k(b, src, kn=KT):
                h = kn // 2
                return [(raw[:, b, 0:h, :], src[:, 0:h]), (raw[:, b, h:kn, :], src[:, h:kn])]

            def by_col(b, lo, hi):
                return [(raw[:, b, :, 0:HD], lo), (raw[:, b, :, HD:P], hi)]

            for j in range(NT):
                sp.dma_start(xt[:, j, :], x_v[:, j, :]).then_inc(x_in[j], 16)
            for n in range(2):
                load(n, n, by_k(n, w_in_v[:, :, 3 * D + n * P:3 * D + (n + 1) * P]), reuse=False)
            for n in range(2, 6):
                load(n, n % RAW, by_k(n % RAW, w_in_v[:, :, (n - 2) * P:(n - 1) * P]), reuse=n >= 4)
            with sp.Fori(0, 5) as i:
                for u in range(4):
                    b = (2 + u) % RAW
                    load(i * 4 + 6 + u, b, by_k(b, w_in_v[:, :, bass.ts(i * 4 + 4 + u, P)]))
            with sp.Fori(0, 2) as i:
                for u in range(4):
                    b = (2 + u) % RAW
                    t = i * 4 + u
                    load(i * 4 + N_QKV + u, b, by_col(b, w_q_v[0][:, :, t, :], w_q_v[1][:, :, t, :]))
            for u in range(4):
                b = (2 + u) % RAW
                kv, g = divmod(u, 2)
                load(N_QKV + 8 + u, b, by_col(b, w_k_v[kv][0][:, :, g, :], w_k_v[kv][1][:, :, g, :]))
            with sp.Fori(0, 4) as i:
                for u in range(4):
                    b = (2 + u) % RAW
                    load(i * 4 + N_GATE + u, b,
                         by_k(b, w_in_v[:, :, RW + QKV:][:, :, bass.ts(i * 4 + u, P)]))
            with sp.Fori(0, 4) as i:
                for u in range(4):
                    b = (2 + u) % RAW
                    cols = bass.ts(i * 2 + u // 2, P)
                    if u % 2 == 0:
                        pieces = by_k(b, w_pa_v[:, :, cols])
                    else:
                        pieces = [(raw[0:HD, b], w_pb_v[0][:, :, cols]),
                                  (raw[HD:P, b], w_pb_v[1][:, :, cols])]
                    load(i * 4 + N_PROJ + u, b, pieces)
            with sp.Fori(0, 2) as i:
                for u in range(4):
                    b = (2 + u) % RAW
                    load(i * 4 + N_OUT + u, b, by_k(b, w_out_v[:, :, bass.ts(i * 4 + u, P)]))
            with sp.Fori(0, FT // 2) as i:
                for u in range(4):
                    b = (2 + u) % RAW
                    src = w_up_v[:, :, (u % 2) * DFF:][:, :, bass.ts(i * 2 + u // 2, P)]
                    load(i * 4 + N_UP + u, b, by_k(b, src))
            with sp.Fori(0, 2) as i:
                for u in range(12):
                    b = (2 + u) % RAW
                    m, s = divmod(u, 3)
                    src = w_down_v[:, 8 * s:8 * s + DOWN_K[s], bass.ts(i * 4 + m, P)]
                    load(i * 12 + N_DOWN + u, b, by_k(b, src, DOWN_K[s]))
            for n in range(N_END, N_END + 2):
                load(n, n % RAW, by_k(n % RAW, w_down_v[:, 0:2, 0:P], 2))
            for j in range(NT):
                sp.wait_ge(out_ready, j + 1)
                sp.dma_start(out_v[:, j, :], yt[:, j, :]).then_inc(stored, 16)
            sp.wait_ge(stored, 16 * NT)

        @block.gpsimd
        def _(pool):
            chain = Chain(pool, pool_chain)
            def diagonal(t, value):
                chain(pool.memset(t[:, :], 0.0))
                chain(pool.affine_select(out=t[:, :], in_=t[:, :], compare_op=ALU.not_equal,
                                         fill=value, base=0, pattern=[[-1, P]],
                                         channel_multiplier=1))

            diagonal(ident, 1.0)
            pool.wait_ge(pool_chain, chain.k)
            pool.memset(eps_col[:, 0:1], 1e-6).then_inc(consts, 1)
            diagonal(ident16, 1.0)
            diagonal(nident16, -1.0)
            chain(pool.memset(eps_col[:, 1:2], 64e-5))
            chain(pool.memset(ones[:, :], 1.0))
            for t, value in ((headones, 1.0), (headmean, 1.0 / HD)):
                chain(pool.memset(t[:, :], 0.0))
                for h in range(2):
                    chain(pool.memset(t[h * HD:(h + 1) * HD, h * HD:(h + 1) * HD], value))
            chain(pool.memset(causal[:, :], 1.0))
            for o, op in ((0, ALU.is_gt), (C, ALU.is_ge)):
                chain(pool.affine_select(out=causal[:, o:o + C], in_=causal[:, o:o + C],
                                         compare_op=op, fill=0.0, base=0, pattern=[[1, C]],
                                         channel_multiplier=-1))
            chain(pool.memset(level_mask[:, :, :], 0.0))
            for lv in range(LEVELS):
                m = 1 << lv
                view = level_mask[:, lv, :].rearrange("p (a b c) -> p a b c", b=2, c=m)[:, :, 0, :]
                chain(pool.memset(view, 1.0))
                n = P // (2 * m)
                chain(pool.affine_select(out=view, in_=view, compare_op=ALU.is_ge, fill=0.0,
                                         base=-m, pattern=[[-2 * m, n], [0, m]],
                                         channel_multiplier=1))
                chain(pool.affine_select(out=view, in_=view, compare_op=ALU.is_ge, fill=0.0,
                                         base=2 * m - 1, pattern=[[2 * m, n], [0, m]],
                                         channel_multiplier=-1))
            chain(pool.memset(notstart[:, :], 1.0))
            chain(pool.memset(notstart[:, :].rearrange("p (j t) -> p j t", t=C)[:, :, 0:1], 0.0))
            chain(pool.memset(notfirst[:, :], 0.0))
            chain(pool.memset(notfirst[:, 0:AC], NEG))
            chain(pool.memset(lora_w_in[HD:P, :], 0.0))
            chain(pool.memset(lora_a_in[0:HD, :], 0.0))
            chain(pool.memset(kb[:, :, 0:AC], 0.0))
            chain(pool.memset(vb[:, :, 0:AC], 0.0))
            chain(pool.memset(kc[0:HD, :, 1, :], 0.0))
            pool.memset(kc[HD:P, :, 0, :], 0.0).then_inc(consts, 1)

            pool.dma_start(lora[0:HD, :], w2[0]).then_inc(misc_in, 16)
            pool.dma_start(lora[HD:P, :], a2[0]).then_inc(misc_in, 16)
            pool.dma_start(g2s[:, :], g2[0]).then_inc(misc_in, 16)
            sv = attn_sink[0].rearrange("(half g ii b) -> b g ii half", half=2, g=2, ii=2)
            for b in range(2):
                for u in range(4):
                    g, ii = divmod(u, 2)
                    src = sv[b][g][ii:ii + 1].to_broadcast([HD, 2])
                    pool.dma_start(sink[b * HD:(b + 1) * HD, 2 * u:2 * u + 2], src,
                                   allow_slow_non_contiguous=True).then_inc(misc_in, 16)

            for u in range(2):
                pool.sem_inc(gst_free[u], 1)
            with pool.Fori(0, 8) as i:
                for u in range(2):
                    pool.wait_ge(ps_free, i * 2 + N_GATE + u + 1)
                    pool.dma_start(gates[i * 2 + u], gst[:, u, :]).then_inc(gate_stored[u], 16)
                    pool.wait_ge(gate_stored[u], i * 16 + 16)
                    pool.sem_inc(gst_free[u], 1)

            pool.wait_ge(o_done, 8)
            chain(pool.memset(gb[:, :, :, :], 0.0))
            chain(pool.memset(gk[:, :, :, :], 0.0))
            chain(pool.memset(bp[HD:P, 0, :], 0.0))
            chain(pool.memset(bp[0:HD, 1, :], 0.0))
            chain(pool.memset(kp[HD:P, 0, :], 0.0))
            chain(pool.memset(kp[0:HD, 1, :], 0.0))
            chain(pool.memset(vp[:, :, 1:3, :], 0.0))
            chain(pool.memset(up[:, 1:3, :], 0.0))
            pool.memset(zp[:, 1:3, :], 0.0).then_inc(consts, 1)
            pool.wait_ge(misc_in, 16 * 11)

            def copies(p):
                pool.tensor_copy(lorap[:, :], lora[:, bass.ts(p, P)]).then_inc(lora_copied, 1)

            def gate_copy(p):
                pool.tensor_copy(g2p[:, :], g2s[:, bass.ts(p, P)]).then_inc(g2_copied, 1)

            def remainder(p):
                pool.wait_ge(n1_ready, p + 1)
                pool.tensor_tensor(n2[:, :, :, :], gb[:, :, :, 0:C], n1[:, :, :, :], ALU.subtract)\
                    .then_inc(n2_ready, 1)

            copies(0)
            gate_copy(0)
            with pool.Fori(0, PAIRS - 1) as i:
                remainder(i)
                pool.wait_ge(lora_ps, i + 1)
                copies(i + 1)
                pool.wait_ge(gmul_ps, i + 1)
                gate_copy(i + 1)
            remainder(PAIRS - 1)

            pool.wait_ge(pair_done, PAIRS)

            def gates_back(m, b):
                pool.dma_start(gl[:, b, 0, :], gates[m]).then_inc(gate_in[b], 16)
                pool.dma_start(gl[:, b, 1, :], gates[m + 8]).then_inc(gate_in[b], 16)

            for m in range(2):
                gates_back(m, m)
            with pool.Fori(0, 3) as i:
                for u in range(2):
                    pool.wait_ge(mix_ready, i * 2 + u + 1)
                    gates_back(i * 2 + 2 + u, u)
            for m in range(2):
                pool.dma_start(xblk[:, m], x_v[:, :, bass.ts(m, P)]).then_inc(xblk_in[m], 16)
            with pool.Fori(0, 3) as i:
                for u in range(2):
                    pool.wait_ge(slot_done, i * 2 + N_OUT + u + 1)
                    pool.dma_start(xblk[:, u], x_v[:, :, bass.ts(i * 2 + 2 + u, P)])\
                        .then_inc(xblk_in[u], 16)
            pool.dma_start(gf[:, :], normf_g.rearrange("(o n) -> o n", o=1).to_broadcast([P, D]))\
                .then_inc(gf_in, 16)
            pool.wait_ge(gf_in, 16)

        @block.scalar
        def _(act):
            chain = Chain(act, act_chain)

            def split(n, b, hb, first=False):
                act.wait_ge(loaded[b], load_values(n, b))
                if not first:
                    act.wait_ge(slot_done, n - 1)
                act.activation(flat(whi[:, hb]), flat(raw[:, b]), ACT.Copy).then_inc(w_hi, 1)

            for name, src in (("g1", norm1_g[0]), ("gn2", norm2_g[0]), ("mu", rwkv_mu[0]),
                              ("w0", w0[0]), ("a0", a0[0]), ("kk", k_k[0]), ("ka", k_a[0]),
                              ("rk", r_k[0].rearrange("h d -> (h d)")), ("lw", lnx_w[0]),
                              ("lb", lnx_b[0]), ("bg", gate_b[0])):
                o, n = PARAMS[name]
                act.dma_start(rows[o:o + n, 0, :], src.rearrange("(n p) -> n p", p=P))\
                    .then_inc(rows_in, 16)
            o = PARAMS["bq"][0]
            bq, bk = b_qkv[0][0:D], b_qkv[0][D:QKV]
            bqv = bq.rearrange("(h t d) -> h t d", h=2, d=HD)
            bkv = bk.rearrange("(b h t d) -> b h t d", b=2, h=2, d=HD)
            for h in range(2):
                dst = rows[:, 0, h * HD:(h + 1) * HD]
                act.dma_start(dst[o:o + 8], bqv[h]).then_inc(rows_in, 16)
                act.dma_start(dst[o + 8:o + 10], bkv[0][h]).then_inc(rows_in, 16)
                act.dma_start(dst[o + 10:o + 12], bkv[1][h]).then_inc(rows_in, 16)
            for i in range(3):
                src = conv_w[0][i].rearrange("(n p) -> n p", p=P)
                dst = rows[(i % 2) * 44:(i % 2) * 44 + 44, 1 + i // 2, :]
                act.dma_start(dst, src).then_inc(rows_in, 16)
            act.dma_start(rows[44:88, 2, :], conv_b[0].rearrange("(n p) -> n p", p=P))\
                .then_inc(rows_in, 16)
            act.wait_ge(consts, 1)
            for j in range(NT):
                act.wait_ge(x_in[j], 16)
                chain(act.activation(junk[:, :], xt[:, j, :], ACT.Square,
                                     accum_out=stat[:, j:j + 1]))
            act.activation(stat[:, 4:8], stat[:, 0:4], ACT.Sqrt, scale=1.0 / D,
                           bias=eps_col[:, 0:1]).then_inc(x_sq, 1)
            act.wait_ge(par_t, 1)
            act.activation(par[:, :], ps[7][:, 0:N_PAR], ACT.Copy).then_inc(par_ready, 1)
            act.wait_ge(par_ready, 1)
            split(0, 0, 0, first=True)
            split(1, 1, 1, first=True)
            for k in range(KT):
                act.wait_ge(x_t, k + 1)
                act.activation(xh[:, k, :], ps[2 + k % 4][:, :], ACT.Copy,
                               scale=col["g1"][:, k:k + 1]).then_inc(xh_ready, 1)

            def keep(dst, n, bank, mt):
                act.wait_ge(slot_done, n + 1)
                act.activation(dst, ps[bank][:, :], ACT.Copy, scale=omu[:, mt:mt + 1] if
                               isinstance(mt, int) else omu[:, bass.ds(mt, 1)]).then_inc(half_read, 1)

            act.wait_ge(consts, 2)
            act.wait_ge(par_ready, 2)
            split(2, 2, 0)
            keep(mixed[:, 0, :], 0, 0, 24)
            split(3, 3, 1)
            keep(mixed[:, 1, :], 1, 1, 25)
            act.wait_ge(ps_free, 2)
            act.activation(lora_w_in[0:HD, :], mixed[0:HD, 0, :], ACT.Tanh)
            act.activation(lora_a_in[HD:P, :], mixed[HD:P, 0, :], ACT.Copy)
            act.activation(lora_g_in[:, :], mixed[:, 1, :], ACT.Sigmoid)
            with act.Fori(0, 6) as i:
                for u in range(4):
                    n, m = i * 4 + N_RKV + u, i * 4 + u
                    split(n + 2, u % RAW, u % 2)
                    keep(z[:, bass.ds(m, 1), :], n, u % 2, m)

            def biased(dst, n, bank, func, bias):
                act.wait_ge(slot_done, n + 1)
                act.activation(dst, ps[bank][:, :], func, bias=bias).then_inc(ps_free, 1)

            oq = PARAMS["bq"][0]
            act.wait_ge(ps_free, N_QKV)
            with act.Fori(0, 2) as i:
                for u in range(4):
                    n, m = i * 4 + N_QKV + u, i * 4 + u
                    split(n + 2, u % RAW, u % 2)
                    biased(q[:, bass.ds(m, 1), :], n, u % 2, ACT.Identity,
                           par[:, bass.ds(m + oq, 1)])
            for u in range(4):
                n = N_QKV + 8 + u
                split(n + 2, u % RAW, u % 2)
                biased((kb, vb)[u // 2][:, u % 2, AC:], n, u % 2, ACT.Identity,
                       par[:, oq + 8 + u:oq + 9 + u])
            og = PARAMS["bg"][0]

            act.wait_ge(ps_free, N_GATE)
            with act.Fori(0, 4) as i:
                for w in range(2):
                    c = i * 2 + w
                    win = bass.ds(c * AC, P)

                    def gate_tile(u):
                        n = i * 4 + N_GATE + 2 * w + u
                        split(n + 2, 2 * w + u, u)
                        act.wait_ge(gst_free[u], c + 1)
                        biased(gst[:, u, :], n, u, ACT.Identity,
                               par[:, bass.ds(i * 4 + og + 2 * w + u, 1)])

                    act.activation(qc[:, :, :], q[:, :, bass.ds(c * AC, AC)], ACT.Copy,
                                   scale=HD ** -0.5)
                    act.activation(kc[0:HD, :, 0, :], kb[0:HD, :, win], ACT.Copy)
                    act.activation(kc[HD:P, :, 1, :], kb[HD:P, :, win], ACT.Copy)
                    act.activation(vc[:, :, :], vb[:, :, win], ACT.Copy).then_inc(win_in, 1)
                    act.wait_ge(vtok_ps, c + 1)
                    act.activation(flat(vtok), ps[4][:, 0:2 * P], ACT.Copy)
                    act.wait_ge(sc_ready, c + 1)
                    for u in range(8):
                        act.activation(sc[:, u, :], sc[:, u, :], ACT.Exp, bias=nmx[:, u:u + 1],
                                       accum_out=den[:, u:u + 1])
                    act.activation(es[:, :], es[:, :], ACT.Exp).then_inc(exp_done, 1)
                    gate_tile(0)
                    act.wait_ge(pt_ps, c + 1)
                    for g in range(2):
                        act.activation(flat(pt[:, 4 * g:4 * g + 4, :]), ps[5 + g][:, :], ACT.Copy)\
                            .then_inc(pt_ready, 1)
                    gate_tile(1)

            act.wait_ge(consts, 3)

            def prepare(n, par2):
                act.activation(vfix[:, :], z[:, bass.ds(n + 16, 1), :], ACT.Copy)
                act.activation(t2[:, :], z[:, bass.ds(n + 8, 1), :], ACT.Square,
                               scale=pcol("kk", n)).then_inc(sq_ready, 1)
                act.wait_ge(ss_ps, n + 1)
                act.activation(kqn[:, :], ps[2][:, :], ACT.Sqrt).then_inc(norm_ready, 1)
                act.wait_ge(lora_ps, n + 1)
                act.activation(t0[:, :], ps[0][:, :], ACT.Tanh, scale=0.5,
                               bias=whalf[:, bass.ds(n, 1)])
                act.activation(t1[:, :], ps[1][:, :], ACT.Tanh, scale=0.5,
                               bias=ahalf[:, bass.ds(n, 1)]).then_inc(tanh_ready, 1)
                act.wait_ge(rel_ready, n + 1)
                cum = wcum[:, :].rearrange("p (j t) -> p j t", t=C)
                act.activation(e[:, :, 1:C + 1], t0[:, :].rearrange("p (j t) -> p j t", t=C), ACT.Exp)
                act.activation(e[:, :, 0:1], cum[:, :, C // 2 - 1:C // 2], ACT.Exp, scale=-1.0)
                act.activation(em[:, par2, :].unsqueeze(2), cum[:, :, C // 2 - 1:C // 2], ACT.Exp)
                act.activation(dtot[:, par2, :].unsqueeze(2), cum[:, :, C - 1:C], ACT.Exp)
                act.activation(ei[:, :], t0[:, :], ACT.Exp, scale=-1.0).then_inc(exps_ready, 1)

            def norm_head(d):
                act.wait_ge(out_ps, d + 1)
                act.activation(ysb[:, :], ps[6][:, :], ACT.Copy).then_inc(y_copied, 1)

            def norm_square(d):
                act.wait_ge(yc_ready, d + 1)
                act.activation(ysq[:, :], ysb[:, :], ACT.Square).then_inc(ysq_ready, 1)
                act.wait_ge(var_ps, d + 1)
                act.activation(ysq[:, :], ps[4][:, :], ACT.Sqrt, bias=eps_col[:, 1:2])\
                    .then_inc(std_ready, 1)

            def copies(n, d):
                if d is not None:
                    norm_head(d)
                act.wait_ge(g_ready, n * 8 + 4)
                act.activation(n1[:, :, :, :], gb[:, :, :, 0:C], ACT.Copy).then_inc(n1_ready, 1)
                if d is not None:
                    norm_square(d)
                act.wait_ge(tok_ps, n + 1)
                act.activation(flat(btok), ps[0][:, :], ACT.Copy)
                act.activation(flat(ktok), ps[1][:, :], ACT.Copy)
                act.activation(vp[:, :, 0:4:3, :],
                               ps[2][:, :].rearrange("p (j h v) -> p j h v", h=2, v=HD), ACT.Copy)\
                    .then_inc(tok_ready, 1)

            def invert(n):
                for lv in range(LEVELS):
                    for g in range(2):
                        act.wait_ge(x_ps, n * (2 * LEVELS) + (2 * lv + g + 1))
                        act.activation(xx[:, 2 * g:2 * g + 2].rearrange("p j h t -> p (j h t)"),
                                       ps[2 * g][:, :], ACT.Copy).then_inc(x_ready, 1)
                for g in range(2):
                    act.wait_ge(r_ps, n * 2 + g + 1)
                    act.activation(v1[:, 2 * g:2 * g + 2].rearrange("p j h t -> p (j h t)"),
                                   ps[2 * g][:, :], ACT.Copy).then_inc(r_ready, 1)

            def pcol(name, n):
                return par[:, bass.ds(n + PARAMS[name][0], 1)]

            def step(n, par2):
                prepare(n, par2)
                copies(n, n - 1)
                invert(n)

            prepare(0, 0)
            copies(0, None)
            invert(0)
            with act.Fori(0, 3) as i:
                step(i * 2 + 1, 1)
                step(i * 2 + 2, 0)
            step(PAIRS - 1, 1)
            norm_head(PAIRS - 1)
            norm_square(PAIRS - 1)

            act.wait_ge(pair_done, PAIRS)
            for dst, src in ((yah, z), (ybh, q)):
                for i in range(4):
                    act.activation(flat(dst[:, 2 * i:2 * i + 2]), flat(src[:, 2 * i:2 * i + 2]),
                                   ACT.Copy).then_inc(yh_ready, 1)
            with act.Fori(0, 4) as i:
                for u in range(4):
                    n, m = i * 4 + N_PROJ + u, i * 2 + u // 2
                    if u % 2 == 0:
                        act.wait_ge(gate_in[u // 2], i * 32 + 32)
                        act.activation(flat(gs[:, u // 2]), flat(gl[:, u // 2]), ACT.Sigmoid)\
                            .then_inc(gate_ready, 1)
                    split(n + 2, u % RAW, u % 2)
                    if u % 2:
                        act.wait_ge(mix_ready, m + 1)
                        act.activation(mh[:, bass.ds(m, 1), :], ta[:, u // 2, :], ACT.Copy)\
                            .then_inc(mh_ready, 1)
            with act.Fori(0, 2) as i:
                for u in range(4):
                    n, m = i * 4 + N_OUT + u, i * 4 + u
                    split(n + 2, u % RAW, u % 2)
                    act.wait_ge(slot_done, n + 1)
                    act.activation(x1[:, bass.ds(m, 1), :], ps[u % 2][:, :], ACT.Copy)
                    act.wait_ge(acc_ready, m + 1)
                    act.activation(sq1[:, 0, :], ps[u % 2][:, :], ACT.Square).then_inc(ps_free, 1)
            act.wait_ge(tot_ps, 1)
            act.activation(rs1[:, :], ps[2][:, :], ACT.Sqrt, scale=1.0 / D, bias=eps_col[:, 0:1])\
                .then_inc(rms_ready, 1)
            for k in range(KT):
                act.wait_ge(xs_ready, k + 1)
                act.activation(xnh[:, k, :], sq1[:, k % 2, :], ACT.Copy,
                               scale=col["gn2"][:, k:k + 1]).then_inc(xnh_ready, 1)
            with act.Fori(0, FT // 2) as i:
                for u in range(4):
                    n, j = i * 4 + N_UP + u, i * 2 + u // 2
                    split(n + 2, u % RAW, u % 2)
                    act.wait_ge(slot_done, n + 1)
                    c, half = (cg, cv)[u % 2], (u % 2) * FT
                    act.activation(c[:, :], ps[u % 2][:, :], ACT.Identity,
                                   scale=par[:, bass.ds(j + (PARAMS["cw2"][0] + half), 1)],
                                   bias=par[:, bass.ds(j + (PARAMS["cb"][0] + half), 1)])\
                        .then_inc(half_read, 1)
                    if u % 2 == 0:
                        act.wait_ge(ps_free, n + 1)
                        act.activation(cg[:, :], cg[:, :], ACT.Silu).then_inc(silu_ready, 1)
                    else:
                        act.wait_ge(h_ready, j + 1)
                        act.activation(hh[:, bass.ds(j, 1), :], cv[:, :], ACT.Copy)\
                            .then_inc(hh_ready, 1)
            with act.Fori(0, 2) as i:
                for u in range(12):
                    split(i * 12 + N_DOWN + u + 2, u % RAW, u % 2)
            for j in range(NT):
                act.wait_ge(y_t, j + 1)
                for h in range(2):
                    chain(act.activation(sq1[:, 0, :], ps[2 + 2 * (j % 2) + h][:, :], ACT.Square,
                                         accum_out=stat[:, 2 * j + h:2 * j + h + 1]))
                act.activation(stat[:, 8 + j:9 + j], stat[:, 2 * j:2 * j + 1], ACT.Identity,
                               bias=stat[:, 2 * j + 1:2 * j + 2]).then_inc(y_sq, 1)
                act.wait_ge(y_sq, 2 * j + 1)
                act.activation(stat[:, 8 + j:9 + j], stat[:, 8 + j:9 + j], ACT.Sqrt, scale=1.0 / D,
                               bias=eps_col[:, 0:1]).then_inc(y_sq, 1)

        @block.vector
        def _(dve):
            chain = Chain(dve, dve_chain)

            def split(n, b, hb):
                dve.wait_ge(w_hi, n + 1)
                dve.tensor_tensor(flat(wlo[:, hb]), flat(raw[:, b]), flat(whi[:, hb]).bitcast(F32),
                                  ALU.subtract).then_inc(w_lo, 1)

            def lo_part(dst, src, hi, s, k):
                dve.tensor_tensor(dst, src, hi.bitcast(F32), ALU.subtract).then_inc(s, k)

            dve.wait_ge(x_sq, 1)
            chain(dve.reciprocal(stat[:, 8:12], stat[:, 4:8]))
            for j in range(NT):
                dve.tensor_scalar(xt[:, j, :], xt[:, j, :], stat[:, 8 + j:9 + j], None, ALU.mult)\
                    .then_inc(x_scaled, 1)
            dve.wait_ge(par_ready, 1)
            dve.tensor_scalar(whalf[:, :], col["w0"], 0.5, None, ALU.mult)
            dve.tensor_scalar(ahalf[:, :], col["a0"], 0.5, None, ALU.mult)
            dve.tensor_scalar(omu[:, :], col["mu"], -1.0, 1.0, ALU.mult, ALU.add)\
                .then_inc(par_ready, 1)
            split(0, 0, 0)
            split(1, 1, 1)
            for k in range(KT):
                dve.wait_ge(xh_ready, k + 1)
                dve.scalar_tensor_tensor(xl[:, k, :], ps[2 + k % 4][:, :], col["g1"][:, k:k + 1],
                                         xh[:, k, :].bitcast(F32), ALU.mult, ALU.subtract)\
                    .then_inc(xl_ready, 1)

            om = PARAMS["mu"][0]

            def shift(dst, n, bank, mt):
                dve.wait_ge(half_read, n + 1)
                dve.scalar_tensor_tensor(dst[:, 1:T], ps[bank][:, 0:T - 1],
                                         par[:, bass.ds(mt + om, 1)], dst[:, 1:T], ALU.mult,
                                         ALU.add).then_inc(ps_free, 1)

            split(2, 2, 0)
            shift(mixed[:, 0, :], 0, 0, 24)
            split(3, 3, 1)
            shift(mixed[:, 1, :], 1, 1, 25)
            with dve.Fori(0, 6) as i:
                for u in range(4):
                    n, m = i * 4 + N_RKV + u, i * 4 + u
                    split(n + 2, u % RAW, u % 2)
                    shift(z[:, bass.ds(m, 1), :].rearrange("p a t -> p (a t)"), n, u % 2, m)
            with dve.Fori(0, 3) as i:
                for u in range(4):
                    split(i * 4 + N_QKV + u + 2, u % RAW, u % 2)

            dve.wait_ge(misc_in, 16 * 11)
            with chain.loop(4, 10) as i:
                for w in range(2):
                    c = i * 2 + w
                    n = i * 4 + N_GATE + 2 * w
                    mask = notfirst[:, bass.ds(c * AC, P)].unsqueeze(1).to_broadcast([P, 4, P])
                    dve.wait_ge(scores_ps, c + 1)
                    for g in range(2):
                        last = dve.tensor_tensor(sc[:, 4 * g:4 * g + 4, :],
                                                 ps[2 + g][:, :].rearrange("p (u k) -> p u k", k=P),
                                                 mask, ALU.add)
                    chain(last)
                    chain(dve.tensor_reduce(mx[:, :], sc[:, :, :], AX, ALU.max))
                    chain(dve.tensor_tensor(mx[:, :], mx[:, :], sink[:, :], ALU.max))
                    dve.tensor_scalar(nmx[:, :], mx[:, :], -1.0, None, ALU.mult)
                    dve.tensor_tensor(es[:, :], sink[:, :], mx[:, :], ALU.subtract)\
                        .then_inc(sc_ready, 1)
                    dve.wait_ge(exp_done, c + 1)
                    chain(dve.tensor_tensor(den[:, :], den[:, :], es[:, :], ALU.add))
                    chain(dve.reciprocal(den[:, :], den[:, :]))
                    dve.tensor_tensor(sc[:, :, :], sc[:, :, :],
                                      den[:, :].unsqueeze(2).to_broadcast([P, 8, P]), ALU.mult)\
                        .then_inc(probs_ready, 1)
                    split(n + 2, 2 * w, 0)
                    dve.wait_ge(o_ps, c + 1)
                    dve.tensor_copy(q[:, :, bass.ds(c * AC, AC)],
                                    ps[7][:, :].rearrange("p (t s) -> p t s", s=AC))\
                        .then_inc(o_done, 1)
                    split(n + 3, 2 * w + 1, 1)

            dve.wait_ge(consts, 3)

            def pcol(name, n):
                return par[:, bass.ds(n + PARAMS[name][0], 1)]

            def tile(n):
                return z[:, bass.ds(n, 1), :].rearrange("p a t -> p (a t)")

            def chunks(t):
                return t.rearrange("p (j t) -> p j t", t=C)

            def prepare(n, par2):
                r_p, k_p = tile(n), tile(n + 8)

                def norms():
                    dve.wait_ge(norm_ready, n + 1)
                    chain(dve.tensor_scalar(kqn[:, :], kqn[:, :], 1e-12, None, ALU.max))
                    chain(dve.reciprocal(kqn[:, :], kqn[:, :]))

                def decays():
                    dve.wait_ge(tanh_ready, n + 1)
                    chain(dve.tensor_scalar(t0[:, :], t0[:, :], 1.0, HALF_EXP, ALU.add, ALU.mult))
                    chain(dve.tensor_tensor_scan(wcum[:, :], notstart[:, :], t0[:, :], 0.0,
                                                 ALU.mult, ALU.add))

                def relative():
                    dve.tensor_tensor(chunks(t0[:, :]), chunks(wcum[:, :]),
                                      chunks(wcum[:, :])[:, :, C // 2 - 1:C // 2].to_broadcast(
                                          [P, NT, C]), ALU.subtract).then_inc(rel_ready, 1)

                def rates():
                    dve.scalar_tensor_tensor(kkn[:, :], k_p, pcol("kk", n), kqn[:, :], ALU.mult,
                                             ALU.mult)
                    chain(dve.tensor_scalar(t1[:, :], t1[:, :], 0.5, 0.5, ALU.mult, ALU.add))

                def modified():
                    chain(dve.tensor_scalar(t2[:, :], t1[:, :], 1.0, pcol("ka", n), ALU.subtract,
                                            ALU.mult))
                    dve.scalar_tensor_tensor(kmod[:, :], t2[:, :], 1.0, k_p, ALU.add, ALU.mult)

                def removed():
                    chain(dve.tensor_tensor(t1[:, :], kkn[:, :], t1[:, :], ALU.mult))

                def bonus():
                    dve.scalar_tensor_tensor(k_p, r_p, pcol("rk", n), kmod[:, :], ALU.mult,
                                             ALU.mult).then_inc(rk_ready, 1)

                def a_tilde():
                    dve.wait_ge(exps_ready, n + 1)
                    dve.scalar_tensor_tensor(ar[:, par2, :, 0:C], chunks(kkn[:, :]), -1.0,
                                             e[:, :, 0:C], ALU.mult, ALU.mult)

                def r_tilde():
                    dve.tensor_tensor(ar[:, par2, :, C:2 * C], chunks(r_p), e[:, :, 1:C + 1],
                                      ALU.mult)

                def padded(dst, src, h, last=False):
                    def piece():
                        hs = slice(h * HD, (h + 1) * HD)
                        ins = dve.tensor_tensor(dst[hs, h, :], src[hs, :], ei[hs, :], ALU.mult)
                        if last:
                            ins.then_inc(ops_ready, 1)
                    return piece

                def to_end():
                    chain(dve.tensor_tensor(chunks(t0[:, :]), chunks(ei[:, :]),
                                            e[:, :, C:C + 1].to_broadcast([P, NT, C]), ALU.mult))

                def hats():
                    dve.tensor_tensor(t1[:, :], t1[:, :], t0[:, :], ALU.mult)
                    dve.tensor_tensor(t0[:, :], kmod[:, :], t0[:, :], ALU.mult)\
                        .then_inc(hats_ready, 1)

                return [norms, decays, relative, rates, modified, removed, bonus, a_tilde, r_tilde,
                        padded(bp, t1, 0), padded(bp, t1, 1), padded(kp, kmod, 0),
                        padded(kp, kmod, 1, last=True), to_end, hats]

            def masked(n, f):
                dst = (gb, gk)[f // 4][:, f % 4]
                dve.wait_ge(g_ps, n * 8 + f + 1)
                dve.memset(carrier[:, f:f + 1], 0.0)
                dve.copy_predicated(dst, causal[:, :].bitcast(U32).unsqueeze(1)
                                    .to_broadcast([P, 2, 2 * C]),
                                    ps[f % 4][:, :].rearrange("p (h t) -> p h t", h=2))\
                    .then_inc(g_ready, 1)

            def centre(d):
                dve.wait_ge(mean_ps, d + 1)
                dve.tensor_tensor(ysb[:, :], ysb[:, :], ps[4][:, :], ALU.subtract)\
                    .then_inc(yc_ready, 1)

            def add_bonus(d):
                dve.wait_ge(bonus_ps, d + 1)
                chain(dve.tensor_tensor(tile(d + 8), tile(d + 16), ps[5][:, :], ALU.mult))

            def finish(d):
                dve.wait_ge(std_ready, d + 1)
                chain(dve.reciprocal(ysq[:, :], ysq[:, :]))
                chain(dve.tensor_tensor(ysb[:, :], ysb[:, :], ysq[:, :], ALU.mult))
                chain(dve.tensor_scalar(ysb[:, :], ysb[:, :], pcol("lw", d), pcol("lb", d), ALU.mult,
                                        ALU.add))
                chain(dve.tensor_tensor(ysb[:, :], ysb[:, :], tile(d + 8), ALU.add))
                dve.wait_ge(gmul_ps, d + 1)
                dve.tensor_tensor(tile(d), ysb[:, :], ps[7][:, :], ALU.mult).then_inc(pair_done, 1)

            def invert(n, d):
                for lv in range(LEVELS):
                    for g in range(2):
                        dve.wait_ge(v_ps, n * (2 * LEVELS) + (2 * lv + g + 1))
                        mask = level_mask[:, lv, :].unsqueeze(1).to_broadcast([P, 4, C])
                        dve.tensor_tensor(v1[:, 2 * g:2 * g + 2].rearrange("p j h t -> p (j h) t"),
                                          ps[2 * g][:, :].rearrange("p (u t) -> p u t", t=C),
                                          mask, ALU.mult).then_inc(v_ready, 1)
                    for g in range(2):
                        yg = yy[:, 2 * g:2 * g + 2].rearrange("p j h t -> p (j h) t")
                        dve.wait_ge(y_ps, n * (2 * LEVELS) + (2 * lv + g + 1))
                        dve.tensor_tensor(yg, ps[2 * g + 1][:, :].rearrange("p (u t) -> p u t", t=C),
                                          yg if lv else
                                          ident16[:, :].unsqueeze(1).to_broadcast([P, 4, C]),
                                          ALU.add).then_inc(y_ready, 1)
                    if lv == 0 and d is not None:
                        finish(d)
                for g in range(2):
                    dve.wait_ge(n_ps, n * 2 + g + 1)
                    dve.tensor_tensor(xf[:, 2 * g:2 * g + 2].rearrange("p j h t -> p (j h t)"),
                                      ps[2 * g][:, :],
                                      xx[:, 2 * g:2 * g + 2].rearrange("p j h t -> p (j h t)"),
                                      ALU.add).then_inc(xf_ready, 1)

            def scan(d, par2, pieces):
                pieces = list(pieces)
                share = -(-len(pieces) // (3 * NT - 1))

                def fill():
                    for _ in range(share):
                        if pieces:
                            pieces.pop(0)()

                dve.memset(state[:, :], 0.0)
                dve.memset(stm[:, :], 0.0).then_inc(s_ready, 1)
                for j in range(NT):
                    dve.wait_ge(z_ps, d * NT + j + 1)
                    dve.tensor_copy(zp[:, 0:4:3, :],
                                    ps[4 + j % 2][:, 0:P].rearrange("p (h v) -> p h v", h=2))\
                        .then_inc(z_ready, 1)
                    fill()
                    dve.wait_ge(u_ps, d * NT + j + 1)
                    dve.tensor_copy(up[:, 0:4:3, :],
                                    ps[5 - j % 2][:, 0:P].rearrange("p (h v) -> p h v", h=2))\
                        .then_inc(u_ready, 1)
                    fill()
                    if j < NT - 1:
                        dve.wait_ge(s_ps, d * (NT - 1) + j + 1)
                        chain(dve.scalar_tensor_tensor(state[:, :], state[:, :],
                                                       dtot[:, par2, j:j + 1],
                                                       ps[4 + j % 2][:, 0:P], ALU.mult, ALU.add))
                        dve.scalar_tensor_tensor(stm[:, :], state[:, :], em[:, par2, j + 1:j + 2],
                                                 headones[:, :], ALU.mult, ALU.mult)\
                            .then_inc(s_ready, 1)
                        fill()
                for piece in pieces:
                    piece()

            def step(n, par2):
                scan(n - 1, 1 - par2, prepare(n, par2))
                for f in range(4):
                    masked(n, f)
                centre(n - 1)
                for f in range(4, 8):
                    masked(n, f)
                add_bonus(n - 1)
                invert(n, n - 1)

            for piece in prepare(0, 0):
                piece()
            for f in range(8):
                masked(0, f)
            invert(0, None)
            with chain.loop(3, 2 * CHAINED) as i:
                step(i * 2 + 1, 1)
                step(i * 2 + 2, 0)
            step(PAIRS - 1, 1)
            scan(PAIRS - 1, 1, [])
            centre(PAIRS - 1)
            add_bonus(PAIRS - 1)
            finish(PAIRS - 1)

            for t, (dst, src, hi) in enumerate(((yal, z, yah), (ybl, q, ybh))):
                for i in range(4):
                    dve.wait_ge(yh_ready, 4 * t + i + 1)
                    lo_part(flat(dst[:, 2 * i:2 * i + 2]), flat(src[:, 2 * i:2 * i + 2]),
                            flat(hi[:, 2 * i:2 * i + 2]), yl_ready, 1)
            with dve.Fori(0, 4) as i:
                for u in range(4):
                    n, m = i * 4 + N_PROJ + u, i * 2 + u // 2
                    split(n + 2, u % RAW, u % 2)
                    dve.wait_ge(slot_done, n + 1)
                    if u % 2 == 0:
                        dve.wait_ge(gate_ready, m + 1)
                        dve.tensor_tensor(ta[:, u // 2, :], ps[0][:, :], gs[:, u // 2, 0, :],
                                          ALU.mult).then_inc(ps_free, 1)
                    else:
                        dve.tensor_tensor(gs[:, u // 2, 1, :], ps[1][:, :], gs[:, u // 2, 1, :],
                                          ALU.mult).then_inc(ps_free, 1)
                        dve.wait_ge(ps_free, n + 1)
                        dve.tensor_tensor(ta[:, u // 2, :], ta[:, u // 2, :], gs[:, u // 2, 1, :],
                                          ALU.add).then_inc(mix_ready, 1)
                        dve.wait_ge(mh_ready, m + 1)
                        lo_part(ml[:, bass.ds(m, 1), :], ta[:, u // 2, :].unsqueeze(1),
                                mh[:, bass.ds(m, 1), :], ml_ready, 1)
            dve.memset(rs1[:, :], 0.0).then_inc(acc_ready, 1)
            with dve.Fori(0, 2) as i:
                for u in range(4):
                    n, m = i * 4 + N_OUT + u, i * 4 + u
                    split(n + 2, u % RAW, u % 2)
                    dve.wait_ge(ps_free, n + 1)
                    dve.wait_ge(acc_ready, m + 1)
                    dve.tensor_tensor(rs1[:, :], rs1[:, :], sq1[:, 0, :], ALU.add)\
                        .then_inc(acc_ready, 1)
            dve.wait_ge(rms_ready, 1)
            chain(dve.reciprocal(rs1[:, :], rs1[:, :]))
            def scaled(k):
                dve.tensor_tensor(sq1[:, k % 2, :], x1[:, k, :], rs1[:, :], ALU.mult)\
                    .then_inc(xs_ready, 1)

            scaled(0)
            for k in range(KT):
                if k + 1 < KT:
                    if k:
                        dve.wait_ge(xnl_ready, k)
                    scaled(k + 1)
                dve.wait_ge(xnh_ready, k + 1)
                dve.scalar_tensor_tensor(xnl[:, k, :], sq1[:, k % 2, :], col["gn2"][:, k:k + 1],
                                         xnh[:, k, :].bitcast(F32), ALU.mult, ALU.subtract)\
                    .then_inc(xnl_ready, 1)
            with chain.loop(FT // 2, 4) as i:
                for u in range(4):
                    n, j = i * 4 + N_UP + u, i * 2 + u // 2
                    split(n + 2, u % RAW, u % 2)
                    c, half = (cg, cv)[u % 2], (u % 2) * FT
                    dve.wait_ge(half_read, n - (N_UP - 26) + 1)
                    chain(dve.scalar_tensor_tensor(
                        c[:, 1:T], ps[u % 2][:, 0:T - 1],
                        par[:, bass.ds(j + (PARAMS["cw1"][0] + half), 1)], c[:, 1:T],
                        ALU.mult, ALU.add))
                    dve.scalar_tensor_tensor(
                        c[:, 2:T], ps[u % 2][:, 0:T - 2],
                        par[:, bass.ds(j + (PARAMS["cw0"][0] + half), 1)], c[:, 2:T],
                        ALU.mult, ALU.add).then_inc(ps_free, 1)
                    if u % 2:
                        dve.wait_ge(ps_free, n + 1)
                        dve.wait_ge(silu_ready, j + 1)
                        dve.tensor_tensor(cv[:, :], cv[:, :], cg[:, :], ALU.mult)\
                            .then_inc(h_ready, 1)
                        dve.wait_ge(hh_ready, j + 1)
                        dve.tensor_tensor(hl[:, bass.ds(j, 1), :], cv[:, :],
                                          hh[:, bass.ds(j, 1), :].bitcast(F32),
                                          ALU.subtract).then_inc(hl_ready, 1)
            with dve.Fori(0, 2) as i:
                for u in range(12):
                    n = i * 12 + N_DOWN + u
                    split(n + 2, u % RAW, u % 2)
                    if u % 3 == 2:
                        m = i * 4 + u // 3
                        xm = x1[:, bass.ds(m, 1), :]
                        dve.wait_ge(slot_done, n + 1)
                        dve.tensor_tensor(xm, xm, ps[(u // 3) % 2][:, :], ALU.add)\
                            .then_inc(ps_free, 1)
            dve.wait_ge(gf_in, 16)
            for j in range(NT):
                dve.wait_ge(y_sq, 2 * j + 2)
                chain(dve.reciprocal(stat[:, 12 + j:13 + j], stat[:, 8 + j:9 + j]))
                for h in range(2):
                    last = dve.scalar_tensor_tensor(
                        yt[:, j, h * T:(h + 1) * T], ps[2 + 2 * (j % 2) + h][:, :],
                        stat[:, 12 + j:13 + j], gf[:, h * T:(h + 1) * T], ALU.mult, ALU.mult)
                last.then_inc(out_ready, 1)

        @block.tensor
        def _(pe):
            def product(n, hb, bank, hi, lo, kn=KT, first=True, last=True, tile_n=None,
                        before_last=None, ready=None):
                pe.wait_ge(w_lo, n + 1)
                if first and tile_n is not None:
                    pe.wait_ge(ps_free, tile_n - 1)
                for k in range(kn):
                    if ready:
                        ready(k)
                    pe.matmul(ps[bank][:, :], whi[:, hb, k, :], hi(k), start=first and k == 0,
                              stop=False)
                    pe.matmul(ps[bank][:, :], whi[:, hb, k, :], lo(k), start=False, stop=False)
                    if k == kn - 1 and before_last:
                        before_last()
                    ins = pe.matmul(ps[bank][:, :], wlo[:, hb, k, :], hi(k), start=False,
                                    stop=last and k == kn - 1)
                ins.then_inc(slot_done, 1)

            pe.wait_ge(consts, 1)
            pe.wait_ge(rows_in, 16 * 21)
            o = 0
            for i, n in enumerate(PAR_ROWS):
                ins = pe.transpose(ps[7][:, o:o + n], rows[0:n, i, :], ident[0:n, 0:n])
                o += n
            ins.then_inc(par_t, 1)
            pe.wait_ge(x_scaled, NT)
            for k in range(KT):
                if k >= 4:
                    pe.wait_ge(xl_ready, k - 3)
                for j in range(NT):
                    ins = pe.transpose(ps[2 + k % 4][:, j * P:(j + 1) * P],
                                       xt[:, j, k * P:(k + 1) * P], ident[:, :])
                ins.then_inc(x_t, 1)

            def xs(t):
                return lambda k: t[:, k, :]

            for n in range(2):
                product(n, n % 2, n % 2, xs(xh), xs(xl),
                        ready=(lambda k: pe.wait_ge(xl_ready, k + 1)) if n == 0 else None)
            for n0, cnt in ((N_RKV, 6), (N_QKV, 3)):
                with pe.Fori(0, cnt) as i:
                    for u in range(4):
                        n = i * 4 + n0 + u
                        product(n, u % 2, u % 2, xs(xh), xs(xl), tile_n=n)

            with pe.Fori(0, 4) as i:
                for w in range(2):
                    c = i * 2 + w
                    n = i * 4 + N_GATE + 2 * w
                    pe.wait_ge(win_in, c + 1)
                    for g in range(2):
                        for ii in range(2):
                            t = 4 * g + 2 * ii
                            ins = pe.matmul(ps[2 + g][:, ii * 2 * P:(ii + 1) * 2 * P],
                                            flat(qc[:, t:t + 2, :]), flat(kc[:, g, :, :]),
                                            start=True, stop=True)
                    ins.then_inc(scores_ps, 1)
                    for g in range(2):
                        ins = pe.transpose(ps[4][:, g * P:(g + 1) * P], vc[:, g, :], ident[:, :])
                    ins.then_inc(vtok_ps, 1)
                    product(n, 0, 0, xs(xh), xs(xl), tile_n=n)
                    pe.wait_ge(probs_ready, c + 1)
                    for u in range(8):
                        ins = pe.transpose(ps[5 + u // 4][:, (u % 4) * P:(u % 4 + 1) * P],
                                           sc[:, u, :], ident[:, :])
                    ins.then_inc(pt_ps, 1)
                    product(n + 1, 1, 1, xs(xh), xs(xl), tile_n=n + 1)
                    for u in range(8):
                        if u % 4 == 0:
                            pe.wait_ge(pt_ready, c * 2 + u // 4 + 1)
                        g, ii, half = u // 4, (u // 2) % 2, u % 2
                        t = 4 * g + 2 * ii
                        ins = pe.matmul(ps[7][half * HD:(half + 1) * HD, t * AC:(t + 2) * AC],
                                        vtok[:, g, half * HD:(half + 1) * HD], pt[:, u, :],
                                        start=True, stop=True)
                    ins.then_inc(o_ps, 1)

            pe.wait_ge(o_done, 8)
            L2 = 2 * LEVELS

            def prepare(n):
                pe.wait_ge(lora_copied, n + 1)
                pe.matmul(ps[0][:, :], lorap[:, :], lora_w_in[:, :], start=True, stop=True)
                pe.matmul(ps[1][:, :], lorap[:, :], lora_a_in[:, :], start=True, stop=True)\
                    .then_inc(lora_ps, 1)
                pe.wait_ge(sq_ready, n + 1)
                pe.matmul(ps[2][:, :], headones[:, :], t2[:, :], start=True, stop=True)\
                    .then_inc(ss_ps, 1)

            def norm_mean(d):
                pe.wait_ge(y_copied, d + 1)
                pe.matmul(ps[4][:, :], headmean[:, :], ysb[:, :], start=True, stop=True)\
                    .then_inc(mean_ps, 1)
                pe.wait_ge(rk_ready, d + 1)
                pe.matmul(ps[5][:, :], headones[:, :],
                          z[:, bass.ds(d + 8, 1), :].rearrange("p a t -> p (a t)"), start=True,
                          stop=True).then_inc(bonus_ps, 1)
                pe.wait_ge(g2_copied, d + 1)
                pe.matmul(ps[7][:, :], g2p[:, :], lora_g_in[:, :], start=True, stop=True)\
                    .then_inc(gmul_ps, 1)

            def norm_var(d):
                pe.wait_ge(ysq_ready, d + 1)
                pe.matmul(ps[4][:, :], headmean[:, :], ysq[:, :], start=True, stop=True)\
                    .then_inc(var_ps, 1)

            def scores(n, par2, d):
                pe.wait_ge(ops_ready, n + 1)
                for f in range(8):
                    src, j = (bp, kp)[f // 4], f % 4
                    if f == 4 and d is not None:
                        norm_mean(d)
                    if f >= 4:
                        pe.wait_ge(g_ready, n * 8 + f - 3)
                    for h in range(2):
                        ins = pe.matmul(ps[f % 4][:, h * 2 * C:(h + 1) * 2 * C],
                                        src[:, h, j * C:(j + 1) * C], ar[:, par2, j, :],
                                        start=True, stop=True)
                    ins.then_inc(g_ps, 1)
                if d is not None:
                    norm_var(d)
                pe.wait_ge(hats_ready, n + 1)
                pe.wait_ge(g_ready, n * 8 + 8)
                for b, src in ((0, t1), (1, t0), (2, vfix)):
                    for j in range(NT):
                        ins = pe.transpose(ps[b][:, j * P:(j + 1) * P], src[:, j * P:(j + 1) * P],
                                           ident[:, :])
                ins.then_inc(tok_ps, 1)
                pe.wait_ge(tok_ready, n + 1)

            def invert(n):
                pe.wait_ge(n1_ready, n + 1)
                for lv in range(LEVELS):
                    for g in range(2):
                        if lv:
                            pe.wait_ge(y_ready, n * L2 + (2 * (lv - 1) + g + 1))
                            pe.wait_ge(x_ready, n * L2 + (2 * (lv - 1) + g + 1))
                        for u in range(4):
                            j, h = 2 * g + u // 2, u % 2
                            ins = pe.matmul(ps[2 * g][:, u * C:(u + 1) * C], n1[:, j, h, :],
                                            yy[:, j, h, :] if lv else ident16[:, :],
                                            start=True, stop=True)
                        ins.then_inc(v_ps, 1)
                    for g in range(2):
                        pe.wait_ge(v_ready, n * L2 + (2 * lv + g + 1))
                        for u in range(4):
                            j, h = 2 * g + u // 2, u % 2
                            ins = pe.matmul(ps[2 * g + 1][:, u * C:(u + 1) * C],
                                            xx[:, j, h, :] if lv else ident16[:, :],
                                            v1[:, j, h, :], start=True, stop=True)
                        ins.then_inc(y_ps, 1)
                        for u in range(4):
                            j, h = 2 * g + u // 2, u % 2
                            x_u = xx[:, j, h, :] if lv else ident16[:, :]
                            o = ps[2 * g][:, u * C:(u + 1) * C]
                            pe.matmul(o, ident16[:, :], x_u, start=True, stop=False)
                            ins = pe.matmul(o, v1[:, j, h, :], x_u, start=False, stop=True)
                        ins.then_inc(x_ps, 1)
                pe.wait_ge(n2_ready, n + 1)
                for g in range(2):
                    pe.wait_ge(y_ready, n * L2 + (2 * (LEVELS - 1) + g + 1))
                    pe.wait_ge(x_ready, n * L2 + (2 * (LEVELS - 1) + g + 1))
                    for u in range(4):
                        j, h = 2 * g + u // 2, u % 2
                        o = ps[2 * g][:, u * C:(u + 1) * C]
                        pe.matmul(o, ident16[:, :], ident16[:, :], start=True, stop=False)
                        pe.matmul(o, nident16[:, :], yy[:, j, h, :], start=False, stop=False)
                        pe.matmul(o, n1[:, j, h, :], yy[:, j, h, :], start=False, stop=False)
                        ins = pe.matmul(o, n2[:, j, h, :], yy[:, j, h, :], start=False, stop=True)
                    ins.then_inc(r_ps, 1)
                for g in range(2):
                    pe.wait_ge(r_ready, n * 2 + g + 1)
                    for u in range(4):
                        j, h = 2 * g + u // 2, u % 2
                        ins = pe.matmul(ps[2 * g][:, u * C:(u + 1) * C], v1[:, j, h, :],
                                        xx[:, j, h, :], start=True, stop=True)
                    ins.then_inc(n_ps, 1)

            def scan(d, par2):
                pe.wait_ge(s_ready, d * NT + 1)
                for j in range(NT):
                    v_h = [flat(vp[:, j, 2 * h:2 * h + 2, :]) for h in range(2)]
                    z_h = [flat(zp[:, 2 * h:2 * h + 2, :]) for h in range(2)]
                    u_h = [flat(up[:, 2 * h:2 * h + 2, :]) for h in range(2)]
                    zb, ub, yb = ps[4 + j % 2][:, 0:P], ps[5 - j % 2][:, 0:P], \
                        ps[6][:, j * C:(j + 1) * C]
                    for h in range(2):
                        pe.matmul(zb, gk[:, j, h, 0:C], v_h[h], start=h == 0, stop=False)
                    if j:
                        pe.wait_ge(s_ready, d * NT + j + 1)
                    pe.matmul(zb, ar[:, par2, j, 0:C], stm[:, :], start=False, stop=True)\
                        .then_inc(z_ps, 1)
                    pe.matmul(yb, stm[:, :], ar[:, par2, j, C:2 * C], start=True, stop=False)
                    for h in range(2):
                        pe.matmul(yb, v_h[h], gk[:, j, h, C:2 * C], start=False, stop=False)
                    pe.wait_ge(z_ready, d * NT + j + 1)
                    pe.matmul(ub, xf[:, j, 0, :], z_h[0], start=True, stop=False)
                    pe.matmul(ub, xf[:, j, 1, :], z_h[1], start=False, stop=True)\
                        .then_inc(u_ps, 1)
                    if j < NT - 1:
                        pe.matmul(zb, ktok[:, j, :], vp[:, j, 0:4:3, :], start=True, stop=False)
                    pe.wait_ge(u_ready, d * NT + j + 1)
                    if j < NT - 1:
                        pe.matmul(zb, btok[:, j, :], up[:, 0:4:3, :], start=False, stop=True)\
                            .then_inc(s_ps, 1)
                    pe.matmul(yb, u_h[0], gb[:, j, 0, C:2 * C], start=False, stop=False)
                    ins = pe.matmul(yb, u_h[1], gb[:, j, 1, C:2 * C], start=False, stop=True)
                ins.then_inc(out_ps, 1)

            def step(n, par2):
                pe.wait_ge(xf_ready, (n - 1) * 2 + 2)
                prepare(n)
                scan(n - 1, 1 - par2)
                scores(n, par2, n - 1)
                invert(n)

            prepare(0)
            scores(0, 0, None)
            invert(0)
            with pe.Fori(0, 3) as i:
                step(i * 2 + 1, 1)
                step(i * 2 + 2, 0)
            step(PAIRS - 1, 1)
            pe.wait_ge(xf_ready, 2 * PAIRS)
            scan(PAIRS - 1, 1)
            norm_mean(PAIRS - 1)
            norm_var(PAIRS - 1)

            with pe.Fori(0, 4) as i:
                for u in range(4):
                    n = i * 4 + N_PROJ + u
                    hi, lo = ((yah, yal), (ybh, ybl))[u % 2]
                    product(n, u % 2, u % 2, xs(hi), xs(lo), tile_n=n,
                            ready=(lambda k: pe.wait_ge(yl_ready, 4 * u + k // 2 + 1))
                            if u < 2 else None)
            pe.wait_ge(ml_ready, KT)
            with pe.Fori(0, 2) as i:
                for u in range(4):
                    n, m = i * 4 + N_OUT + u, i * 4 + u

                    def residual():
                        pe.wait_ge(xblk_in[u % 2], (i * 2 + u // 2) * 16 + 16)
                        for j in range(NT):
                            pe.matmul(ps[u % 2][:, j * P:(j + 1) * P], xblk[:, u % 2, j, :],
                                      ident[:, :], start=False, stop=False)

                    product(n, u % 2, u % 2, xs(mh), xs(ml), tile_n=n, before_last=residual)
            pe.wait_ge(acc_ready, 9)
            pe.matmul(ps[2][:, :], ones[:, :], rs1[:, :], start=True, stop=True).then_inc(tot_ps, 1)
            with pe.Fori(0, FT // 2) as i:
                for u in range(4):
                    n = i * 4 + N_UP + u
                    product(n, u % 2, u % 2, xs(xnh), xs(xnl), tile_n=n,
                            ready=(lambda k: pe.wait_ge(xnl_ready, k + 1)) if u == 0 else None)
            pe.wait_ge(hl_ready, FT)
            with pe.Fori(0, 2) as i:
                for u in range(12):
                    n = i * 12 + N_DOWN + u
                    m, s = divmod(u, 3)
                    product(n, u % 2, m % 2, lambda k: hh[:, 8 * s + k, :],
                            lambda k: hl[:, 8 * s + k, :], kn=DOWN_K[s], first=s == 0,
                            last=s == 2, tile_n=i * 4 + N_DOWN + m)
            pe.wait_ge(ps_free, N_DOWN + KT)
            for j in range(NT):
                if j >= 2:
                    pe.wait_ge(out_ready, j - 1)
                for k in range(KT):
                    ins = pe.transpose(ps[2 + 2 * (j % 2) + k // 4][:, (k % 4) * P:(k % 4 + 1) * P],
                                       x1[:, k, j * P:(j + 1) * P], ident[:, :])
                ins.then_inc(y_t, 1)


_INS = ["x", "norm1_g", "w_in", "rwkv_mu", "w0", "w2", "a0", "a2", "g2", "k_k", "k_a", "r_k",
        "lnx_w", "lnx_b", "b_qkv", "attn_sink", "gate_b", "w_proj_a", "w_proj_b", "w_out",
        "norm2_g", "w_up", "conv_w", "conv_b", "w_down", "normf_g"]


def kernel(**inputs):
    import concourse.bacc as bacc
    from concourse.bass_utils import run_bass_kernel_spmd

    nc = bacc.Bacc("TRN2", target_bir_lowering=False, num_devices=1)
    arrays, args = {}, []
    for name in _INS:
        a = np.ascontiguousarray(inputs[name])
        arrays[f"in_{name}"] = a
        args.append(nc.dram_tensor(f"in_{name}", a.shape, mybir.dt.from_np(a.dtype),
                                   kind="ExternalInput").ap())
    args.append(nc.dram_tensor("out", (1, T, D), F32, kind="ExternalOutput").ap())
    build(nc, *args)
    return run_bass_kernel_spmd(nc, [arrays], core_ids=[0]).results[0]["out"]
```

```python
from contextlib import ExitStack, contextmanager

import numpy as np

import concourse.bass as bass
from concourse import mybir

F32 = mybir.dt.float32
F32R = mybir.dt.float32r
F16 = mybir.dt.float16
U32 = mybir.dt.uint32
ALU = mybir.AluOpType
ACT = mybir.ActivationFunctionType
AX = mybir.AxisListType.X

P = 128
T = 512
D = 1024
KT = D // P
NT = T // P
C = 128
HD = 64
PAIRS = 8
DFF = 2816
FT = DFF // P
RW = 3328
QKV = 1536
AC = 64
LEVELS = 7
CHAINED = 14
HALF_EXP = float(-0.5 * np.exp(-0.5))
NEG = -1e30

RAW, HL = 4, 2
N_AUX, N_QKV, N_RKV, N_GATE, N_PROJ, N_OUT, N_UP = 0, 2, 14, 38, 54, 70, 78
N_DOWN = N_UP + 2 * FT
N_END = N_DOWN + 3 * KT
DOWN_K = (8, 8, FT - 16)


PARAMS, N_PAR = {}, 0
for _name, _n in (("g1", 8), ("gn2", 8), ("mu", 26), ("w0", 8), ("a0", 8), ("kk", 8), ("ka", 8),
                  ("rk", 8), ("lw", 8), ("lb", 8), ("bq", 12), ("bg", 16),
                  ("cw0", 2 * FT), ("cw1", 2 * FT), ("cw2", 2 * FT), ("cb", 2 * FT)):
    PARAMS[_name] = (N_PAR, _n)
    N_PAR += _n
PAR_ROWS = (126, 88, 88)


class Chain:

    def __init__(self, eng, sem):
        self.eng, self.sem, self.base, self.k = eng, sem, 0, 0

    def __call__(self, ins):
        self.k += 1
        ins.then_inc(self.sem, 1)
        self.eng.wait_ge(self.sem, self.base + self.k)

    @contextmanager
    def loop(self, count, per):
        start = self.base + self.k
        with self.eng.Fori(0, count) as i:
            self.base, self.k = i * per + start, 0
            yield i
            assert self.k == per, f"the body uses the chain {self.k} times"
        self.base, self.k = start + count * per, 0


def build(nc, x, norm1_g, w_in, rwkv_mu, w0, w2, a0, a2, g2, k_k, k_a, r_k, lnx_w, lnx_b,
          b_qkv, attn_sink, gate_b, w_proj_a, w_proj_b, w_out, norm2_g, w_up, conv_w,
          conv_b, w_down, normf_g, out):
    with ExitStack() as ctx:
        def sb(name, shape, dt=F32):
            return ctx.enter_context(nc.sbuf_tensor(name, shape, dt))

        def sem(name):
            return ctx.enter_context(nc.semaphore(name))

        ident = sb("ident", [P, P])
        ident16 = sb("ident16", [P, P], F16)
        nident16 = sb("nident16", [P, P], F16)
        headones = sb("headones", [P, P])
        headmean = sb("headmean", [P, P])
        ones = sb("ones", [P, P])
        level_mask = sb("level_mask", [P, LEVELS, P], F16)
        causal = sb("causal", [P, 2 * C])
        notstart = sb("notstart", [P, T])
        notfirst = sb("notfirst", [P, AC * 9])
        par = sb("par", [P, N_PAR])
        col = {name: par[:, o:o + n] for name, (o, n) in PARAMS.items()}
        omu = sb("omu", [P, 26])
        whalf = sb("whalf", [P, KT])
        ahalf = sb("ahalf", [P, KT])
        eps_col = sb("eps_col", [P, 2])
        sink = sb("sink", [P, 8])
        lora = sb("lora", [P, D])
        g2s = sb("g2s", [P, D])
        lora_w_in = sb("lora_w_in", [P, T])
        lora_a_in = sb("lora_a_in", [P, T])
        lora_g_in = sb("lora_g_in", [P, T])
        raw = sb("raw", [P, RAW, KT, P])
        whi = sb("whi", [P, HL, KT, P], F32R)
        wlo = sb("wlo", [P, HL, KT, P], F32R)
        stat = sb("stat", [P, 16])
        carrier = sb("carrier", [P, 8])
        spare = sb("spare", [P, 1])

        arena_bytes = (nc.sbuf_top - nc.sbuf_base - 64) // 32 * 32
        arena = sb("arena", [P, arena_bytes // 4])
        base = nc.lookup_mloc(arena).addr
        K = 1024

        def size(shape, dt):
            return (int(np.prod(shape[1:])) * (2 if dt == F16 else 4) + 31) // 32 * 32

        def at(off, name, shape, dt=F32):
            assert off + size(shape, dt) <= arena_bytes, name
            return nc.alloc_sbuf_tensor_at(name, shape, dt, offset=base + off)

        def taker(off, end):
            place = [off]

            def take(name, shape, dt=F32):
                t = at(place[0], name, shape, dt)
                place[0] += size(shape, dt)
                assert place[0] <= end, name
                return t
            return take

        XHL, ZR, QR, KVR = 0, 32 * K, 80 * K, 96 * K
        WR = KVR + 2 * 2 * (T + AC) * 4
        xh = at(XHL, "xh", [P, KT, T], F32R)
        xl = at(XHL + 16 * K, "xl", [P, KT, T], F32R)
        z = at(ZR, "z", [P, 24, T])
        q = at(QR, "q", [P, KT, T])
        kb = at(KVR, "kb", [P, 2, AC + T])
        vb = at(KVR + 2 * (T + AC) * 4, "vb", [P, 2, AC + T])
        xt = at(ZR, "xt", [P, NT, D])
        junk = at(QR, "junk", [P, D])
        rows = at(QR + 4 * K, "rows", [P, 3, P])
        mixed = at(WR, "mixed", [P, 2, T])
        gst = at(WR + 4 * K, "gst", [P, 2, T])

        take = taker(WR + 8 * K, arena_bytes)
        qc = take("qc", [P, KT, AC])
        kc = take("kc", [P, 2, 2, P])
        vc = take("vc", [P, 2, P])
        vtok = take("vtok", [P, 2, 4, HD])
        sc = take("sc", [P, 8, P])
        pt = take("pt", [P, 8, P])
        mx = take("mx", [P, 8])
        nmx = take("nmx", [P, 8])
        es = take("es", [P, 8])
        den = take("den", [P, 8])

        take = taker(KVR, arena_bytes)
        gb = take("gb", [P, NT, 2, 2 * C])
        ar = take("ar", [P, 2, NT, 2 * C])
        xf = take("xf", [P, NT, 2, C])
        gk = take("gk", [P, NT, 2, 2 * C])
        bp = take("bp", [P, 2, T])
        kp = take("kp", [P, 2, T])
        vp = take("vp", [P, NT, 4, HD])
        e = take("e", [P, NT, C + 1])
        vfix = take("vfix", [P, T])
        kqn = take("kqn", [P, T])
        ysb = take("ysb", [P, T])
        ysq = take("ysq", [P, T])
        wcum = take("wcum", [P, T])
        take = taker(XHL, ZR)
        ei = take("ei", [P, T])
        kkn = take("kkn", [P, T])
        kmod = take("kmod", [P, T])
        t0 = take("t0", [P, T])
        t1 = take("t1", [P, T])
        t2 = take("t2", [P, T])
        btok = take("btok", [P, NT, P])
        ktok = take("ktok", [P, NT, P])
        n1 = take("n1", [P, NT, 2, C], F16)
        n2 = take("n2", [P, NT, 2, C], F16)
        xx = take("xx", [P, NT, 2, C], F16)
        yy = take("yy", [P, NT, 2, C], F16)
        v1 = take("v1", [P, NT, 2, C], F16)
        up = take("up", [P, 4, HD])
        zp = take("zp", [P, 4, HD])
        state = take("state", [P, P])
        stm = take("stm", [P, P])
        lorap = take("lorap", [P, P])
        g2p = take("g2p", [P, P])
        knorm = take("knorm", [P, 2 * NT])
        ystd = take("ystd", [P, 2 * NT])
        em = take("em", [P, 2, NT])
        dtot = take("dtot", [P, 2, NT])

        yah = at(XHL, "yah", [P, KT, T], F32R)
        yal = at(XHL + 16 * K, "yal", [P, KT, T], F32R)
        ybh = at(ZR + 16 * K, "ybh", [P, KT, T], F32R)
        ybl = at(ZR + 32 * K, "ybl", [P, KT, T], F32R)
        mh = at(ZR, "mh", [P, KT, T], F32R)
        ml = at(QR, "ml", [P, KT, T], F32R)
        gl = at(KVR, "gl", [P, 2, 2, T])
        gs = at(KVR + 28 * K + 8 * K, "gs", [P, 2, 2, T])
        ta = at(KVR + 8 * K, "ta", [P, 2, T])
        xblk = at(KVR + 12 * K, "xblk", [P, 2, NT, P])
        hh = at(ZR, "hh", [P, FT, T], F32R)
        hl = at(ZR + 2 * K * FT, "hl", [P, FT, T], F32R)
        X1 = ZR + 4 * K * FT
        x1 = at(X1, "x1", [P, KT, T])
        sq1 = at(X1 + 16 * K, "sq1", [P, 2, T])
        rs1 = at(X1 + 20 * K, "rs1", [P, T])
        ot = at(X1 + 16 * K, "ot", [P, 2, T])
        junk2 = at(X1 + 23 * K, "junk2", [P, NT, P])
        ysums = at(X1 + 22 * K, "ysums", [P, NT, KT])
        xnh = at(XHL, "xnh", [P, KT, T], F32R)
        xnl = at(XHL + 16 * K, "xnl", [P, KT, T], F32R)
        cg = at(X1 + 22 * K, "cg", [P, T])
        cv = at(X1 + 24 * K, "cv", [P, T])
        gf = at(X1 + 26 * K, "gf", [P, D])
        yt = at(XHL, "yt", [P, NT, D])

        gates = nc.dram_tensor("gates_scratch", (16, P, T), F32, kind="Internal").ap()
        ps = [ctx.enter_context(nc.psum_tensor(f"ps{b}", [P, T], F32)) for b in range(8)]

        loaded = [sem(f"loaded{b}") for b in range(RAW)]
        w_hi = sem("w_hi")
        w_lo = sem("w_lo")
        slot_done = sem("slot_done")
        ps_free = sem("ps_free")
        half_read = sem("half_read")
        consts = sem("consts")
        pool_chain = sem("pool_chain")
        act_chain = sem("act_chain")
        dve_chain = sem("dve_chain")
        rows_in = sem("rows_in")
        rows_in_pool = sem("rows_in_pool")
        misc_in = sem("misc_in")
        x_in = [sem(f"x_in{j}") for j in range(NT)]
        par_t = sem("par_t")
        par_ready = sem("par_ready")
        x_sq = sem("x_sq")
        x_scaled = sem("x_scaled")
        x_t = sem("x_t")
        xh_ready = sem("xh_ready")
        xl_ready = sem("xl_ready")
        gst_free = [sem(f"gst_free{b}") for b in range(2)]
        gate_stored = [sem(f"gate_stored{b}") for b in range(2)]
        gate_in = [sem(f"gate_in{b}") for b in range(2)]
        gate_ready = sem("gate_ready")
        win_in = sem("win_in")
        scores_ps = sem("scores_ps")
        vwin_in = sem("vwin_in")
        vtok_ps = sem("vtok_ps")
        vtok_ready = sem("vtok_ready")
        sc_ready = sem("sc_ready")
        exp_done = sem("exp_done")
        probs_ready = sem("probs_ready")
        pt_ps = sem("pt_ps")
        pt_ready = sem("pt_ready")
        o_ps = sem("o_ps")
        o_done = sem("o_done")
        lora_copied = sem("lora_copied")
        g2_copied = sem("g2_copied")
        pair_done = sem("pair_done")
        lora_ps = sem("lora_ps")
        sq_ready = sem("sq_ready")
        ss_ps = sem("ss_ps")
        norm_ready = sem("norm_ready")
        kex_ready = sem("kex_ready")
        kn_ps = sem("kn_ps")
        kqn_ready = sem("kqn_ready")
        tanh_ready = sem("tanh_ready")
        rel_ready = sem("rel_ready")
        exps_ready = sem("exps_ready")
        ops_ready = sem("ops_ready")
        hats_ready = sem("hats_ready")
        kmod_ready = sem("kmod_ready")
        removed_ready = sem("removed_ready")
        end_ready = sem("end_ready")
        rk_product = sem("rk_product")
        rk_ready = sem("rk_ready")
        g_ps = sem("g_ps")
        g_ready = sem("g_ready")
        tok_ps = sem("tok_ps")
        tok_ready = sem("tok_ready")
        vp_ready = sem("vp_ready")
        n1_ready = sem("n1_ready")
        n2_ready = sem("n2_ready")
        v_ps = sem("v_ps")
        v_ready = sem("v_ready")
        y_ps = sem("y_ps")
        y_start = sem("y_start")
        y_ready = [sem(f"y_ready{g}") for g in range(2)]
        x_ps = sem("x_ps")
        x_ready = sem("x_ready")
        r_ps = sem("r_ps")
        r_ready = sem("r_ready")
        n_ps = sem("n_ps")
        xf_ready = sem("xf_ready")
        z_ps = sem("z_ps")
        z_ready = sem("z_ready")
        u_ps = sem("u_ps")
        u_ready = sem("u_ready")
        s_ps = sem("s_ps")
        s_ready = sem("s_ready")
        out_ps = sem("out_ps")
        y_copied = sem("y_copied")
        mean_ps = sem("mean_ps")
        yc_ready = sem("yc_ready")
        ysq_ready = sem("ysq_ready")
        var_ps = sem("var_ps")
        std_ready = sem("std_ready")
        vex_ready = sem("vex_ready")
        rstd_ps = sem("rstd_ps")
        bonus_ps = sem("bonus_ps")
        gmul_ps = sem("gmul_ps")
        yh_ready = sem("yh_ready")
        yl_ready = sem("yl_ready")
        mix_ready = sem("mix_ready")
        mh_ready = sem("mh_ready")
        ml_ready = sem("ml_ready")
        xblk_in = [sem(f"xblk_in{b}") for b in range(2)]
        sq1_ready = sem("sq1_ready")
        acc_ready = sem("acc_ready")
        tot_ps = sem("tot_ps")
        rms_ready = sem("rms_ready")
        rms_ps = sem("rms_ps")
        xs_ready = sem("xs_ready")
        xnh_ready = sem("xnh_ready")
        xnl_ready = sem("xnl_ready")
        silu_ready = sem("silu_ready")
        h_ready = sem("h_ready")
        hh_ready = sem("hh_ready")
        hl_ready = sem("hl_ready")
        gf_in = sem("gf_in")
        y_t = sem("y_t")
        y_gained = sem("y_gained")
        ysum_ready = sem("ysum_ready")
        y_sq = sem("y_sq")
        y_rms = sem("y_rms")
        out_ready = [sem(f"out_ready{e}") for e in range(2)]
        stored = sem("stored")

        w_in_v = w_in[0].rearrange("(k p) c -> p k c", p=P)
        w_up_v = w_up[0].rearrange("(k p) c -> p k c", p=P)
        w_down_v = w_down[0].rearrange("(k p) c -> p k c", p=P)
        w_out_v = w_out[0].rearrange("(k p) c -> p k c", p=P)
        w_pa_v = w_proj_a[0].rearrange("(k p) c -> p k c", p=P)
        w_pb_v = w_proj_b[0].rearrange("(h k p) c -> h p k c", h=2, p=HD)
        w_q_v = w_in[0, :, RW:RW + D].rearrange("(k p) (h t c) -> h p k t c", p=P, h=2, c=HD)
        w_k_v = w_in[0, :, RW + D:RW + QKV].rearrange("(k p) (b h t c) -> b h p k t c", p=P, b=2,
                                                      h=2, c=HD)
        x_v = x[0].rearrange("(j p) c -> p j c", p=P)
        out_v = out[0].rearrange("(j p) c -> p j c", p=P)

        def flat(ap):
            return ap.rearrange("p a b -> p (a b)")

        def load_values(n, b):
            return (n - b) * 8 + 32

        block = ctx.enter_context(nc.Block())

        @block.sync
        def _(sp):
            def load(n, b, pieces, reuse=True):
                if reuse:
                    sp.wait_ge(w_lo, n - 3)
                for dst, src in pieces:
                    sp.dma_start(dst, src).then_inc(loaded[b], 16)

            def by_k(b, src, kn=KT):
                h = kn // 2
                return [(raw[:, b, 0:h, :], src[:, 0:h]), (raw[:, b, h:kn, :], src[:, h:kn])]

            def by_col(b, lo, hi):
                return [(raw[:, b, :, 0:HD], lo), (raw[:, b, :, HD:P], hi)]

            for j in range(NT):
                sp.dma_start(xt[:, j, :], x_v[:, j, :]).then_inc(x_in[j], 16)
            for n in range(2):
                load(n, n, by_k(n, w_in_v[:, :, 3 * D + n * P:3 * D + (n + 1) * P]), reuse=False)
            o = PARAMS["bq"][0]
            bq, bk = b_qkv[0][0:D], b_qkv[0][D:QKV]
            bqv = bq.rearrange("(h t d) -> h t d", h=2, d=HD)
            bkv = bk.rearrange("(b h t d) -> b h t d", b=2, h=2, d=HD)
            for h in range(2):
                dst = rows[:, 0, h * HD:(h + 1) * HD]
                sp.dma_start(dst[o:o + 8], bqv[h]).then_inc(rows_in, 16)
                sp.dma_start(dst[o + 8:o + 10], bkv[0][h]).then_inc(rows_in, 16)
                sp.dma_start(dst[o + 10:o + 12], bkv[1][h]).then_inc(rows_in, 16)
            for t in range(8):
                n = N_QKV + t
                load(n, n % RAW, by_col(n % RAW, w_q_v[0][:, :, t, :], w_q_v[1][:, :, t, :]),
                     reuse=n >= RAW)
            for u in range(4):
                b = (2 + u) % RAW
                kv, g = divmod(u, 2)
                load(N_QKV + 8 + u, b, by_col(b, w_k_v[kv][0][:, :, g, :], w_k_v[kv][1][:, :, g, :]))
            with sp.Fori(0, 6) as i:
                for u in range(4):
                    b = (2 + u) % RAW
                    load(i * 4 + N_RKV + u, b, by_k(b, w_in_v[:, :, bass.ts(i * 4 + u, P)]))
            with sp.Fori(0, 4) as i:
                for u in range(4):
                    b = (2 + u) % RAW
                    load(i * 4 + N_GATE + u, b,
                         by_k(b, w_in_v[:, :, RW + QKV:][:, :, bass.ts(i * 4 + u, P)]))
            with sp.Fori(0, 4) as i:
                for u in range(4):
                    b = (2 + u) % RAW
                    cols = bass.ts(i * 2 + u // 2, P)
                    if u % 2 == 0:
                        pieces = by_k(b, w_pa_v[:, :, cols])
                    else:
                        pieces = [(raw[0:HD, b], w_pb_v[0][:, :, cols]),
                                  (raw[HD:P, b], w_pb_v[1][:, :, cols])]
                    load(i * 4 + N_PROJ + u, b, pieces)
            with sp.Fori(0, 2) as i:
                for u in range(4):
                    b = (2 + u) % RAW
                    load(i * 4 + N_OUT + u, b, by_k(b, w_out_v[:, :, bass.ts(i * 4 + u, P)]))
            with sp.Fori(0, FT // 2) as i:
                for u in range(4):
                    b = (2 + u) % RAW
                    src = w_up_v[:, :, (u % 2) * DFF:][:, :, bass.ts(i * 2 + u // 2, P)]
                    load(i * 4 + N_UP + u, b, by_k(b, src))
            with sp.Fori(0, 2) as i:
                for u in range(12):
                    b = (2 + u) % RAW
                    m, s = divmod(u, 3)
                    src = w_down_v[:, 8 * s:8 * s + DOWN_K[s], bass.ts(i * 4 + m, P)]
                    load(i * 12 + N_DOWN + u, b, by_k(b, src, DOWN_K[s]))
            for n in range(N_END, N_END + 2):
                load(n, n % RAW, by_k(n % RAW, w_down_v[:, 0:2, 0:P], 2))
            for j in range(NT):
                sp.wait_ge(out_ready[j % 2], j // 2 + 1)
                sp.dma_start(out_v[:, j, :], yt[:, j, :]).then_inc(stored, 16)
            sp.wait_ge(stored, 16 * NT)

        @block.gpsimd
        def _(pool):
            chain = Chain(pool, pool_chain)
            def diagonal(t, value):
                chain(pool.memset(t[:, :], 0.0))
                chain(pool.affine_select(out=t[:, :], in_=t[:, :], compare_op=ALU.not_equal,
                                         fill=value, base=0, pattern=[[-1, P]],
                                         channel_multiplier=1))

            diagonal(ident, 1.0)
            pool.wait_ge(pool_chain, chain.k)
            pool.memset(eps_col[:, 0:1], 1e-6).then_inc(consts, 1)
            for name, src in (("ka", k_a[0]), ("rk", r_k[0].rearrange("h d -> (h d)")),
                              ("lw", lnx_w[0]), ("lb", lnx_b[0])):
                o, n = PARAMS[name]
                pool.dma_start(rows[o:o + n, 0, :], src.rearrange("(n p) -> n p", p=P))\
                    .then_inc(rows_in_pool, 16)
            for i in range(3):
                src = conv_w[0][i].rearrange("(n p) -> n p", p=P)
                dst = rows[(i % 2) * 44:(i % 2) * 44 + 44, 1 + i // 2, :]
                pool.dma_start(dst, src).then_inc(rows_in_pool, 16)
            pool.dma_start(rows[44:88, 2, :], conv_b[0].rearrange("(n p) -> n p", p=P))\
                .then_inc(rows_in_pool, 16)
            chain(pool.memset(notfirst[:, :], 0.0))
            chain(pool.memset(notfirst[:, 0:AC], NEG))
            chain(pool.memset(lora_w_in[HD:P, :], 0.0))
            chain(pool.memset(lora_a_in[0:HD, :], 0.0))
            chain(pool.memset(kb[:, :, 0:AC], 0.0))
            chain(pool.memset(vb[:, :, 0:AC], 0.0))
            chain(pool.memset(kc[0:HD, :, 1, :], 0.0))
            chain(pool.memset(vtok[:, :, 1:3, :], 0.0))
            pool.memset(kc[HD:P, :, 0, :], 0.0).then_inc(consts, 1)

            pool.dma_start(lora[0:HD, :], w2[0]).then_inc(misc_in, 16)
            pool.dma_start(lora[HD:P, :], a2[0]).then_inc(misc_in, 16)
            pool.dma_start(g2s[:, :], g2[0]).then_inc(misc_in, 16)
            sv = attn_sink[0].rearrange("(half g ii b) -> b g ii half", half=2, g=2, ii=2)
            for b in range(2):
                for u in range(4):
                    g, ii = divmod(u, 2)
                    src = sv[b][g][ii:ii + 1].to_broadcast([HD, 2])
                    pool.dma_start(sink[b * HD:(b + 1) * HD, 2 * u:2 * u + 2], src,
                                   allow_slow_non_contiguous=True).then_inc(misc_in, 16)

            pool.wait_ge(consts, 2)
            diagonal(ident16, 1.0)
            diagonal(nident16, -1.0)
            chain(pool.memset(eps_col[:, 1:2], 64e-5))
            chain(pool.memset(ones[:, :], 1.0))
            for t, value in ((headones, 1.0), (headmean, 1.0 / HD)):
                chain(pool.memset(t[:, :], 0.0))
                for h in range(2):
                    chain(pool.memset(t[h * HD:(h + 1) * HD, h * HD:(h + 1) * HD], value))
            chain(pool.memset(causal[:, :], 1.0))
            for o, op in ((0, ALU.is_gt), (C, ALU.is_ge)):
                chain(pool.affine_select(out=causal[:, o:o + C], in_=causal[:, o:o + C],
                                         compare_op=op, fill=0.0, base=0, pattern=[[1, C]],
                                         channel_multiplier=-1))
            chain(pool.memset(level_mask[:, :, :], 0.0))
            for lv in range(LEVELS):
                m = 1 << lv
                view = level_mask[:, lv, :].rearrange("p (a b c) -> p a b c", b=2, c=m)[:, :, 0, :]
                chain(pool.memset(view, 1.0))
                n = P // (2 * m)
                chain(pool.affine_select(out=view, in_=view, compare_op=ALU.is_ge, fill=0.0,
                                         base=-m, pattern=[[-2 * m, n], [0, m]],
                                         channel_multiplier=1))
                chain(pool.affine_select(out=view, in_=view, compare_op=ALU.is_ge, fill=0.0,
                                         base=2 * m - 1, pattern=[[2 * m, n], [0, m]],
                                         channel_multiplier=-1))
            chain(pool.memset(notstart[:, :], 1.0))
            chain(pool.memset(notstart[:, :].rearrange("p (j t) -> p j t", t=C)[:, :, 0:1], 0.0))

            for u in range(2):
                pool.sem_inc(gst_free[u], 1)

            def gate_out(i, u):
                pool.wait_ge(ps_free, i * 2 + N_GATE + u + 1)
                pool.dma_start(gates[i * 2 + u], gst[:, u, :]).then_inc(gate_stored[u], 16)

            def gate_out_done(i, u):
                pool.wait_ge(gate_stored[u], i * 16 + 16)
                pool.sem_inc(gst_free[u], 1)

            with pool.Fori(0, 7) as i:
                for u in range(2):
                    gate_out(i, u)
                    gate_out_done(i, u)
            gate_out(7, 0)

            def copies(p):
                pool.tensor_copy(lorap[:, :], lora[:, bass.ts(p, P)]).then_inc(lora_copied, 1)

            def gate_copy(p):
                pool.tensor_copy(g2p[:, :], g2s[:, bass.ts(p, P)]).then_inc(g2_copied, 1)

            def remainder(p):
                pool.wait_ge(n1_ready, p + 1)
                pool.tensor_tensor(n2[:, :, :, :], gb[:, :, :, 0:C], n1[:, :, :, :], ALU.subtract)\
                    .then_inc(n2_ready, 1)

            def to_chunk_end(n):
                k_p = z[:, bass.ds(n + 8, 1), :].rearrange("p a t -> p (a t)")
                pool.wait_ge(kmod_ready, n + 1)
                pool.tensor_tensor(k_p, z[:, bass.ds(n, 1), :].rearrange("p a t -> p (a t)"),
                                   kmod[:, :], ALU.mult).then_inc(rk_product, 1)
                pool.wait_ge(exps_ready, n + 1)
                pool.tensor_tensor(t0[:, :].rearrange("p (j t) -> p j t", t=C),
                                   ei[:, :].rearrange("p (j t) -> p j t", t=C),
                                   e[:, :, C:C + 1].to_broadcast([P, NT, C]), ALU.mult)\
                    .then_inc(end_ready, 1)
                pool.wait_ge(end_ready, n + 1)
                pool.wait_ge(removed_ready, n + 1)
                pool.tensor_tensor(t2[:, :], t1[:, :], t0[:, :], ALU.mult)
                pool.tensor_tensor(t0[:, :], kmod[:, :], t0[:, :], ALU.mult)\
                    .then_inc(hats_ready, 1)

            pool.wait_ge(misc_in, 16 * 11)
            pool.wait_ge(o_done, 8)
            chain(pool.memset(gb[:, :, :, :], 0.0))
            chain(pool.memset(gk[:, :, :, :], 0.0))
            chain(pool.memset(bp[HD:P, 0, :], 0.0))
            chain(pool.memset(bp[0:HD, 1, :], 0.0))
            chain(pool.memset(kp[HD:P, 0, :], 0.0))
            pool.wait_ge(slot_done, N_PROJ)
            copies(0)
            chain(pool.memset(kp[0:HD, 1, :], 0.0))
            gate_out(7, 1)
            gate_copy(0)
            chain(pool.memset(vp[:, :, 1:3, :], 0.0))
            chain(pool.memset(up[:, 1:3, :], 0.0))
            pool.memset(zp[:, 1:3, :], 0.0).then_inc(consts, 1)
            for u in range(2):
                gate_out_done(7, u)

            def pair(n, following=True):
                if following:
                    pool.wait_ge(lora_ps, n * 2 + 2)
                    copies(n + 1)
                to_chunk_end(n)
                remainder(n)

            def next_gate_copy(n):
                pool.wait_ge(gmul_ps, n)
                gate_copy(n)

            pair(0)
            with pool.Fori(0, PAIRS - 2) as i:
                pair(i + 1)
                next_gate_copy(i + 1)
            pair(PAIRS - 1, following=False)
            next_gate_copy(PAIRS - 1)

            pool.wait_ge(pair_done, PAIRS)

            def gates_back(m, b):
                pool.dma_start(gl[:, b, 0, :], gates[m]).then_inc(gate_in[b], 16)
                pool.dma_start(gl[:, b, 1, :], gates[m + 8]).then_inc(gate_in[b], 16)

            for m in range(2):
                gates_back(m, m)
            with pool.Fori(0, 3) as i:
                for u in range(2):
                    pool.wait_ge(mix_ready, i * 2 + u + 1)
                    gates_back(i * 2 + 2 + u, u)
            for m in range(2):
                pool.dma_start(xblk[:, m], x_v[:, :, bass.ts(m, P)]).then_inc(xblk_in[m], 16)
            with pool.Fori(0, 3) as i:
                for u in range(2):
                    pool.wait_ge(slot_done, i * 2 + N_OUT + u + 1)
                    pool.dma_start(xblk[:, u], x_v[:, :, bass.ts(i * 2 + 2 + u, P)])\
                        .then_inc(xblk_in[u], 16)
            pool.dma_start(gf[:, :], normf_g.rearrange("(o n) -> o n", o=1).to_broadcast([P, D]))\
                .then_inc(gf_in, 16)
            pool.wait_ge(gf_in, 16)

        @block.scalar
        def _(act):
            chain = Chain(act, act_chain)

            def split(n, b, hb, first=False):
                act.wait_ge(loaded[b], load_values(n, b))
                if not first:
                    act.wait_ge(slot_done, n - 1)
                act.activation(flat(whi[:, hb]), flat(raw[:, b]), ACT.Copy).then_inc(w_hi, 1)

            def table(func):
                act.activation(spare[:, :], eps_col[:, 0:1], func)

            for name, src in (("g1", norm1_g[0]), ("gn2", norm2_g[0]), ("mu", rwkv_mu[0]),
                              ("w0", w0[0]), ("a0", a0[0]), ("kk", k_k[0]), ("bg", gate_b[0])):
                o, n = PARAMS[name]
                act.dma_start(rows[o:o + n, 0, :], src.rearrange("(n p) -> n p", p=P))\
                    .then_inc(rows_in, 16)
            act.wait_ge(consts, 1)
            table(ACT.Sqrt)
            for j in range(NT):
                act.wait_ge(x_in[j], 16)
                chain(act.activation(junk[:, :], xt[:, j, :], ACT.Square,
                                     accum_out=stat[:, j:j + 1]))
            act.activation(stat[:, 4:8], stat[:, 0:4], ACT.Sqrt, scale=1.0 / D,
                           bias=eps_col[:, 0:1]).then_inc(x_sq, 1)
            act.wait_ge(par_t, 1)
            act.activation(par[:, :], ps[7][:, 0:N_PAR], ACT.Copy).then_inc(par_ready, 1)
            act.wait_ge(par_ready, 1)
            split(0, 0, 0, first=True)
            split(1, 1, 1, first=True)
            for k in range(KT):
                act.wait_ge(x_t, k + 1)
                act.activation(xh[:, k, :], ps[2 + k % 4][:, :], ACT.Copy,
                               scale=col["g1"][:, k:k + 1]).then_inc(xh_ready, 1)

            def keep(dst, n, bank, mt):
                act.wait_ge(slot_done, n + 1)
                act.activation(dst, ps[bank][:, :], ACT.Copy, scale=omu[:, mt:mt + 1] if
                               isinstance(mt, int) else omu[:, bass.ds(mt, 1)]).then_inc(half_read, 1)

            act.wait_ge(consts, 2)
            act.wait_ge(par_ready, 2)
            split(2, 2, 0)
            keep(mixed[:, 0, :], 0, 0, 24)
            split(3, 3, 1)
            keep(mixed[:, 1, :], 1, 1, 25)
            act.wait_ge(ps_free, 2)
            act.activation(lora_w_in[0:HD, :], mixed[0:HD, 0, :], ACT.Tanh)
            act.activation(lora_a_in[HD:P, :], mixed[HD:P, 0, :], ACT.Copy)
            act.activation(lora_g_in[:, :], mixed[:, 1, :], ACT.Sigmoid)
            def biased(dst, n, bank, func, bias):
                act.wait_ge(slot_done, n + 1)
                act.activation(dst, ps[bank][:, :], func, bias=bias).then_inc(ps_free, 1)

            oq = PARAMS["bq"][0]
            act.wait_ge(ps_free, N_QKV)
            with act.Fori(0, 2) as i:
                for u in range(4):
                    n, m = i * 4 + N_QKV + u, i * 4 + u
                    split(n + 2, u % RAW, u % 2)
                    biased(q[:, bass.ds(m, 1), :], n, u % 2, ACT.Identity,
                           par[:, bass.ds(m + oq, 1)])
            for u in range(4):
                n = N_QKV + 8 + u
                split(n + 2, u % RAW, u % 2)
                biased((kb, vb)[u // 2][:, u % 2, AC:], n, u % 2, ACT.Identity,
                       par[:, oq + 8 + u:oq + 9 + u])

            def window(c):
                act.activation(qc[:, :, :], q[:, :, bass.ds(c * AC, AC)], ACT.Copy,
                               scale=HD ** -0.5)
                act.activation(kc[0:HD, :, 0, :], kb[0:HD, :, bass.ds(c * AC, P)], ACT.Copy)
                act.activation(kc[HD:P, :, 1, :], kb[HD:P, :, bass.ds(c * AC, P)], ACT.Copy)\
                    .then_inc(win_in, 1)

            def values(c):
                act.activation(vc[:, :, :], vb[:, :, bass.ds(c * AC, P)], ACT.Copy)\
                    .then_inc(vwin_in, 1)

            def values_back(c):
                act.wait_ge(vtok_ps, c + 1)
                act.activation(vtok[:, :, 0:4:3, :],
                               ps[4][:, 0:2 * P].rearrange("p (g h v) -> p g h v", g=2, h=2),
                               ACT.Copy).then_inc(vtok_ready, 1)

            def exponentials(c):
                act.wait_ge(sc_ready, c + 1)
                for u in range(8):
                    act.activation(sc[:, u, :], sc[:, u, :], ACT.Exp, bias=nmx[:, u:u + 1],
                                   accum_out=den[:, u:u + 1])
                act.activation(es[:, :], es[:, :], ACT.Exp).then_inc(exp_done, 1)

            def rkv(i, u):
                n, m = i * 4 + N_RKV + u, i * 4 + u
                split(n + 2, u % RAW, u % 2)
                keep(z[:, m:m + 1, :] if isinstance(m, int) else z[:, bass.ds(m, 1), :], n, u % 2, m)

            act.wait_ge(ps_free, N_RKV)
            window(0)
            values(0)
            rkv(0, 0)
            values_back(0)
            values(1)
            rkv(0, 1)
            exponentials(0)
            rkv(0, 2)
            window(1)
            rkv(0, 3)
            with act.Fori(1, 6) as i:
                for u in range(4):
                    rkv(i, u)

            act.wait_ge(ps_free, N_GATE)

            def pcol(name, n):
                return par[:, bass.ds(n + PARAMS[name][0], 1)]

            def key_square(n):
                act.activation(t2[:, :], z[:, bass.ds(n + 8, 1), :], ACT.Square,
                               scale=pcol("kk", n)).then_inc(sq_ready, 1)
                act.activation(vfix[:, :], z[:, bass.ds(n + 16, 1), :], ACT.Copy)

            def attend(i, c, w, follow=2):
                def gate_tile(u):
                    n = i * 4 + N_GATE + 2 * w + u
                    act.wait_ge(gst_free[u], c + 1)
                    biased(gst[:, u, :], n, u, ACT.Identity,
                           par[:, bass.ds(i * 4 + og + 2 * w + u, 1)])

                if follow == 0:
                    table(ACT.Sqrt)
                act.wait_ge(pt_ps, c + 1)
                for g in range(2):
                    act.activation(flat(pt[:, 4 * g:4 * g + 4, :]), ps[5 + g][:, :], ACT.Copy)\
                        .then_inc(pt_ready, 1)
                if follow > 0:
                    exponentials(c + 1)
                split(i * 4 + N_GATE + 2 * w + 2, 2 * w, 0)
                gate_tile(0)
                if follow > 1:
                    window(c + 2)
                if follow > 0:
                    values_back(c + 1)
                if follow > 1:
                    values(c + 2)
                if follow == 0:
                    gate_tile(1)
                    key_square(0)
                split(i * 4 + N_GATE + 2 * w + 3, 2 * w + 1, 1)
                if follow == 0:
                    return
                gate_tile(1)

            og = PARAMS["bg"][0]
            with act.Fori(0, 3) as i:
                for w in range(2):
                    attend(i, i * 2 + w, w)
            attend(3, 6, 0, follow=1)
            attend(3, 7, 1, follow=0)


            def key_norm(n):
                act.wait_ge(ss_ps, n + 1)
                act.activation(knorm[:, :], ps[6][:, 0:2 * NT], ACT.Sqrt).then_inc(norm_ready, 1)

            def key_norm_back(n):
                act.wait_ge(kn_ps, n + 1)
                act.activation(kqn[:, :], ps[6][:, :], ACT.Copy).then_inc(kqn_ready, 1)

            def decay_tanh(n):
                act.wait_ge(lora_ps, n * 2 + 1)
                act.activation(t0[:, :], ps[5][:, :], ACT.Tanh, scale=0.5,
                               bias=whalf[:, bass.ds(n, 1)]).then_inc(tanh_ready, 1)

            def rate_tanh(n):
                act.wait_ge(lora_ps, n * 2 + 2)
                act.activation(t1[:, :], ps[7][:, :], ACT.Tanh, scale=0.5,
                               bias=ahalf[:, bass.ds(n, 1)]).then_inc(tanh_ready, 1)

            def exponentials_of(n, par2):
                act.wait_ge(rel_ready, n + 1)
                cum = wcum[:, :].rearrange("p (j t) -> p j t", t=C)
                act.activation(e[:, :, 1:C + 1], t0[:, :].rearrange("p (j t) -> p j t", t=C), ACT.Exp)
                act.activation(e[:, :, 0:1], cum[:, :, C // 2 - 1:C // 2], ACT.Exp, scale=-1.0)
                act.activation(em[:, par2, :].unsqueeze(2), cum[:, :, C // 2 - 1:C // 2], ACT.Exp)
                act.activation(dtot[:, par2, :].unsqueeze(2), cum[:, :, C - 1:C], ACT.Exp)
                act.activation(ei[:, :], t0[:, :], ACT.Exp, scale=-1.0).then_inc(exps_ready, 1)
                table(ACT.Sqrt)

            def norm_head(d):
                act.wait_ge(out_ps, d + 1)
                act.activation(ysb[:, :], ps[6][:, :], ACT.Copy).then_inc(y_copied, 1)

            def norm_square(d):
                act.wait_ge(yc_ready, d + 1)
                act.activation(ysq[:, :], ysb[:, :], ACT.Square).then_inc(ysq_ready, 1)

            def deviation(d):
                act.wait_ge(var_ps, d + 1)
                act.activation(ystd[:, :], ps[4][:, 0:2 * NT], ACT.Sqrt, bias=eps_col[:, 1:2])\
                    .then_inc(std_ready, 1)

            def copies(n, d):
                if d is not None:
                    norm_head(d)
                act.wait_ge(g_ready, n * 8 + 4)
                act.activation(n1[:, :, :, :], gb[:, :, :, 0:C], ACT.Copy).then_inc(n1_ready, 1)
                if d is not None:
                    norm_square(d)
                act.wait_ge(tok_ps, n + 1)
                act.activation(flat(btok), ps[0][:, :], ACT.Copy).then_inc(tok_ready, 1)
                act.activation(flat(ktok), ps[1][:, :], ACT.Copy).then_inc(tok_ready, 1)

            def group(t, g):
                return t[:, 2 * g:2 * g + 2].rearrange("p j h t -> p (j h t)")

            def invert(n, par2, d, following=True):
                def transposed(lv):
                    for g in range(2):
                        act.wait_ge(x_ps, n * (2 * LEVELS) + (2 * lv + g + 1))
                        act.activation(group(xx, g), ps[2 * g + 1][:, :], ACT.Copy)\
                            .then_inc(x_ready, 1)

                for lv in range(LEVELS):
                    if lv:
                        transposed(lv - 1)
                        act.wait_ge(y_ps, n * (2 * LEVELS - 2) + (2 * lv - 1))
                        act.activation(group(yy, 0), ps[0][:, :], ACT.Copy).then_inc(y_ready[0], 1)
                    if lv == 0 and d is not None:
                        deviation(d)
                    if lv == 3 and following:
                        key_norm(n + 1)
                        table(ACT.Tanh)
                    if lv == 2:
                        act.wait_ge(rk_product, n + 1)
                        act.activation(z[:, bass.ds(n + 8, 1), :], z[:, bass.ds(n + 8, 1), :],
                                       ACT.Copy, scale=pcol("rk", n)).then_inc(rk_ready, 1)
                    if lv == 5 and following:
                        decay_tanh(n + 1)
                    if lv == 6 and following:
                        key_norm_back(n + 1)
                transposed(LEVELS - 1)
                for g in range(2):
                    act.wait_ge(r_ps, n * 2 + g + 1)
                    act.activation(v1[:, 2 * g:2 * g + 2].rearrange("p j h t -> p (j h t)"),
                                   ps[2 * g][:, :], ACT.Copy).then_inc(r_ready, 1)
                if following:
                    rate_tanh(n + 1)
                    exponentials_of(n + 1, 1 - par2)

            def step(n, par2, following=True):
                copies(n, n - 1)
                if following:
                    key_square(n + 1)
                invert(n, par2, n - 1, following)

            key_norm(0)
            table(ACT.Tanh)
            decay_tanh(0)
            rate_tanh(0)
            key_norm_back(0)
            exponentials_of(0, 0)
            copies(0, None)
            key_square(1)
            invert(0, 0, None)
            with act.Fori(0, 3) as i:
                step(i * 2 + 1, 1)
                step(i * 2 + 2, 0)
            step(PAIRS - 1, 1, following=False)
            def hi_part(dst, src, i):
                act.activation(flat(dst[:, 2 * i:2 * i + 2]), flat(src[:, 2 * i:2 * i + 2]),
                               ACT.Copy).then_inc(yh_ready, 1)

            act.wait_ge(pair_done, 4)
            for i in range(2):
                hi_part(yah, z, i)
            norm_head(PAIRS - 1)
            norm_square(PAIRS - 1)
            deviation(PAIRS - 1)

            act.wait_ge(pair_done, PAIRS)
            for i in range(2, 4):
                hi_part(yah, z, i)
            for i in range(4):
                hi_part(ybh, q, i)
            with act.Fori(0, 4) as i:
                for u in range(4):
                    n, m = i * 4 + N_PROJ + u, i * 2 + u // 2
                    if u % 2 == 0:
                        act.wait_ge(gate_in[u // 2], i * 32 + 32)
                        act.activation(flat(gs[:, u // 2]), flat(gl[:, u // 2]), ACT.Sigmoid)\
                            .then_inc(gate_ready, 1)
                    split(n + 2, u % RAW, u % 2)
                    if u % 2:
                        act.wait_ge(mix_ready, m + 1)
                        act.activation(mh[:, bass.ds(m, 1), :], ta[:, u // 2, :], ACT.Copy)\
                            .then_inc(mh_ready, 1)
            with act.Fori(0, 2) as i:
                for u in range(4):
                    n, m = i * 4 + N_OUT + u, i * 4 + u
                    if u < 3:
                        split(n + 2, u % RAW, u % 2)
                    act.wait_ge(slot_done, n + 1)
                    act.wait_ge(acc_ready, m + 1)
                    act.activation(sq1[:, 0, :], ps[u % 2][:, :], ACT.Square)\
                        .then_inc(sq1_ready, 1)
                    act.activation(x1[:, bass.ds(m, 1), :], ps[u % 2][:, :], ACT.Copy)\
                        .then_inc(ps_free, 1)
                split(i * 4 + N_OUT + 5, 3, 1)
            table(ACT.Sqrt)
            act.wait_ge(tot_ps, 1)
            act.activation(stat[:, 0:NT], ps[2][:, 0:NT], ACT.Sqrt, scale=1.0 / D,
                           bias=eps_col[:, 0:1]).then_inc(rms_ready, 1)
            for k in range(KT):
                act.wait_ge(xs_ready, k + 1)
                act.activation(xnh[:, k, :], sq1[:, k % 2, :], ACT.Copy,
                               scale=col["gn2"][:, k:k + 1]).then_inc(xnh_ready, 1)
            with act.Fori(0, FT // 2) as i:
                for u in range(4):
                    n, j = i * 4 + N_UP + u, i * 2 + u // 2
                    split(n + 2, u % RAW, u % 2)
                    act.wait_ge(slot_done, n + 1)
                    c, half = (cg, cv)[u % 2], (u % 2) * FT
                    act.activation(c[:, :], ps[u % 2][:, :], ACT.Identity,
                                   scale=par[:, bass.ds(j + (PARAMS["cw2"][0] + half), 1)],
                                   bias=par[:, bass.ds(j + (PARAMS["cb"][0] + half), 1)])\
                        .then_inc(half_read, 1)
                    if u % 2 == 0:
                        act.wait_ge(ps_free, n + 1)
                        act.activation(cg[:, :], cg[:, :], ACT.Silu).then_inc(silu_ready, 1)
                    else:
                        act.wait_ge(h_ready, j + 1)
                        act.activation(hh[:, bass.ds(j, 1), :], cv[:, :], ACT.Copy)\
                            .then_inc(hh_ready, 1)
            def squares(t):
                act.wait_ge(y_t, t + 1)
                if t:
                    act.wait_ge(y_sq, t)
                for j in range(NT):
                    ins = act.activation(junk2[:, j, :], ps[2 + t % 2][:, j * P:(j + 1) * P],
                                         ACT.Square, accum_out=ysums[:, j, t:t + 1])
                ins.then_inc(y_sq, 1)

            table(ACT.Sqrt)
            for u in range(24):
                split(N_DOWN + u + 2, u % RAW, u % 2)
                if u % 12 in (3, 6, 9):
                    squares(u // 3 - 1)
                if u % 12 == 11:
                    squares(u // 3)
            act.wait_ge(ysum_ready, 1)
            act.activation(stat[:, 4:8], stat[:, 0:4], ACT.Sqrt, scale=1.0 / D,
                           bias=eps_col[:, 0:1]).then_inc(y_rms, 1)
            act.wait_ge(ysum_ready, 2)
            act.wait_ge(y_gained, KT)
            for j in (1, 3):
                act.activation(yt[:, j, :], yt[:, j, :], ACT.Copy, scale=stat[:, 8 + j:9 + j])\
                    .then_inc(out_ready[1], 1)

        @block.vector
        def _(dve):
            chain = Chain(dve, dve_chain)

            def split(n, b, hb):
                dve.wait_ge(w_hi, n + 1)
                dve.tensor_tensor(flat(wlo[:, hb]), flat(raw[:, b]), flat(whi[:, hb]).bitcast(F32),
                                  ALU.subtract).then_inc(w_lo, 1)

            def lo_part(dst, src, hi, s, k):
                dve.tensor_tensor(dst, src, hi.bitcast(F32), ALU.subtract).then_inc(s, k)

            dve.wait_ge(x_sq, 1)
            chain(dve.reciprocal(stat[:, 8:12], stat[:, 4:8]))
            for j in range(NT):
                dve.tensor_scalar(xt[:, j, :], xt[:, j, :], stat[:, 8 + j:9 + j], None, ALU.mult)\
                    .then_inc(x_scaled, 1)
            dve.wait_ge(par_ready, 1)
            dve.tensor_scalar(whalf[:, :], col["w0"], 0.5, None, ALU.mult)
            dve.tensor_scalar(ahalf[:, :], col["a0"], 0.5, None, ALU.mult)
            dve.tensor_scalar(omu[:, :], col["mu"], -1.0, 1.0, ALU.mult, ALU.add)\
                .then_inc(par_ready, 1)
            split(0, 0, 0)
            split(1, 1, 1)
            for k in range(KT):
                dve.wait_ge(xh_ready, k + 1)
                dve.scalar_tensor_tensor(xl[:, k, :], ps[2 + k % 4][:, :], col["g1"][:, k:k + 1],
                                         xh[:, k, :].bitcast(F32), ALU.mult, ALU.subtract)\
                    .then_inc(xl_ready, 1)

            om = PARAMS["mu"][0]

            def shift(dst, n, bank, mt):
                dve.wait_ge(half_read, n + 1 if isinstance(n, int) and n < 2 else n - (N_RKV - 2) + 1)
                dve.scalar_tensor_tensor(dst[:, 1:T], ps[bank][:, 0:T - 1],
                                         par[:, bass.ds(mt + om, 1)], dst[:, 1:T], ALU.mult,
                                         ALU.add).then_inc(ps_free, 1)

            split(2, 2, 0)
            shift(mixed[:, 0, :], 0, 0, 24)
            split(3, 3, 1)
            shift(mixed[:, 1, :], 1, 1, 25)
            with dve.Fori(0, 3) as i:
                for u in range(4):
                    split(i * 4 + N_QKV + u + 2, u % RAW, u % 2)

            def maxima(c):
                mask = notfirst[:, bass.ds(c * AC, P)].unsqueeze(1).to_broadcast([P, 4, P])
                dve.wait_ge(scores_ps, c + 1)
                for g in range(2):
                    last = dve.tensor_tensor(sc[:, 4 * g:4 * g + 4, :],
                                             ps[2 + g][:, :].rearrange("p (u k) -> p u k", k=P),
                                             mask, ALU.add)
                chain(last)
                chain(dve.tensor_reduce(mx[:, :], sc[:, :, :], AX, ALU.max))
                chain(dve.tensor_tensor(mx[:, :], mx[:, :], sink[:, :], ALU.max))
                dve.tensor_scalar(nmx[:, :], mx[:, :], -1.0, None, ALU.mult)
                dve.tensor_tensor(es[:, :], sink[:, :], mx[:, :], ALU.subtract)\
                    .then_inc(sc_ready, 1)

            def normalise(c):
                dve.wait_ge(exp_done, c + 1)
                chain(dve.tensor_tensor(den[:, :], den[:, :], es[:, :], ALU.add))
                chain(dve.reciprocal(den[:, :], den[:, :]))
                dve.tensor_tensor(sc[:, :, :], sc[:, :, :],
                                  den[:, :].unsqueeze(2).to_broadcast([P, 8, P]), ALU.mult)\
                    .then_inc(probs_ready, 1)

            def rkv(i, u):
                n, m = i * 4 + N_RKV + u, i * 4 + u
                split(n + 2, u % RAW, u % 2)
                dst = z[:, m:m + 1, :] if isinstance(m, int) else z[:, bass.ds(m, 1), :]
                shift(dst.rearrange("p a t -> p (a t)"), n, u % 2, m)

            dve.wait_ge(ps_free, N_RKV)
            dve.wait_ge(misc_in, 16 * 11)
            rkv(0, 0)
            maxima(0)
            rkv(0, 1)
            rkv(0, 2)
            normalise(0)
            rkv(0, 3)
            with dve.Fori(1, 6) as i:
                for u in range(4):
                    rkv(i, u)


            def attend(i, c, w, last=False):
                if not last:
                    maxima(c + 1)
                split(i * 4 + N_GATE + 2 * w + 2, 2 * w, 0)
                dve.wait_ge(o_ps, c + 1)
                dve.tensor_copy(q[:, :, bass.ds(c * AC, AC)],
                                ps[7][:, :].rearrange("p (t s) -> p t s", s=AC))\
                    .then_inc(o_done, 1)
                if not last:
                    normalise(c + 1)
                split(i * 4 + N_GATE + 2 * w + 3, 2 * w + 1, 1)

            with chain.loop(3, 10) as i:
                for w in range(2):
                    attend(i, i * 2 + w, w)
            attend(3, 6, 0)
            attend(3, 7, 1, last=True)


            def pcol(name, n):
                return par[:, bass.ds(n + PARAMS[name][0], 1)]

            def tile(n):
                return z[:, bass.ds(n, 1), :].rearrange("p a t -> p (a t)")

            def chunks(t):
                return t.rearrange("p (j t) -> p j t", t=C)

            def decays(n):
                dve.wait_ge(tanh_ready, n * 2 + 1)
                chain(dve.tensor_scalar(t0[:, :], t0[:, :], 1.0, HALF_EXP, ALU.add, ALU.mult))
                chain(dve.tensor_tensor_scan(wcum[:, :], notstart[:, :], t0[:, :], 0.0,
                                             ALU.mult, ALU.add))
                dve.tensor_tensor(chunks(t0[:, :]), chunks(wcum[:, :]),
                                  chunks(wcum[:, :])[:, :, C // 2 - 1:C // 2].to_broadcast(
                                      [P, NT, C]), ALU.subtract).then_inc(rel_ready, 1)

            def prepare(n, par2):
                r_p, k_p = tile(n), tile(n + 8)

                def key():
                    dve.wait_ge(kqn_ready, n + 1)
                    dve.scalar_tensor_tensor(kkn[:, :], k_p, pcol("kk", n), kqn[:, :], ALU.mult,
                                             ALU.mult)

                def rates():
                    dve.wait_ge(tanh_ready, n * 2 + 2)
                    chain(dve.tensor_scalar(t1[:, :], t1[:, :], 0.5, 0.5, ALU.mult, ALU.add))

                def factor():
                    chain(dve.tensor_scalar(t2[:, :], t1[:, :], 1.0, pcol("ka", n), ALU.subtract,
                                            ALU.mult))

                def modified():
                    dve.scalar_tensor_tensor(kmod[:, :], t2[:, :], 1.0, k_p, ALU.add, ALU.mult)\
                        .then_inc(kmod_ready, 1)

                def removed():
                    chain(dve.tensor_tensor(t1[:, :], kkn[:, :], t1[:, :], ALU.mult))

                def a_tilde():
                    dve.wait_ge(exps_ready, n + 1)
                    if isinstance(n, int) and n == 0:
                        dve.wait_ge(consts, 3)
                        for u in range(2):
                            dve.wait_ge(gst_free[u], 9)
                    dve.scalar_tensor_tensor(ar[:, par2, :, 0:C], chunks(kkn[:, :]), -1.0,
                                             e[:, :, 0:C], ALU.mult, ALU.mult)\
                        .then_inc(removed_ready, 1)

                def r_tilde():
                    dve.tensor_tensor(ar[:, par2, :, C:2 * C], chunks(r_p), e[:, :, 1:C + 1],
                                      ALU.mult)

                def padded(dst, src, h, last=False):
                    def piece():
                        hs = slice(h * HD, (h + 1) * HD)
                        ins = dve.tensor_tensor(dst[hs, h, :], src[hs, :], ei[hs, :], ALU.mult)
                        if last:
                            ins.then_inc(ops_ready, 1)
                    return piece

                return [key, rates, factor, modified, removed, a_tilde, r_tilde,
                        padded(bp, t1, 0), padded(bp, t1, 1), padded(kp, kmod, 0),
                        padded(kp, kmod, 1, last=True)]

            def value_tokens(n):
                dve.wait_ge(tok_ps, n + 1)
                dve.tensor_copy(vp[:, :, 0:4:3, :],
                                ps[2][:, :].rearrange("p (j h v) -> p j h v", h=2, v=HD))\
                    .then_inc(vp_ready, 1)

            def spread(dst, src):
                return dve.tensor_copy(dst[:, :].rearrange("p (u v) -> p u v", v=HD),
                                       src[:, :].unsqueeze(2).to_broadcast([P, 2 * NT, HD]))

            def key_norms(n):
                dve.wait_ge(norm_ready, n + 1)
                chain(dve.tensor_scalar(knorm[:, :], knorm[:, :], 1e-12, None, ALU.max))
                chain(dve.reciprocal(knorm[:, :], knorm[:, :]))
                spread(kqn, knorm).then_inc(kex_ready, 1)

            def deviations(d):
                dve.wait_ge(std_ready, d + 1)
                chain(dve.reciprocal(ystd[:, :], ystd[:, :]))
                spread(ysq, ystd).then_inc(vex_ready, 1)

            def masked(n, f):
                dst = (gb, gk)[f // 4][:, f % 4]
                dve.wait_ge(g_ps, n * 8 + f + 1)
                dve.memset(carrier[:, f:f + 1], 0.0)
                dve.copy_predicated(dst, causal[:, :].bitcast(U32).unsqueeze(1)
                                    .to_broadcast([P, 2, 2 * C]),
                                    ps[f % 4][:, :].rearrange("p (h t) -> p h t", h=2))\
                    .then_inc(g_ready, 1)

            def centre(d):
                dve.wait_ge(mean_ps, d + 1)
                dve.tensor_tensor(ysb[:, :], ysb[:, :], ps[4][:, :], ALU.subtract)\
                    .then_inc(yc_ready, 1)

            def add_bonus(d):
                dve.wait_ge(bonus_ps, d + 1)
                chain(dve.tensor_tensor(tile(d + 8), tile(d + 16), ps[5][:, :], ALU.mult))

            def scaled_output(d):
                dve.wait_ge(rstd_ps, d + 1)
                chain(dve.scalar_tensor_tensor(ysb[:, :], ysb[:, :], pcol("lw", d), ps[4][:, :],
                                               ALU.mult, ALU.mult))

            def with_bonus(d):
                chain(dve.scalar_tensor_tensor(ysb[:, :], ysb[:, :], pcol("lb", d), tile(d + 8),
                                               ALU.add, ALU.add))

            def gated(d):
                dve.wait_ge(gmul_ps, d + 1)
                dve.tensor_tensor(tile(d), ysb[:, :], ps[7][:, :], ALU.mult).then_inc(pair_done, 1)

            def invert(n, d, following=True):
                for lv in range(LEVELS):
                    for g in range(2):
                        dve.wait_ge(v_ps, n * (2 * LEVELS) + (2 * lv + g + 1))
                        mask = level_mask[:, lv, :].unsqueeze(1).to_broadcast([P, 4, C])
                        dve.tensor_tensor(v1[:, 2 * g:2 * g + 2].rearrange("p j h t -> p (j h) t"),
                                          ps[2 * g][:, :].rearrange("p (u t) -> p u t", t=C),
                                          mask, ALU.mult).then_inc(v_ready, 1)
                    if lv == 0:
                        for g in range(2):
                            yg, vg = (t[:, 2 * g:2 * g + 2].rearrange("p j h t -> p (j h) t")
                                      for t in (yy, v1))
                            dve.wait_ge(v_ready, n * (2 * LEVELS) + (g + 1))
                            dve.tensor_tensor(yg, vg, ident16[:, :].unsqueeze(1).to_broadcast(
                                [P, 4, C]), ALU.add).then_inc(y_start, 1)
                    else:
                        yg = yy[:, 2:4].rearrange("p j h t -> p (j h) t")
                        dve.wait_ge(y_ps, n * (2 * LEVELS - 2) + 2 * lv)
                        dve.tensor_tensor(yg, ps[2][:, :].rearrange("p (u t) -> p u t", t=C),
                                          yg, ALU.add).then_inc(y_ready[1], 1)
                    if lv == 1 and d is not None:
                        deviations(d)
                    if lv == 4 and following:
                        key_norms(n + 1)
                    if lv >= 2 and lv < 6 and d is not None:
                        (add_bonus, scaled_output, with_bonus, gated)[lv - 2](d)
                if following:
                    decays(n + 1)
                for g in range(2):
                    dve.wait_ge(n_ps, n * 2 + g + 1)
                    dve.tensor_tensor(xf[:, 2 * g:2 * g + 2].rearrange("p j h t -> p (j h t)"),
                                      ps[2 * g][:, :],
                                      xx[:, 2 * g:2 * g + 2].rearrange("p j h t -> p (j h t)"),
                                      ALU.add).then_inc(xf_ready, 1)

            def scan(d, par2, pieces):
                pieces = list(pieces)

                def fill():
                    if pieces:
                        pieces.pop(0)()

                dve.memset(state[:, :], 0.0)
                dve.memset(stm[:, :], 0.0).then_inc(s_ready, 1)
                for j in range(NT):
                    dve.wait_ge(z_ps, d * NT + j + 1)
                    dve.tensor_copy(zp[:, 0:4:3, :],
                                    ps[4 + j % 2][:, 0:P].rearrange("p (h v) -> p h v", h=2))\
                        .then_inc(z_ready, 1)
                    fill()
                    dve.wait_ge(u_ps, d * NT + j + 1)
                    dve.tensor_copy(up[:, 0:4:3, :],
                                    ps[5 - j % 2][:, 0:P].rearrange("p (h v) -> p h v", h=2))\
                        .then_inc(u_ready, 1)
                    fill()
                    if j < NT - 1:
                        dve.wait_ge(s_ps, d * (NT - 1) + j + 1)
                        chain(dve.scalar_tensor_tensor(state[:, :], state[:, :],
                                                       dtot[:, par2, j:j + 1],
                                                       ps[4 + j % 2][:, 0:P], ALU.mult, ALU.add))
                        dve.scalar_tensor_tensor(stm[:, :], state[:, :], em[:, par2, j + 1:j + 2],
                                                 headones[:, :], ALU.mult, ALU.mult)\
                            .then_inc(s_ready, 1)
                        fill()
                for piece in pieces:
                    piece()

            def step(n, par2, following=True):
                scan(n - 1, 1 - par2, prepare(n, par2))
                for f in range(4):
                    masked(n, f)
                centre(n - 1)
                for f in range(4, 8):
                    masked(n, f)
                value_tokens(n)
                invert(n, n - 1, following)

            key_norms(0)
            decays(0)
            for piece in prepare(0, 0):
                piece()
            for f in range(8):
                masked(0, f)
            value_tokens(0)
            invert(0, None)
            with chain.loop(3, 2 * CHAINED) as i:
                step(i * 2 + 1, 1)
                step(i * 2 + 2, 0)
            step(PAIRS - 1, 1, following=False)
            def y_lo(t, i):
                dst, src, hi = ((yal, z, yah), (ybl, q, ybh))[t]
                dve.wait_ge(yh_ready, 4 * t + i + 1)
                lo_part(flat(dst[:, 2 * i:2 * i + 2]), flat(src[:, 2 * i:2 * i + 2]),
                        flat(hi[:, 2 * i:2 * i + 2]), yl_ready, 1)

            scan(PAIRS - 1, 1, [lambda: y_lo(0, 0), lambda: y_lo(0, 1)])
            centre(PAIRS - 1)
            add_bonus(PAIRS - 1)
            deviations(PAIRS - 1)
            scaled_output(PAIRS - 1)
            with_bonus(PAIRS - 1)
            gated(PAIRS - 1)

            for t in range(2):
                for i in range(4):
                    if t or i >= 2:
                        y_lo(t, i)
            with dve.Fori(0, 4) as i:
                for u in range(4):
                    n, m = i * 4 + N_PROJ + u, i * 2 + u // 2
                    split(n + 2, u % RAW, u % 2)
                    dve.wait_ge(slot_done, n + 1)
                    if u % 2 == 0:
                        dve.wait_ge(gate_ready, m + 1)
                        dve.tensor_tensor(ta[:, u // 2, :], ps[0][:, :], gs[:, u // 2, 0, :],
                                          ALU.mult).then_inc(ps_free, 1)
                    else:
                        dve.tensor_tensor(gs[:, u // 2, 1, :], ps[1][:, :], gs[:, u // 2, 1, :],
                                          ALU.mult).then_inc(ps_free, 1)
                        dve.wait_ge(ps_free, n + 1)
                        dve.tensor_tensor(ta[:, u // 2, :], ta[:, u // 2, :], gs[:, u // 2, 1, :],
                                          ALU.add).then_inc(mix_ready, 1)
                        dve.wait_ge(mh_ready, m + 1)
                        lo_part(ml[:, bass.ds(m, 1), :], ta[:, u // 2, :].unsqueeze(1),
                                mh[:, bass.ds(m, 1), :], ml_ready, 1)
            dve.memset(rs1[:, :], 0.0).then_inc(acc_ready, 1)
            with dve.Fori(0, 2) as i:
                for u in range(4):
                    n, m = i * 4 + N_OUT + u, i * 4 + u
                    if u < 3:
                        split(n + 2, u % RAW, u % 2)
                    dve.wait_ge(sq1_ready, m + 1)
                    dve.wait_ge(acc_ready, m + 1)
                    dve.tensor_tensor(rs1[:, :], rs1[:, :], sq1[:, 0, :], ALU.add)\
                        .then_inc(acc_ready, 1)
                split(i * 4 + N_OUT + 5, 3, 1)
            dve.wait_ge(rms_ready, 1)
            chain(dve.reciprocal(stat[:, 4:8], stat[:, 0:NT]))
            dve.tensor_copy(rs1[:, :].rearrange("p (j c) -> p j c", c=P),
                            stat[:, 4:8].unsqueeze(2).to_broadcast([P, NT, P]))\
                .then_inc(rms_ready, 1)
            dve.wait_ge(rms_ps, 1)
            def scaled(k):
                dve.tensor_tensor(sq1[:, k % 2, :], x1[:, k, :], ps[3][:, :], ALU.mult)\
                    .then_inc(xs_ready, 1)

            scaled(0)
            for k in range(KT):
                if k + 1 < KT:
                    if k:
                        dve.wait_ge(xnl_ready, k)
                    scaled(k + 1)
                dve.wait_ge(xnh_ready, k + 1)
                dve.scalar_tensor_tensor(xnl[:, k, :], sq1[:, k % 2, :], col["gn2"][:, k:k + 1],
                                         xnh[:, k, :].bitcast(F32), ALU.mult, ALU.subtract)\
                    .then_inc(xnl_ready, 1)
            with chain.loop(FT // 2, 4) as i:
                for u in range(4):
                    n, j = i * 4 + N_UP + u, i * 2 + u // 2
                    split(n + 2, u % RAW, u % 2)
                    c, half = (cg, cv)[u % 2], (u % 2) * FT
                    dve.wait_ge(half_read, n - (N_UP - 26) + 1)
                    chain(dve.scalar_tensor_tensor(
                        c[:, 1:T], ps[u % 2][:, 0:T - 1],
                        par[:, bass.ds(j + (PARAMS["cw1"][0] + half), 1)], c[:, 1:T],
                        ALU.mult, ALU.add))
                    dve.scalar_tensor_tensor(
                        c[:, 2:T], ps[u % 2][:, 0:T - 2],
                        par[:, bass.ds(j + (PARAMS["cw0"][0] + half), 1)], c[:, 2:T],
                        ALU.mult, ALU.add).then_inc(ps_free, 1)
                    if u % 2:
                        dve.wait_ge(ps_free, n + 1)
                        dve.wait_ge(silu_ready, j + 1)
                        dve.tensor_tensor(cv[:, :], cv[:, :], cg[:, :], ALU.mult)\
                            .then_inc(h_ready, 1)
                        dve.wait_ge(hh_ready, j + 1)
                        dve.tensor_tensor(hl[:, bass.ds(j, 1), :], cv[:, :],
                                          hh[:, bass.ds(j, 1), :].bitcast(F32),
                                          ALU.subtract).then_inc(hl_ready, 1)
            dve.wait_ge(gf_in, 16)

            def gained(t, b):
                dve.wait_ge(y_sq, t + 1)
                cols = bass.ds(t * P, P)
                ins = dve.tensor_tensor(yt[:, :, cols],
                                        ps[2 + b][:, :].rearrange("p (j c) -> p j c", c=P),
                                        gf[:, cols].unsqueeze(1).to_broadcast([P, NT, P]),
                                        ALU.mult)
                ins.then_inc(y_gained, 1)

            with dve.Fori(0, 2) as i:
                for u in range(12):
                    n = i * 12 + N_DOWN + u
                    if u < 11:
                        split(n + 2, u % RAW, u % 2)
                    if u in (3, 6, 9):
                        gained(i * 4 + u // 3 - 1, (u // 3 - 1) % 2)
                    if u % 3 == 2:
                        m = i * 4 + u // 3
                        xm = x1[:, bass.ds(m, 1), :]
                        dve.wait_ge(slot_done, n + 1)
                        dve.tensor_tensor(ot[:, (u // 3) % 2, :].unsqueeze(1), xm,
                                          ps[(u // 3) % 2][:, :].unsqueeze(1), ALU.add)\
                            .then_inc(ps_free, 1)
                split(i * 12 + N_DOWN + 13, 3, 1)
                gained(i * 4 + 3, 1)
            dve.wait_ge(y_sq, KT)
            dve.tensor_reduce(stat[:, 0:4], ysums[:, :, :], AX, ALU.add).then_inc(ysum_ready, 1)
            dve.wait_ge(y_rms, 1)
            dve.reciprocal(stat[:, 8:12], stat[:, 4:8]).then_inc(ysum_ready, 1)
            dve.wait_ge(ysum_ready, 2)
            dve.wait_ge(y_gained, KT)
            for j in (0, 2):
                dve.tensor_scalar(yt[:, j, :], yt[:, j, :], stat[:, 8 + j:9 + j], None, ALU.mult)\
                    .then_inc(out_ready[0], 1)

        @block.tensor
        def _(pe):
            def product(n, hb, bank, hi, lo, kn=KT, first=True, last=True, tile_n=None,
                        before_last=None, ready=None):
                pe.wait_ge(w_lo, n + 1)
                if first and tile_n is not None:
                    pe.wait_ge(ps_free, tile_n - 1)
                for k in range(kn):
                    if ready:
                        ready(k)
                    pe.matmul(ps[bank][:, :], whi[:, hb, k, :], hi(k), start=first and k == 0,
                              stop=False)
                    pe.matmul(ps[bank][:, :], whi[:, hb, k, :], lo(k), start=False, stop=False)
                    if k == kn - 1 and before_last:
                        before_last()
                    ins = pe.matmul(ps[bank][:, :], wlo[:, hb, k, :], hi(k), start=False,
                                    stop=last and k == kn - 1)
                ins.then_inc(slot_done, 1)

            pe.wait_ge(consts, 1)
            pe.wait_ge(rows_in, 16 * 13)
            pe.wait_ge(rows_in_pool, 16 * 8)
            o = 0
            for i, n in enumerate(PAR_ROWS):
                ins = pe.transpose(ps[7][:, o:o + n], rows[0:n, i, :], ident[0:n, 0:n])
                o += n
            ins.then_inc(par_t, 1)
            pe.wait_ge(x_scaled, NT)
            for k in range(KT):
                if k >= 4:
                    pe.wait_ge(xl_ready, k - 3)
                for j in range(NT):
                    ins = pe.transpose(ps[2 + k % 4][:, j * P:(j + 1) * P],
                                       xt[:, j, k * P:(k + 1) * P], ident[:, :])
                ins.then_inc(x_t, 1)

            def xs(t):
                return lambda k: t[:, k, :]

            for n in range(2):
                product(n, n % 2, n % 2, xs(xh), xs(xl),
                        ready=(lambda k: pe.wait_ge(xl_ready, k + 1)) if n == 0 else None)
            def tiles(i, n0):
                for u in range(4):
                    n = i * 4 + n0 + u
                    product(n, u % 2, u % 2, xs(xh), xs(xl), tile_n=n)
                    if isinstance(n, int) and n == N_RKV:
                        attention_scores(0)
                        values(0)

            def attention_scores(c):
                pe.wait_ge(win_in, c + 1)
                for g in range(2):
                    for ii in range(2):
                        t = 4 * g + 2 * ii
                        ins = pe.matmul(ps[2 + g][:, ii * 2 * P:(ii + 1) * 2 * P],
                                        flat(qc[:, t:t + 2, :]), flat(kc[:, g, :, :]),
                                        start=True, stop=True)
                ins.then_inc(scores_ps, 1)

            def values(c):
                pe.wait_ge(vwin_in, c + 1)
                for g in range(2):
                    ins = pe.transpose(ps[4][:, g * P:(g + 1) * P], vc[:, g, :], ident[:, :])
                ins.then_inc(vtok_ps, 1)

            with pe.Fori(0, 3) as i:
                tiles(i, N_QKV)
            tiles(0, N_RKV)
            with pe.Fori(1, 6) as i:
                tiles(i, N_RKV)

            def attend(i, c, w, last=False):
                n = i * 4 + N_GATE + 2 * w
                pe.wait_ge(probs_ready, c + 1)
                for u in range(8):
                    ins = pe.transpose(ps[5 + u // 4][:, (u % 4) * P:(u % 4 + 1) * P],
                                       sc[:, u, :], ident[:, :])
                ins.then_inc(pt_ps, 1)
                if not last:
                    attention_scores(c + 1)
                product(n, 0, 0, xs(xh), xs(xl), tile_n=n)
                pe.wait_ge(vtok_ready, c + 1)
                for u in range(8):
                    if u % 4 == 0:
                        pe.wait_ge(pt_ready, c * 2 + u // 4 + 1)
                    g, ii, half = u // 4, (u // 2) % 2, u % 2
                    t = 4 * g + 2 * ii
                    ins = pe.matmul(ps[7][:, t * AC:(t + 2) * AC],
                                    flat(vtok[:, g, 2 * half:2 * half + 2, :]), pt[:, u, :],
                                    start=half == 0, stop=half == 1)
                ins.then_inc(o_ps, 1)
                if not last:
                    values(c + 1)
                product(n + 1, 1, 1, xs(xh), xs(xl), tile_n=n + 1)

            with pe.Fori(0, 3) as i:
                for w in range(2):
                    attend(i, i * 2 + w, w)
            attend(3, 6, 0)
            attend(3, 7, 1, last=True)

            pe.wait_ge(o_done, 8)
            L2 = 2 * LEVELS

            def decay_lora(n):
                pe.wait_ge(lora_copied, n + 1)
                pe.matmul(ps[5][:, :], lorap[:, :], lora_w_in[:, :], start=True, stop=True)\
                    .then_inc(lora_ps, 1)

            def rate_lora(n):
                pe.matmul(ps[7][:, :], lorap[:, :], lora_a_in[:, :], start=True, stop=True)\
                    .then_inc(lora_ps, 1)

            def by_token(bank, src, heads):
                for j in range(NT):
                    ins = pe.matmul(ps[bank][:, 2 * j:2 * j + 2], src[:, j * C:(j + 1) * C],
                                    heads[:, 0:P:HD], start=True, stop=True)
                return ins

            def turned(bank, src):
                for j in range(NT):
                    ins = pe.transpose(ps[bank][:, j * P:(j + 1) * P], src[:, j * P:(j + 1) * P],
                                       ident[:, :])
                return ins

            def key_sums(n):
                pe.wait_ge(sq_ready, n + 1)
                by_token(6, t2, headones).then_inc(ss_ps, 1)

            def key_norms(n):
                pe.wait_ge(kex_ready, n + 1)
                turned(6, kqn).then_inc(kn_ps, 1)

            def deviations(d):
                pe.wait_ge(vex_ready, d + 1)
                turned(4, ysq).then_inc(rstd_ps, 1)

            def norm_mean(d):
                pe.wait_ge(y_copied, d + 1)
                pe.matmul(ps[4][:, :], headmean[:, :], ysb[:, :], start=True, stop=True)\
                    .then_inc(mean_ps, 1)

            def bonus(d):
                pe.wait_ge(rk_ready, d + 1)
                pe.matmul(ps[5][:, :], headones[:, :],
                          z[:, bass.ds(d + 8, 1), :].rearrange("p a t -> p (a t)"), start=True,
                          stop=True).then_inc(bonus_ps, 1)

            def gate(d):
                pe.wait_ge(g2_copied, d + 1)
                pe.matmul(ps[7][:, :], g2p[:, :], lora_g_in[:, :], start=True, stop=True)\
                    .then_inc(gmul_ps, 1)

            def norm_var(d):
                pe.wait_ge(ysq_ready, d + 1)
                by_token(4, ysq, headmean).then_inc(var_ps, 1)

            def scores(n, par2, d):
                pe.wait_ge(ops_ready, n + 1)
                for f in range(8):
                    src, j = (bp, kp)[f // 4], f % 4
                    if f == 4 and d is not None:
                        norm_mean(d)
                    if f >= 4:
                        pe.wait_ge(g_ready, n * 8 + f - 3)
                    for h in range(2):
                        ins = pe.matmul(ps[f % 4][:, h * 2 * C:(h + 1) * 2 * C],
                                        src[:, h, j * C:(j + 1) * C], ar[:, par2, j, :],
                                        start=True, stop=True)
                    ins.then_inc(g_ps, 1)
                if d is not None:
                    norm_var(d)
                pe.wait_ge(hats_ready, n + 1)
                pe.wait_ge(g_ready, n * 8 + 8)
                for b, src in ((0, t2), (1, t0), (2, vfix)):
                    ins = turned(b, src)
                ins.then_inc(tok_ps, 1)
                if d is not None:
                    bonus(d)

            def invert(n, d, following=True):
                def y_written(g, lv):
                    if lv == 1:
                        pe.wait_ge(y_start, n * 2 + g + 1)
                    else:
                        pe.wait_ge(y_ready[g], n * (LEVELS - 1) + (lv - 1))

                def transposed(g):
                    for u in range(4):
                        j, h = 2 * g + u // 2, u % 2
                        ins = pe.matmul(ps[2 * g + 1][:, u * C:(u + 1) * C], yy[:, j, h, :],
                                        ident16[:, :], start=True, stop=True)
                    return ins

                pe.wait_ge(n1_ready, n + 1)
                for lv in range(LEVELS):
                    if lv == 1 and d is not None:
                        gate(d)
                    if lv == 2 and d is not None:
                        deviations(d)
                    if lv == 3 and following:
                        key_sums(n + 1)
                    if lv == 5 and following:
                        decay_lora(n + 1)
                    if lv == 6 and following:
                        key_norms(n + 1)
                    for g in range(2):
                        if lv == 0:
                            if g == 0:
                                pe.wait_ge(tok_ready, n * 2 + 1)
                            else:
                                pe.wait_ge(vp_ready, n + 1)
                        else:
                            y_written(g, lv)
                        for u in range(4):
                            j, h = 2 * g + u // 2, u % 2
                            ins = pe.matmul(ps[2 * g][:, u * C:(u + 1) * C], n1[:, j, h, :],
                                            yy[:, j, h, :] if lv else ident16[:, :],
                                            start=True, stop=True)
                        ins.then_inc(v_ps, 1)
                        if lv:
                            if lv == 1 and g == 0:
                                pe.wait_ge(tok_ready, n * 2 + 2)
                            transposed(g).then_inc(x_ps, 1)
                    if lv == 0:
                        continue
                    for g in range(2):
                        pe.wait_ge(v_ready, n * L2 + (2 * lv + g + 1))
                        pe.wait_ge(x_ready, n * L2 + (2 * (lv - 1) + g + 1))
                        for u in range(4):
                            j, h = 2 * g + u // 2, u % 2
                            o = ps[2 * g][:, u * C:(u + 1) * C]
                            if g == 0:
                                pe.matmul(o, ident16[:, :], yy[:, j, h, :], start=True, stop=False)
                            ins = pe.matmul(o, xx[:, j, h, :], v1[:, j, h, :], start=g == 1,
                                            stop=True)
                        ins.then_inc(y_ps, 1)
                if following:
                    if d is not None:
                        pe.wait_ge(pair_done, n)
                    rate_lora(n + 1)
                pe.wait_ge(n2_ready, n + 1)
                for g in range(2):
                    y_written(g, LEVELS)
                    transposed(g).then_inc(x_ps, 1)
                    for u in range(4):
                        j, h = 2 * g + u // 2, u % 2
                        o = ps[2 * g][:, u * C:(u + 1) * C]
                        pe.matmul(o, ident16[:, :], ident16[:, :], start=True, stop=False)
                        pe.matmul(o, nident16[:, :], yy[:, j, h, :], start=False, stop=False)
                        pe.matmul(o, n1[:, j, h, :], yy[:, j, h, :], start=False, stop=False)
                        ins = pe.matmul(o, n2[:, j, h, :], yy[:, j, h, :], start=False, stop=True)
                    ins.then_inc(r_ps, 1)
                for g in range(2):
                    pe.wait_ge(x_ready, n * L2 + (2 * (LEVELS - 1) + g + 1))
                    pe.wait_ge(r_ready, n * 2 + g + 1)
                    for u in range(4):
                        j, h = 2 * g + u // 2, u % 2
                        ins = pe.matmul(ps[2 * g][:, u * C:(u + 1) * C], v1[:, j, h, :],
                                        xx[:, j, h, :], start=True, stop=True)
                    ins.then_inc(n_ps, 1)

            def scan(d, par2):
                pe.wait_ge(s_ready, d * NT + 1)
                for j in range(NT):
                    v_h = [flat(vp[:, j, 2 * h:2 * h + 2, :]) for h in range(2)]
                    z_h = [flat(zp[:, 2 * h:2 * h + 2, :]) for h in range(2)]
                    u_h = [flat(up[:, 2 * h:2 * h + 2, :]) for h in range(2)]
                    zb, ub, yb = ps[4 + j % 2][:, 0:P], ps[5 - j % 2][:, 0:P], \
                        ps[6][:, j * C:(j + 1) * C]
                    for h in range(2):
                        pe.matmul(zb, gk[:, j, h, 0:C], v_h[h], start=h == 0, stop=False)
                    if j:
                        pe.wait_ge(s_ready, d * NT + j + 1)
                    pe.matmul(zb, ar[:, par2, j, 0:C], stm[:, :], start=False, stop=True)\
                        .then_inc(z_ps, 1)
                    pe.matmul(yb, stm[:, :], ar[:, par2, j, C:2 * C], start=True, stop=False)
                    for h in range(2):
                        pe.matmul(yb, v_h[h], gk[:, j, h, C:2 * C], start=False, stop=False)
                    pe.wait_ge(z_ready, d * NT + j + 1)
                    pe.matmul(ub, xf[:, j, 0, :], z_h[0], start=True, stop=False)
                    pe.matmul(ub, xf[:, j, 1, :], z_h[1], start=False, stop=True)\
                        .then_inc(u_ps, 1)
                    if j < NT - 1:
                        pe.matmul(zb, ktok[:, j, :], vp[:, j, 0:4:3, :], start=True, stop=False)
                    pe.wait_ge(u_ready, d * NT + j + 1)
                    if j < NT - 1:
                        pe.matmul(zb, btok[:, j, :], up[:, 0:4:3, :], start=False, stop=True)\
                            .then_inc(s_ps, 1)
                    pe.matmul(yb, u_h[0], gb[:, j, 0, C:2 * C], start=False, stop=False)
                    ins = pe.matmul(yb, u_h[1], gb[:, j, 1, C:2 * C], start=False, stop=True)
                ins.then_inc(out_ps, 1)

            def step(n, par2, following=True):
                pe.wait_ge(xf_ready, (n - 1) * 2 + 2)
                pe.wait_ge(kqn_ready, n + 1)
                scan(n - 1, 1 - par2)
                scores(n, par2, n - 1)
                invert(n, n - 1, following)

            key_sums(0)
            decay_lora(0)
            rate_lora(0)
            key_norms(0)
            scores(0, 0, None)
            invert(0, None)
            with pe.Fori(0, 3) as i:
                step(i * 2 + 1, 1)
                step(i * 2 + 2, 0)
            step(PAIRS - 1, 1, following=False)
            pe.wait_ge(xf_ready, 2 * PAIRS)
            scan(PAIRS - 1, 1)
            norm_mean(PAIRS - 1)
            bonus(PAIRS - 1)
            gate(PAIRS - 1)
            norm_var(PAIRS - 1)
            deviations(PAIRS - 1)

            with pe.Fori(0, 4) as i:
                for u in range(4):
                    n = i * 4 + N_PROJ + u
                    hi, lo = ((yah, yal), (ybh, ybl))[u % 2]
                    product(n, u % 2, u % 2, xs(hi), xs(lo), tile_n=n,
                            ready=(lambda k: pe.wait_ge(yl_ready, 4 * u + k // 2 + 1))
                            if u < 2 else None)
            with pe.Fori(0, 2) as i:
                for u in range(4):
                    n, m = i * 4 + N_OUT + u, i * 4 + u

                    def residual():
                        pe.wait_ge(xblk_in[u % 2], (i * 2 + u // 2) * 16 + 16)
                        for j in range(NT):
                            pe.matmul(ps[u % 2][:, j * P:(j + 1) * P], xblk[:, u % 2, j, :],
                                      ident[:, :], start=False, stop=False)

                    product(n, u % 2, u % 2, xs(mh), xs(ml), tile_n=n, before_last=residual,
                            ready=(lambda k: pe.wait_ge(ml_ready, k + 1)) if u == 0 else None)
            pe.wait_ge(acc_ready, 9)
            for j in range(NT):
                ins = pe.matmul(ps[2][:, j:j + 1], rs1[:, j * P:(j + 1) * P], ones[:, 0:1],
                                start=True, stop=True)
            ins.then_inc(tot_ps, 1)
            pe.wait_ge(rms_ready, 2)
            for j in range(NT):
                ins = pe.transpose(ps[3][:, j * P:(j + 1) * P], rs1[:, j * P:(j + 1) * P],
                                   ident[:, :])
            ins.then_inc(rms_ps, 1)
            with pe.Fori(0, FT // 2) as i:
                for u in range(4):
                    n = i * 4 + N_UP + u
                    product(n, u % 2, u % 2, xs(xnh), xs(xnl), tile_n=n,
                            ready=(lambda k: pe.wait_ge(xnl_ready, k + 1)) if u == 0 else None)
            def turn_output(t, b):
                pe.wait_ge(ps_free, t + (N_DOWN + 1))
                for j in range(NT):
                    ins = pe.transpose(ps[2 + b][:, j * P:(j + 1) * P],
                                       ot[:, b, j * P:(j + 1) * P], ident[:, :])
                ins.then_inc(y_t, 1)

            with pe.Fori(0, 2) as i:
                for u in range(12):
                    n = i * 12 + N_DOWN + u
                    m, s = divmod(u, 3)
                    product(n, u % 2, m % 2, lambda k: hh[:, 8 * s + k, :],
                            lambda k: hl[:, 8 * s + k, :], kn=DOWN_K[s], first=s == 0,
                            last=s == 2, tile_n=i * 4 + N_DOWN + m,
                            ready=(lambda k: pe.wait_ge(hl_ready, 8 * s + k + 1)) if m == 0
                            else None)
                    if s == 0 and m:
                        turn_output(i * 4 + m - 1, (m - 1) % 2)
                turn_output(i * 4 + 3, 1)


_INS = ["x", "norm1_g", "w_in", "rwkv_mu", "w0", "w2", "a0", "a2", "g2", "k_k", "k_a", "r_k",
        "lnx_w", "lnx_b", "b_qkv", "attn_sink", "gate_b", "w_proj_a", "w_proj_b", "w_out",
        "norm2_g", "w_up", "conv_w", "conv_b", "w_down", "normf_g"]


def kernel(**inputs):
    import concourse.bacc as bacc
    from concourse.bass_utils import run_bass_kernel_spmd

    nc = bacc.Bacc("TRN2", target_bir_lowering=False, num_devices=1)
    arrays, args = {}, []
    for name in _INS:
        a = np.ascontiguousarray(inputs[name])
        arrays[f"in_{name}"] = a
        args.append(nc.dram_tensor(f"in_{name}", a.shape, mybir.dt.from_np(a.dtype),
                                   kind="ExternalInput").ap())
    args.append(nc.dram_tensor("out", (1, T, D), F32, kind="ExternalOutput").ap())
    build(nc, *args)
    return run_bass_kernel_spmd(nc, [arrays], core_ids=[0]).results[0]["out"]
```
